# Optimizing a Trainium2 kernel written in Bass

```python
import math
import jax, jax.numpy as jnp
from jax import lax
import numpy as np

D_MODEL = 1024
BATCH = 1
SEQ = 256
DEPTH = 2

N_META = 16
NORM_EPS = 1e-6
N_MIXERS = 2
N_MLA = (DEPTH + 1) // 2
N_LRU = DEPTH // 2

MLA_HEADS = 8
QK_NOPE = 128
QK_ROPE = 64
V_HEAD = 128
Q_LORA = 384
KV_LORA = 256
ROPE_THETA = 10000.0
Q_BLOCK = 128

LRU_WIDTH = D_MODEL
LRU_BLOCKS = 8
LRU_BW = LRU_WIDTH // LRU_BLOCKS
CONV_W = 4
LRU_C = 8.0

PEER_HEADS = 8
N_KEYS = 128
N_EXPERTS = N_KEYS * N_KEYS
PEER_TOPK = 16
PEER_QDIM = 256
PEER_QHALF = PEER_QDIM // 2
PEER_BLOCK = 256

kernel_name = "hybrid_mla_rglru_peer_meta"

def rms_norm(x, g):
    x32 = x.astype(jnp.float32)
    y = x32 * lax.rsqrt(jnp.mean(x32 * x32, axis=-1, keepdims=True) + NORM_EPS)
    return (y * g.astype(jnp.float32)).astype(x.dtype)

def rope(x, pos):
    half = QK_ROPE // 2
    freqs = ROPE_THETA ** (-jnp.arange(half, dtype=jnp.float32) / half)
    ang = pos.astype(jnp.float32)[..., None] * freqs
    cos = jnp.cos(ang)[:, :, None, :]
    sin = jnp.sin(ang)[:, :, None, :]
    x32 = x.astype(jnp.float32)
    x1, x2 = x32[..., :half], x32[..., half:]
    return jnp.concatenate([x1 * cos - x2 * sin, x2 * cos + x1 * sin], axis=-1).astype(x.dtype)

def mla_mixer(h, pos, w_in, q_norm, w_q_up, kv_norm, w_kv_up, w_out):
    B, L, _ = h.shape
    a = h @ w_in
    q_lat = a[..., :Q_LORA]
    kv_lat = a[..., Q_LORA:Q_LORA + KV_LORA]
    k_rot = a[..., Q_LORA + KV_LORA:]
    q = (rms_norm(q_lat, q_norm) @ w_q_up).reshape(B, L, MLA_HEADS, QK_NOPE + QK_ROPE)
    kv = (rms_norm(kv_lat, kv_norm) @ w_kv_up).reshape(B, L, MLA_HEADS, QK_NOPE + V_HEAD)
    q = jnp.concatenate([q[..., :QK_NOPE], rope(q[..., QK_NOPE:], pos)], axis=-1)
    k_pe = rope(k_rot[:, :, None, :], pos)
    k = jnp.concatenate([kv[..., :QK_NOPE],
                         jnp.broadcast_to(k_pe, (B, L, MLA_HEADS, QK_ROPE))], axis=-1)
    v = kv[..., QK_NOPE:]
    n_qb = -(-L // Q_BLOCK)
    Lp = n_qb * Q_BLOCK
    pad = ((0, 0), (0, Lp - L), (0, 0), (0, 0))
    q, k, v = jnp.pad(q, pad), jnp.pad(k, pad), jnp.pad(v, pad)
    k32 = k.astype(jnp.float32)
    scale = 1.0 / math.sqrt(QK_NOPE + QK_ROPE)
    key_idx = jnp.arange(Lp)
    q_blocks = q.reshape(B, n_qb, Q_BLOCK, MLA_HEADS, QK_NOPE + QK_ROPE).transpose(1, 0, 2, 3, 4)

    def attend(args):
        qi, qb = args
        s = jnp.einsum('bqhd,bkhd->bhqk', qb.astype(jnp.float32), k32) * scale
        q_idx = qi * Q_BLOCK + jnp.arange(Q_BLOCK)
        causal = key_idx[None, :] <= q_idx[:, None]
        s = jnp.where(causal[None, None], s, -1e30)
        p = jax.nn.softmax(s, axis=-1)
        return jnp.einsum('bhqk,bkhd->bqhd', p.astype(v.dtype), v)

    o = lax.map(attend, (jnp.arange(n_qb), q_blocks))
    o = o.transpose(1, 0, 2, 3, 4).reshape(B, Lp, MLA_HEADS * V_HEAD)[:, :L]
    return o @ w_out

def rglru_mixer(h, w_in, conv_w, conv_b, w_gate_a, b_gate_a, w_gate_x, b_gate_x, lam, w_out):
    B, L, _ = h.shape
    proj = h @ w_in
    gate = jax.nn.gelu(proj[..., :LRU_WIDTH], approximate=True)
    xr = proj[..., LRU_WIDTH:]
    xpad = jnp.pad(xr, ((0, 0), (CONV_W - 1, 0), (0, 0)))
    xc = conv_b
    for j in range(CONV_W):
        xc = xc + xpad[:, j:j + L] * conv_w[j]
    xb = xc.reshape(B, L, LRU_BLOCKS, LRU_BW)
    r = jax.nn.sigmoid((jnp.einsum('blnd,nde->blne', xb, w_gate_a).reshape(B, L, LRU_WIDTH)
                        + b_gate_a).astype(jnp.float32))
    i = jax.nn.sigmoid((jnp.einsum('blnd,nde->blne', xb, w_gate_x).reshape(B, L, LRU_WIDTH)
                        + b_gate_x).astype(jnp.float32))
    log_a = -LRU_C * r * jax.nn.softplus(-lam.astype(jnp.float32))
    a = jnp.exp(log_a)
    mult = jnp.sqrt(-jnp.expm1(2.0 * log_a))
    b = mult * (i * xc.astype(jnp.float32))

    def combine(e1, e2):
        a1, b1 = e1
        a2, b2 = e2
        return a1 * a2, a2 * b1 + b2

    _, hs = lax.associative_scan(combine, (a, b), axis=1)
    y = hs.astype(h.dtype) * gate
    return y @ w_out

def peer_ffn(h, w_query, sub_keys, u_tab, v_tab):
    B, L, D = h.shape
    tok = h.reshape(B * L, D)
    T = B * L
    n_blk = -(-T // PEER_BLOCK)
    tok = jnp.pad(tok, ((0, n_blk * PEER_BLOCK - T), (0, 0))).reshape(n_blk, PEER_BLOCK, D)

    def retrieve(xb):
        q = (xb @ w_query).reshape(-1, PEER_HEADS, 2, PEER_QHALF)
        s = jnp.einsum('thpd,pkd->thpk', q, sub_keys).astype(jnp.float32)
        sv, si = lax.top_k(s, PEER_TOPK)
        cand = (sv[:, :, 0, :, None] + sv[:, :, 1, None, :]).reshape(-1, PEER_HEADS, PEER_TOPK * PEER_TOPK)
        cidx = (si[:, :, 0, :, None] * N_KEYS + si[:, :, 1, None, :]).reshape(-1, PEER_HEADS, PEER_TOPK * PEER_TOPK)
        top_s, top_p = lax.top_k(cand, PEER_TOPK)
        eidx = jnp.take_along_axis(cidx, top_p, axis=-1)
        g = jax.nn.softmax(top_s, axis=-1)
        u = u_tab[eidx]
        act = jax.nn.gelu(jnp.einsum('thkd,td->thk', u, xb).astype(jnp.float32))
        w = (g * act).astype(xb.dtype)
        return jnp.einsum('thk,thkd->td', w, v_tab[eidx])

    out = lax.map(retrieve, tok)
    return out.reshape(n_blk * PEER_BLOCK, D)[:T].reshape(B, L, D)

def setup_inputs(seed: int = 0) -> dict:
    key = jax.random.key(seed)
    ks = iter(jax.random.split(key, 32))
    f32 = jnp.float32

    def nrm(shape, scale):
        return jax.random.normal(next(ks), shape, f32) * scale

    def gain(shape):
        return 1.0 + 0.05 * jax.random.normal(next(ks), shape, f32)

    x = jax.random.normal(next(ks), (BATCH, SEQ, D_MODEL), f32)
    positions = jnp.broadcast_to(jnp.arange(SEQ, dtype=jnp.int32)[None, :], (BATCH, SEQ))
    meta_tokens = nrm((N_META, D_MODEL), 1.0)
    mixer_norm = gain((DEPTH, D_MODEL))
    ffn_norm = gain((DEPTH, D_MODEL))
    final_norm = gain((D_MODEL,))

    mla_w_in = nrm((N_MLA, D_MODEL, Q_LORA + KV_LORA + QK_ROPE), D_MODEL ** -0.5)
    mla_q_norm = gain((N_MLA, Q_LORA))
    mla_w_q_up = nrm((N_MLA, Q_LORA, MLA_HEADS * (QK_NOPE + QK_ROPE)), Q_LORA ** -0.5)
    mla_kv_norm = gain((N_MLA, KV_LORA))
    mla_w_kv_up = nrm((N_MLA, KV_LORA, MLA_HEADS * (QK_NOPE + V_HEAD)), KV_LORA ** -0.5)
    mla_w_out = nrm((N_MLA, MLA_HEADS * V_HEAD, D_MODEL), (MLA_HEADS * V_HEAD) ** -0.5)

    lru_w_in = nrm((N_LRU, D_MODEL, 2 * LRU_WIDTH), D_MODEL ** -0.5)
    lru_conv_w = nrm((N_LRU, CONV_W, LRU_WIDTH), CONV_W ** -0.5)
    lru_conv_b = nrm((N_LRU, LRU_WIDTH), 0.01)
    lru_w_gate_a = nrm((N_LRU, LRU_BLOCKS, LRU_BW, LRU_BW), LRU_BW ** -0.5)
    lru_b_gate_a = nrm((N_LRU, LRU_WIDTH), 0.01)
    lru_w_gate_x = nrm((N_LRU, LRU_BLOCKS, LRU_BW, LRU_BW), LRU_BW ** -0.5)
    lru_b_gate_x = nrm((N_LRU, LRU_WIDTH), 0.01)
    u = jax.random.uniform(next(ks), (N_LRU, LRU_WIDTH), f32, 0.9, 0.999)
    s = u ** (1.0 / LRU_C)
    lru_lambda = jnp.log(s) - jnp.log1p(-s)
    lru_w_out = nrm((N_LRU, LRU_WIDTH, D_MODEL), LRU_WIDTH ** -0.5)

    peer_w_query = nrm((DEPTH, D_MODEL, PEER_HEADS * PEER_QDIM), D_MODEL ** -0.5)
    peer_sub_keys = nrm((DEPTH, 2, N_KEYS, PEER_QHALF), PEER_QHALF ** -0.5)
    peer_u = nrm((DEPTH, N_EXPERTS, D_MODEL), D_MODEL ** -0.5)
    peer_v = nrm((DEPTH, N_EXPERTS, D_MODEL), PEER_TOPK ** -0.5)

    return {"x": x, "positions": positions, "meta_tokens": meta_tokens,
            "mixer_norm": mixer_norm, "ffn_norm": ffn_norm, "final_norm": final_norm,
            "mla_w_in": mla_w_in, "mla_q_norm": mla_q_norm, "mla_w_q_up": mla_w_q_up,
            "mla_kv_norm": mla_kv_norm, "mla_w_kv_up": mla_w_kv_up, "mla_w_out": mla_w_out,
            "lru_w_in": lru_w_in, "lru_conv_w": lru_conv_w, "lru_conv_b": lru_conv_b,
            "lru_w_gate_a": lru_w_gate_a, "lru_b_gate_a": lru_b_gate_a,
            "lru_w_gate_x": lru_w_gate_x, "lru_b_gate_x": lru_b_gate_x,
            "lru_lambda": lru_lambda, "lru_w_out": lru_w_out,
            "peer_w_query": peer_w_query, "peer_sub_keys": peer_sub_keys,
            "peer_u": peer_u, "peer_v": peer_v}

def reference(x, positions, meta_tokens, mixer_norm, ffn_norm, final_norm,
              mla_w_in, mla_q_norm, mla_w_q_up, mla_kv_norm, mla_w_kv_up, mla_w_out,
              lru_w_in, lru_conv_w, lru_conv_b, lru_w_gate_a, lru_b_gate_a,
              lru_w_gate_x, lru_b_gate_x, lru_lambda, lru_w_out,
              peer_w_query, peer_sub_keys, peer_u, peer_v):
    B = x.shape[0]
    meta = jnp.broadcast_to(meta_tokens[None].astype(x.dtype), (B, N_META, x.shape[-1]))
    h = jnp.concatenate([meta, x], axis=1)
    meta_pos = jnp.broadcast_to(jnp.arange(N_META, dtype=jnp.int32)[None], (B, N_META))
    pos = jnp.concatenate([meta_pos, positions.astype(jnp.int32) + N_META], axis=1)
    for layer in range(DEPTH):
        hn = rms_norm(h, mixer_norm[layer])
        j = layer // N_MIXERS
        if layer % N_MIXERS == 0:
            mix = mla_mixer(hn, pos, mla_w_in[j], mla_q_norm[j], mla_w_q_up[j],
                            mla_kv_norm[j], mla_w_kv_up[j], mla_w_out[j])
        else:
            mix = rglru_mixer(hn, lru_w_in[j], lru_conv_w[j], lru_conv_b[j],
                              lru_w_gate_a[j], lru_b_gate_a[j], lru_w_gate_x[j],
                              lru_b_gate_x[j], lru_lambda[j], lru_w_out[j])
        h = h + mix
        h = h + peer_ffn(rms_norm(h, ffn_norm[layer]), peer_w_query[layer],
                         peer_sub_keys[layer], peer_u[layer], peer_v[layer])
    out = rms_norm(h, final_norm)
    return out[:, N_META:]


_drawn_inputs = setup_inputs


def setup_inputs(seed=0):
    import zlib

    import numpy as np

    out = dict(_drawn_inputs(seed))
    spreads = {}
    factors = {'mla_q_norm': 2.701, 'lru_b_gate_a': 44.871, 'lru_b_gate_x': 28.84}
    for name, (base, spread) in spreads.items():
        noise = np.random.default_rng([zlib.crc32(name.encode()), seed]).standard_normal(out[name].shape)
        drawn = base * np.exp(spread * noise) if base else spread * noise
        out[name] = __import__('jax').numpy.asarray(drawn.astype(out[name].dtype))
    for name, factor in factors.items():
        out[name] = (out[name] * factor).astype(out[name].dtype)
    return out
```

```python
from contextlib import ExitStack

import numpy as np

import concourse.bass as bass
from concourse import mybir

P = 128
D = 1024
DC = D // P
SEQ = 256
META = 16
L = SEQ + META
EPS = 1e-6

HEADS, NOPE, ROPE, VH = 8, 128, 64, 128
QLORA, KVLORA = 384, 256
QC, KVC = QLORA // P, KVLORA // P
SCALE = float(1.0 / np.sqrt(NOPE + ROPE))
Q0 = (0, 128, L - P)
NKEYS_SEEN = (128, 256, L)

PH, NK, TOPK, QH = 8, 128, 16, 128
GT = 16
HALF = NK // 2
ST = 8
UNROLL = 4

CONV = 4
LRU_C = 8.0

BIG = NK * L
NEG = -3.0e38

ALU = mybir.AluOpType
ACT = mybir.ActivationFunctionType
AX = mybir.AxisListType
F32 = mybir.dt.float32
F32R = mybir.dt.float32r
U32 = mybir.dt.uint32
I32 = mybir.dt.int32

VEC = {}
for _i, _n in enumerate(["mix0", "mix1", "ffn0", "ffn1", "final", "b_a", "b_x", "conv_b", "cw0", "cw1", "cw2",
                         "cw3", "lam"]):
    VEC[_n] = _i * DC
VEC["q_norm"] = 13 * DC
VEC["kv_norm"] = VEC["q_norm"] + QC
NVEC = VEC["kv_norm"] + KVC

CON = {"iota": 0, "head": P, "token": P + PH, "freq": P + PH + GT, "sign": P + PH + GT + 1}
NCON = P + PH + GT + 2


def constants():
    p = np.arange(P)
    con = np.zeros((P, NCON), np.float32)
    con[:, :P] = np.arange(P)
    con[:, CON["head"]:CON["head"] + PH] = (p[:, None] // GT) == np.arange(PH)
    con[:, CON["token"]:CON["token"] + GT] = (p[:, None] % GT) == np.arange(GT)
    half = ROPE // 2
    freqs = np.float32(10000.0) ** (-np.arange(half, dtype=np.float32) / np.float32(half))
    con[:, CON["freq"]] = freqs[p % half]
    con[:, CON["sign"]] = np.where(p % ROPE < half, -1.0, 1.0)
    x = np.arange(L) - (L - P)
    tri = np.where(x[None, :] > p[:, None], -1e30, 0.0)
    return con, np.concatenate([np.eye(P), tri], axis=1).astype(np.float32)


class Steps:

    def __init__(self, eng, sem):
        self.eng, self.sem, self.n = eng, sem, 0

    def done(self, ins):
        ins.then_inc(self.sem, 1)
        self.n = self.n + 1
        self.eng.wait_ge(self.sem, self.n)

    def enter(self, turn, per_turn):
        self.base = self.n
        self.n = turn * per_turn + self.base

    def leave(self, turns, per_turn):
        self.n = self.base + turns * per_turn


class Stage:

    def __init__(self, nc):
        self.nc, self.sems = nc, []

    def __enter__(self):
        return self

    def sem(self, name):
        self.sems.append(self.nc.alloc_semaphore(name))
        return self.sems[-1]

    def __exit__(self, kind, *_):
        if kind is None:
            self.nc.clear_and_free_semaphores(self.sems)
            self.nc.all_engine_barrier()


class Memory:

    def __init__(self, nc, ctx):
        def sb(name, shape, dt=F32):
            return ctx.enter_context(nc.sbuf_tensor(name, shape, dt))

        self.big = sb("big", [P, BIG])
        self.h = sb("h", [P, DC, L])
        self.xhi = sb("xhi", [P, DC, L], F32R)
        self.xlo = sb("xlo", [P, DC, L], F32R)
        self.raw = sb("raw", [P, UNROLL, D])
        self.whi = sb("whi", [P, 2, D], F32R)
        self.wlo = sb("wlo", [P, 2, D], F32R)
        self.a_hi = sb("a_hi", [P, ST, HALF], F32R)
        self.a_lo = sb("a_lo", [P, ST, HALF], F32R)
        self.b_hot = sb("b_hot", [P, ST, P], F32R)
        self.idx_i = sb("idx_i", [P, L])
        self.idx_j = sb("idx_j", [P, L])
        self.g_hi = sb("g_hi", [P, L], F32R)
        self.g_lo = sb("g_lo", [P, L], F32R)
        self.con = sb("con", [P, NCON])
        self.vec = sb("vec", [P, NVEC])
        self.ones = sb("ones", [P, P])
        self.ps = ctx.enter_context(nc.psum_tensor("ps", [P, 8, 512], F32))

    def take(self, at, shape):
        n = int(np.prod(shape))
        assert at + n <= BIG, (at, shape)
        v = self.big[:, at:at + n]
        if len(shape) == 2:
            v = v.rearrange("p (a b) -> p a b", b=shape[1])
        if len(shape) == 3:
            v = v.rearrange("p (a b c) -> p a b c", b=shape[1], c=shape[2])
        if len(shape) == 4:
            v = v.rearrange("p (a b c d) -> p a b c d", b=shape[1], c=shape[2], d=shape[3])
        return v, at + n


class Stream:

    def __init__(self, nc, ctx, mem, name, tokens):
        def sem(what):
            return ctx.sem(f"{name}_{what}")

        self.mem, self.T = mem, tokens
        self.landed = [sem(f"landed{s}") for s in range(UNROLL)]
        self.hi_ready = sem("hi_ready")
        self.lo_ready = [sem(f"lo_ready{r}") for r in range(2)]
        self.done = [sem(f"done{r}") for r in range(2)]
        self.free = [sem(f"free{r}") for r in range(2)]

    def load(self, sp, turn, s, src, first=False):
        if not first:
            sp.wait_ge(self.lo_ready[s % 2], turn * 2 + (s // 2 - 1))
        sp.dma_start(self.mem.raw[:, s, :], src).then_inc(self.landed[s], 16)

    def cut_hi(self, act, turn, s):
        act.wait_ge(self.landed[s], turn * 16 + 16)
        act.wait_ge(self.done[s % 2], turn * 2 + s // 2)
        act.copy(self.mem.whi[:, s % 2, :], self.mem.raw[:, s, :]).then_inc(self.hi_ready, 1)

    def cut_lo(self, eng, turn, s):
        eng.wait_ge(self.hi_ready, turn * UNROLL + (s + 1))
        eng.tensor_tensor(self.mem.wlo[:, s % 2, :], self.mem.raw[:, s, :],
                          self.mem.whi[:, s % 2, :].bitcast(F32), ALU.subtract).then_inc(self.lo_ready[s % 2], 1)

    def open(self, pe):
        for free in self.free:
            pe.sem_inc(free, 1)

    def multiply(self, pe, turn, s, out):
        m, r = self.mem, s % 2
        pe.wait_ge(self.hi_ready, turn * UNROLL + (s + 1))
        pe.wait_ge(self.free[r], turn * 2 + (s // 2 + 1))
        for c in range(DC):
            w = m.whi[:, r, c * P:(c + 1) * P]
            pe.matmul(out, w, m.xhi[:, c, 0:self.T], start=(c == 0), stop=False)
            pe.matmul(out, w, m.xlo[:, c, 0:self.T], start=False, stop=False)
        pe.wait_ge(self.lo_ready[r], turn * 2 + (s // 2 + 1))
        for c in range(DC):
            mm = pe.matmul(out, m.wlo[:, r, c * P:(c + 1) * P], m.xhi[:, c, 0:self.T], start=False,
                           stop=(c == DC - 1))
        mm.then_inc(self.done[r], 1)

    def wait_product(self, eng, turn, s):
        eng.wait_ge(self.done[s % 2], turn * 2 + (s // 2 + 1))

    def bank(self, s):
        return self.mem.ps[:, s % 2, 0:self.T]


class Norm:

    def __init__(self, nc, ctx, mem, name, src, chunks, gain, squares, rstd, bank, tokens):
        def sem(what):
            return ctx.sem(f"{name}_{what}")

        self.mem, self.src, self.C, self.gain = mem, src, chunks, gain
        self.squares, self.rstd, self.T = squares, rstd, tokens
        self.sum = mem.ps[:, bank, 0:tokens]
        self.squared, self.summed, self.mean = sem("squared"), sem("summed"), sem("mean")
        self.rooted, self.scaled, self.cut = sem("rooted"), sem("scaled"), sem("cut")

    def square(self, dve):
        dve.tensor_tensor(self.squares, self.src, self.src, ALU.mult).then_inc(self.squared, 1)

    def add_up(self, pe):
        pe.wait_ge(self.squared, 1)
        for c in range(self.C):
            mm = pe.matmul(self.sum, self.mem.ones[:, :], self.squares[:, c, :], start=(c == 0),
                           stop=(c == self.C - 1))
        mm.then_inc(self.summed, 1)

    def root(self, act):
        act.wait_ge(self.mean, 1)
        act.activation(self.rstd, self.rstd, ACT.Sqrt).then_inc(self.rooted, 1)

    def scale(self, dve, out):
        dve.wait_ge(self.summed, 1)
        dve.tensor_scalar(self.rstd, self.sum, 1.0 / (self.C * P), EPS, ALU.mult, ALU.add).then_inc(self.mean, 1)
        dve.wait_ge(self.rooted, 1)
        dve.reciprocal(self.rstd, self.rstd).then_inc(self.mean, 1)
        dve.wait_ge(self.mean, 2)
        for c in range(self.C):
            dve.scalar_tensor_tensor(out[:, c, :], self.src[:, c, :], self.mem.vec[:, self.gain + c:self.gain + c + 1],
                                     self.rstd, ALU.mult, ALU.mult).then_inc(self.scaled, 1)


class Cut:

    def __init__(self, nc, ctx, mem, name, src, tokens):
        self.mem, self.src, self.T = mem, src, tokens
        self.hi_cut = ctx.sem(f"{name}_hi_cut")
        self.lo_cut = ctx.sem(f"{name}_lo_cut")

    def hi(self, act, ready):
        for c in range(DC):
            act.wait_ge(ready, c + 1)
            act.copy(self.mem.xhi[:, c, 0:self.T], self.src[:, c, :]).then_inc(self.hi_cut, 1)

    def lo(self, dve):
        for c in range(DC):
            dve.wait_ge(self.hi_cut, c + 1)
            dve.tensor_tensor(self.mem.xlo[:, c, 0:self.T], self.src[:, c, :],
                              self.mem.xhi[:, c, 0:self.T].bitcast(F32), ALU.subtract).then_inc(self.lo_cut, 1)

    def wait(self, pe):
        pe.wait_ge(self.hi_cut, DC)
        pe.wait_ge(self.lo_cut, DC)


def mla(nc, ctx, mem, d):
    def sem(name):
        return ctx.sem("mla_" + name)

    take = mem.take
    lat, at = take(0, (QC + KVC, L))
    kr, at = take(at, (2, L))
    latn, at = take(at, (QC + KVC, L))
    qn, at = take(at, (HEADS, L))
    kn, at = take(at, (HEADS, L))
    qr, at = take(at, (HEADS // 2, L))
    qs, at = take(at, (HEADS // 2, L))
    v, at = take(at, (3, HEADS * VH))
    wq, at = take(at, (QC, 2 * HEADS * P))
    wkv, at = take(at, (KVC, 2 * HEADS * P))
    cosv, at = take(at, (1, L))
    sinv, at = take(at, (1, L))
    ang, at = take(at, (1, L))
    tmp, at = take(at, (1, L))
    rstd, at = take(at, (2, L))
    idm, at = take(at, (1, P + L))
    post, at = take(at, (1, L))
    xn, at = take(at, (DC, L))
    sm, pt = xn[:, 0:3, :], xn[:, 3:6, :]
    o, at = take(at, (HEADS, L))
    small = wq[:, 0, 0:16]
    ident, smask = idm[:, 0, 0:P], idm[:, 0, P:P + L]
    kpe, post = kr[:, 0, :], post[:, 0, :]
    posi = post.bitcast(I32)
    cosv, sinv, ang, tmp = cosv[:, 0, :], sinv[:, 0, :], ang[:, 0, :], tmp[:, 0, :]

    consts_in, x_in, w_in, pos_in, ones_set = sem("consts_in"), sem("x_in"), sem("w_in"), sem("pos_in"), sem("ones")
    dstep, pos_ready, pos_spread, reduced, sines, angles = (
        sem("dve_steps"), sem("pos_ready"), sem("pos_spread"), sem("reduced"), sem("sines"), sem("angles"))
    up_done, up_out, rotated = sem("up_done"), [sem(f"up_out{r}") for r in range(2)], sem("rotated")
    scored, top_found, exped, probs, turned, turned_out, weighed, o_out = (
        sem("scored"), sem("top_found"), sem("exped"), sem("probs"), sem("turned"),
        sem("turned_out"), sem("weighed"), sem("o_out"))

    norm = Norm(nc, ctx, mem, "mla_n", mem.h[:, :, :], DC, VEC["mix0"], xn, rstd[:, 0, :], 2, L)
    cut = Cut(nc, ctx, mem, "mla_x", xn, L)
    down = Stream(nc, ctx, mem, "mla_down", L)
    norm_q = Norm(nc, ctx, mem, "mla_nq", lat[:, 0:QC, :], QC, VEC["q_norm"], latn[:, 0:QC, :], rstd[:, 0, :], 2, L)
    norm_kv = Norm(nc, ctx, mem, "mla_nkv", lat[:, QC:, :], KVC, VEC["kv_norm"], latn[:, QC:, :], rstd[:, 1, :], 3,
                   L)
    out_cut = Cut(nc, ctx, mem, "mla_o", o, L)
    proj = Stream(nc, ctx, mem, "mla_out", L)
    n_down = QC + KVC + 2
    ups = ([(qn[:, h, :], wq, h * P, 0, QC) for h in range(HEADS)]
           + [(qr[:, h, :], wq, (HEADS + h) * P, 0, QC) for h in range(HEADS // 2)]
           + [(qs[:, h, :], wq, (HEADS + HEADS // 2 + h) * P, 0, QC) for h in range(HEADS // 2)]
           + [(kn[:, h, :], wkv, h * P, QC, KVC) for h in range(HEADS)])
    vals = [(t, min(P, L - t * P), half) for t in range(3) for half in range(2)]
    n_up = len(ups) + len(vals)

    def take_up(copy, n):
        if n < len(ups):
            return copy(ups[n][0], mem.ps[:, 4 + n % 4, 0:L])
        t, rows, half = vals[n - len(ups)]
        return copy(v[0:rows, t, half * 512:half * 512 + 512], mem.ps[0:rows, 4 + n % 4, :])

    with nc.Block() as block:
        @block.sync
        def _(sp):
            for c in range(2):
                sp.dma_start(mem.h[:, 4 * c:4 * c + 4, META:L], d["x"][:, 4 * c:4 * c + 4, :]).then_inc(x_in, 16)
            sp.dma_start(mem.h[:, :, 0:META], d["meta"]).then_inc(x_in, 16)
            sp.dma_start(mem.con[:, :], d["con"]).then_inc(consts_in, 16)
            sp.dma_start(mem.vec[:, :], d["vec"]).then_inc(consts_in, 16)
            sp.dma_start(idm[:, 0, :], d["idm"]).then_inc(consts_in, 16)
            sp.dma_start(posi[0:1, META:L], d["pos"]).then_inc(pos_in, 16)
            for n in range(UNROLL):
                down.load(sp, 0, n, d["mla_down"][n], first=True)
            sp.dma_start(wq, d["mla_q_up"]).then_inc(w_in, 16)
            sp.dma_start(wkv, d["mla_kv_up"]).then_inc(w_in, 16)
            for n in range(UNROLL, n_down):
                down.load(sp, n // UNROLL, n % UNROLL, d["mla_down"][n])
            sp.wait_ge(down.lo_ready[0], (n_down + 1) // 2)
            sp.wait_ge(down.lo_ready[1], n_down // 2)
            for s in range(UNROLL):
                proj.load(sp, 0, s, d["mla_out"][s], first=True)
            with sp.Fori(1, DC // UNROLL) as turn:
                for s in range(UNROLL):
                    proj.load(sp, turn, s, tile_of(d["mla_out"], turn, s))

        @block.gpsimd
        def _(pool):
            for n in range(n_down):
                down.cut_lo(pool, n // UNROLL, n % UNROLL)
            with pool.Fori(0, DC // UNROLL) as turn:
                for s in range(UNROLL):
                    proj.cut_lo(pool, turn, s)

        @block.scalar
        def _(act):
            norm.root(act)
            down.cut_hi(act, 0, 0)
            down.cut_hi(act, 0, 1)
            cut.hi(act, norm.scaled)
            act.wait_ge(reduced, 1)
            act.activation(sinv, ang, ACT.Sin).then_inc(sines, 1)
            act.activation(cosv, ang, ACT.Sin, scale=0.5).then_inc(sines, 1)
            for n in range(n_down):
                down.wait_product(act, n // UNROLL, n % UNROLL)
                if n + 2 < n_down:
                    down.cut_hi(act, (n + 2) // UNROLL, (n + 2) % UNROLL)
                dst = lat[:, n, :] if n < QC + KVC else kr[:, n - QC - KVC, :]
                act.copy(dst, down.bank(n)).then_inc(down.free[n % 2], 1)
            norm_q.root(act)
            norm_kv.root(act)
            for n in range(1, n_up, 2):
                act.wait_ge(up_done, n + 1)
                take_up(act.copy, n).then_inc(up_out[1], 1)
            act.wait_ge(down.done[0], (n_down + 1) // 2)
            act.wait_ge(down.done[1], n_down // 2)
            proj.cut_hi(act, 0, 0)
            proj.cut_hi(act, 0, 1)
            with act.Fori(0, HEADS // 2) as pair:
                for e in range(2):
                    for t in range(3):
                        nk = NKEYS_SEEN[t]
                        act.wait_ge(top_found, (pair * 2 + e) * 3 + (t + 1))
                        act.activation(sm[:, t, 0:nk], sm[:, t, 0:nk], ACT.Exp, bias=small[:, t:t + 1],
                                       accum_out=small[:, 3 + t:4 + t]).then_inc(exped, 1)
                    act.wait_ge(weighed, pair * 2 + (e + 1))
                    act.copy(o[:, bass.ds(pair * 2 + e, 1), :], mem.ps[:, 7, 0:L]).then_inc(o_out, 1)
            act.wait_ge(o_out, HEADS)
            out_cut.hi(act, o_out)
            with act.Fori(0, DC // UNROLL - 1) as turn:
                for s in range(UNROLL):
                    proj.wait_product(act, turn, s)
                    proj.cut_hi(act, turn + (s + 2) // UNROLL, (s + 2) % UNROLL)
            for s in range(2):
                proj.wait_product(act, DC // UNROLL - 1, s)
                proj.cut_hi(act, DC // UNROLL - 1, s + 2)

        @block.vector
        def _(dve):
            step = Steps(dve, dstep)
            dve.memset(mem.ones[:, :], 1.0).then_inc(ones_set, 1)
            dve.wait_ge(x_in, 48)
            norm.square(dve)
            dve.wait_ge(consts_in, 48)
            dve.tensor_copy(post[0:1, 0:META], mem.con[0:1, 0:META]).then_inc(pos_ready, 1)
            dve.wait_ge(pos_in, 16)
            dve.tensor_scalar(post[0:1, META:L], posi[0:1, META:L], float(META), None,
                              ALU.add).then_inc(pos_ready, 1)
            norm.scale(dve, xn)
            cut.lo(dve)
            two_pi = (6.28125, float(np.float32(2 * np.pi - 6.28125) // 2.0 ** -20 * 2.0 ** -20))
            rest = 2 * np.pi - two_pi[0] - two_pi[1]
            magic = 1.5 * 2.0 ** 23
            dve.wait_ge(pos_spread, 1)
            step.done(dve.tensor_scalar(ang, mem.ps[:, 3, 0:L], mem.con[:, CON["freq"]:CON["freq"] + 1], None,
                                        ALU.mult))
            step.done(dve.tensor_scalar(tmp, ang, float(1 / (2 * np.pi)), magic, ALU.mult, ALU.add))
            step.done(dve.tensor_scalar(tmp, tmp, -magic, None, ALU.add))
            for part in (*two_pi, rest):
                step.done(dve.scalar_tensor_tensor(ang, tmp, -float(part), ang, ALU.mult, ALU.add))
            dve.tensor_scalar(ang, ang, float(np.float32(-np.pi)), float(np.float32(np.pi)), ALU.max,
                              ALU.min).then_inc(reduced, 1)
            dve.wait_ge(sines, 2)
            step.done(dve.tensor_tensor(cosv, cosv, cosv, ALU.mult))
            step.done(dve.tensor_scalar(cosv, cosv, -2.0, 1.0, ALU.mult, ALU.add))
            step.done(dve.tensor_scalar(sinv, sinv, mem.con[:, CON["sign"]:CON["sign"] + 1], None, ALU.mult))
            dve.wait_ge(down.free[0], (n_down + 1) // 2 + 1)
            dve.wait_ge(down.free[1], n_down // 2 + 1)
            norm_q.square(dve)
            norm_kv.square(dve)
            step.done(dve.tensor_tensor(kr[:, 0, :], kr[:, 0, :], cosv, ALU.mult))
            step.done(dve.tensor_tensor(kr[:, 1, :], kr[:, 1, :], sinv, ALU.mult))
            dve.tensor_tensor(kr[:, 0, :], kr[:, 0, :], kr[:, 1, :], ALU.add).then_inc(rotated, 1)
            norm_q.scale(dve, latn[:, 0:QC, :])
            norm_kv.scale(dve, latn[:, QC:, :])
            for n in range(0, n_up, 2):
                dve.wait_ge(up_done, n + 1)
                take_up(dve.tensor_copy, n).then_inc(up_out[0], 1)
            dve.wait_ge(up_out[0], (n_up + 1) // 2)
            dve.wait_ge(up_out[1], n_up // 2)
            wide = [P, HEADS // 2, L]
            step.done(dve.tensor_tensor(qr, qr, cosv.unsqueeze(1).to_broadcast(wide), ALU.mult))
            step.done(dve.tensor_tensor(qs, qs, sinv.unsqueeze(1).to_broadcast(wide), ALU.mult))
            dve.tensor_tensor(qr, qr, qs, ALU.add).then_inc(rotated, 1)
            per_pair = 2 * 3 * 2
            with dve.Fori(0, HEADS // 2) as pair:
                step.enter(pair, per_pair)
                for e in range(2):
                    for t in range(3):
                        nk = NKEYS_SEEN[t]
                        dve.wait_ge(scored, (pair * 2 + e) * 3 + (t + 1))
                        step.done(dve.scalar_tensor_tensor(sm[:, t, 0:nk], mem.ps[:, t, 0:nk], SCALE,
                                                           smask[:, L - P - Q0[t]:L - P - Q0[t] + nk],
                                                           ALU.mult, ALU.add))
                        dve.tensor_reduce(small[:, t:t + 1], sm[:, t, 0:nk], AX.X, ALU.max,
                                          negate=True).then_inc(top_found, 1)
                    for t in range(3):
                        nk = NKEYS_SEEN[t]
                        dve.wait_ge(exped, (pair * 2 + e) * 3 + (t + 1))
                        step.done(dve.reciprocal(small[:, 6 + t:7 + t], small[:, 3 + t:4 + t]))
                        dve.tensor_scalar(sm[:, t, 0:nk], sm[:, t, 0:nk], small[:, 6 + t:7 + t], None,
                                          ALU.mult).then_inc(probs, 1)
                    for k in range(3):
                        rows = min(P, L - k * P)
                        first = Q0[2] if k == 2 else k * P
                        dve.wait_ge(turned, (pair * 2 + e) * 3 + (k + 1))
                        dve.tensor_copy(pt[0:rows, k, first:L], mem.ps[0:rows, 3 + k, first:L]).then_inc(turned_out, 1)
                step.leave(HEADS // 2, per_pair)
            out_cut.lo(dve)
            with dve.Fori(0, DC // UNROLL) as turn:
                for s in range(UNROLL):
                    proj.wait_product(dve, turn, s)
                    hc = mem.h[:, bass.ds(turn * UNROLL + s, 1), :]
                    dve.tensor_tensor(hc, hc, proj.bank(s).unsqueeze(1), ALU.add).then_inc(proj.free[s % 2], 1)

        @block.tensor
        def _(pe):
            down.open(pe)
            proj.open(pe)
            pe.wait_ge(ones_set, 1)
            norm.add_up(pe)
            pe.wait_ge(pos_ready, 2)
            pe.matmul(mem.ps[:, 3, 0:L], mem.ones[0:1, :], post[0:1, :], start=True, stop=True).then_inc(pos_spread, 1)
            cut.wait(pe)
            for n in range(n_down):
                down.multiply(pe, n // UNROLL, n % UNROLL, down.bank(n))
            pe.wait_ge(reduced, 1)
            norm_q.add_up(pe)
            norm_kv.add_up(pe)
            pe.wait_ge(w_in, 32)
            pe.wait_ge(norm_q.scaled, QC)
            pe.wait_ge(norm_kv.scaled, KVC)
            for n in range(n_up):
                if n >= 4:
                    pe.wait_ge(up_out[n % 2], (n - 4) // 2 + 1)
                bank = 4 + n % 4
                if n < len(ups):
                    _, w, col, c0, count = ups[n]
                    for c in range(count):
                        mm = pe.matmul(mem.ps[:, bank, 0:L], w[:, c, col:col + P], latn[:, c0 + c, :], start=(c == 0),
                                       stop=(c == count - 1))
                else:
                    t, rows, half = vals[n - len(ups)]
                    for c in range(KVC):
                        mm = pe.matmul(mem.ps[0:rows, bank, :], latn[:, QC + c, t * P:t * P + rows],
                                       wkv[:, c, HEADS * P + half * 512:HEADS * P + half * 512 + 512], start=(c == 0),
                                       stop=(c == KVC - 1))
                mm.then_inc(up_done, 1)
            pe.wait_ge(rotated, 2)
            pe.wait_ge(up_out[0], (n_up + 1) // 2)
            pe.wait_ge(up_out[1], n_up // 2)
            for head in range(HEADS):
                pair, lanes = head // 2, slice(ROPE * (head % 2), ROPE * (head % 2) + ROPE)
                for t in range(3):
                    nk = NKEYS_SEEN[t]
                    pe.matmul(mem.ps[:, t, 0:nk], qn[:, head, Q0[t]:Q0[t] + P], kn[:, head, 0:nk], start=True,
                              stop=False)
                    pe.matmul(mem.ps[:, t, 0:nk], qr[lanes, pair, Q0[t]:Q0[t] + P], kpe[lanes, 0:nk], start=False,
                              stop=True).then_inc(scored, 1)
                for k in range(3):
                    rows = min(P, L - k * P)
                    for t in range(k, 3):
                        pe.wait_ge(probs, head * 3 + t + 1)
                        tr = pe.transpose(mem.ps[0:rows, 3 + k, Q0[t]:Q0[t] + P], sm[:, t, k * P:k * P + rows], ident)
                    tr.then_inc(turned, 1)
                pe.wait_ge(o_out, head)
                for k in range(3):
                    rows = min(P, L - k * P)
                    first = Q0[2] if k == 2 else k * P
                    pe.wait_ge(turned_out, head * 3 + k + 1)
                    mm = pe.matmul(mem.ps[:, 7, first:L], v[0:rows, k, head * P:head * P + P], pt[0:rows, k, first:L],
                                   start=(k == 0), stop=(k == 2))
                mm.then_inc(weighed, 1)
            out_cut.wait(pe)
            with pe.Fori(0, DC // UNROLL) as turn:
                for s in range(UNROLL):
                    proj.multiply(pe, turn, s, proj.bank(s))


def tile_of(tiles, turn, s):
    return tiles[bass.ds(turn * UNROLL + s, 1)].rearrange("a p f -> p (a f)")


def rglru(nc, ctx, mem, d):
    def sem(name):
        return ctx.sem("lru_" + name)

    take = mem.take
    xn, at = take(0, (DC, L))
    gate, at = take(at, (DC, L))
    xp, at = take(at, (DC, L + CONV - 1))
    xc, at = take(at, (DC, L))
    r, at = take(at, (DC, L))
    i, at = take(at, (DC, L))
    a, at = take(at, (DC, L))
    b, at = take(at, (DC, L))
    wa, at = take(at, (DC, P))
    wx, at = take(at, (DC, P))
    rstd, at = take(at, (1, L))
    sp_, at = take(at, (8, DC))
    rstd = rstd[:, 0, :]
    nlam, e, z, z2, poly, c8, negc8 = (sp_[:, n, :] for n in range(7))

    norm = Norm(nc, ctx, mem, "lru_n", mem.h[:, :, :], DC, VEC["mix1"], xn, rstd, 2, L)
    cut = Cut(nc, ctx, mem, "lru_x", xn, L)
    into = Stream(nc, ctx, mem, "lru_in", L)
    out = Stream(nc, ctx, mem, "lru_out", L)
    ycut = Cut(nc, ctx, mem, "lru_y", b, L)
    dstep, padded, w_in, conved, gated, gate_out, lam_abs, lam_exp, c8_ready, decays, squared, rooted, states = (
        sem(n) for n in ("dve_steps", "padded", "w_in", "conved", "gated", "gate_out", "lam_abs", "lam_exp",
                         "c8_ready", "decays", "squared", "rooted", "states"))
    turns_in, turns_out = 2 * DC // UNROLL, DC // UNROLL

    with nc.Block() as block:
        @block.sync
        def _(sp):
            for s in range(UNROLL):
                into.load(sp, 0, s, d["lru_in"][s], first=True)
            sp.dma_start(wa, d["lru_wa"]).then_inc(w_in, 16)
            sp.dma_start(wx, d["lru_wx"]).then_inc(w_in, 16)
            with sp.Fori(1, turns_in) as turn:
                for s in range(UNROLL):
                    into.load(sp, turn, s, tile_of(d["lru_in"], turn, s))
            for half in range(2):
                sp.wait_ge(into.lo_ready[half], turns_in * 2)
            for s in range(UNROLL):
                out.load(sp, 0, s, d["lru_out"][s], first=True)
            with sp.Fori(1, turns_out) as turn:
                for s in range(UNROLL):
                    out.load(sp, turn, s, tile_of(d["lru_out"], turn, s))

        @block.gpsimd
        def _(pool):
            with pool.Fori(0, turns_in) as turn:
                for s in range(UNROLL):
                    into.cut_lo(pool, turn, s)
            with pool.Fori(0, turns_out) as turn:
                for s in range(UNROLL):
                    out.cut_lo(pool, turn, s)

        @block.scalar
        def _(act):
            norm.root(act)
            into.cut_hi(act, 0, 0)
            into.cut_hi(act, 0, 1)
            cut.hi(act, norm.scaled)
            act.wait_ge(lam_abs, 1)
            act.activation(e, z, ACT.Exp, scale=-1.0).then_inc(lam_exp, 1)
            for first, last in ((0, turns_out), (turns_out, turns_in)):
                with act.Fori(first, last - (last == turns_in)) as turn:
                    for s in range(UNROLL):
                        lru_in_out(act, into, gate, xp, turn, s, first, cut_next=True)
            for s in range(UNROLL):
                lru_in_out(act, into, gate, xp, turns_in - 1, s, turns_out, cut_next=s < 2)
            for c in range(DC):
                for k, (dst, bias) in enumerate(((r, "b_a"), (i, "b_x"))):
                    act.wait_ge(gated, 2 * c + k + 1)
                    act.activation(dst[:, c, :], mem.ps[:, 2 + (2 * c + k) % 4, 0:L], ACT.Sigmoid,
                                   bias=mem.vec[:, VEC[bias] + c:VEC[bias] + c + 1]).then_inc(gate_out, 1)
            act.wait_ge(c8_ready, 2)
            act.wait_ge(gate_out, 2 * DC)
            for c in range(DC):
                act.activation(a[:, c, :], r[:, c, :], ACT.Exp, scale=negc8[:, c:c + 1]).then_inc(decays, 1)
            for c in range(DC):
                act.activation(r[:, c, :], r[:, c, :], ACT.Tanh, scale=c8[:, c:c + 1]).then_inc(decays, 1)
            act.wait_ge(squared, 1)
            act.activation(b, b, ACT.Sqrt).then_inc(rooted, 1)
            for half in range(2):
                act.wait_ge(into.done[half], turns_in * 2)
            out.cut_hi(act, 0, 0)
            out.cut_hi(act, 0, 1)
            ycut.hi(act, states)
            with act.Fori(0, turns_out - 1) as turn:
                for s in range(UNROLL):
                    out.wait_product(act, turn, s)
                    out.cut_hi(act, turn + (s + 2) // UNROLL, (s + 2) % UNROLL)
            for s in range(2):
                out.wait_product(act, turns_out - 1, s)
                out.cut_hi(act, turns_out - 1, s + 2)

        @block.vector
        def _(dve):
            step = Steps(dve, dstep)
            lam = mem.vec[:, VEC["lam"]:VEC["lam"] + DC]
            norm.square(dve)
            dve.memset(xp[:, :, 0:CONV - 1], 0.0).then_inc(padded, 1)
            step.done(dve.tensor_scalar(nlam, lam, -1.0, None, ALU.mult))
            dve.tensor_tensor(z, lam, nlam, ALU.max).then_inc(lam_abs, 1)
            norm.scale(dve, xn)
            cut.lo(dve)
            dve.wait_ge(lam_exp, 1)
            step.done(dve.tensor_scalar(z, e, 2.0, None, ALU.add))
            step.done(dve.reciprocal(z, z))
            step.done(dve.tensor_tensor(z, z, e, ALU.mult))
            step.done(dve.tensor_tensor(z2, z, z, ALU.mult))
            step.done(dve.tensor_scalar(poly, z2, 1.0 / 17, 1.0 / 15, ALU.mult, ALU.add))
            for k in (13, 11, 9, 7, 5, 3, 1):
                step.done(dve.tensor_tensor(poly, poly, z2, ALU.mult))
                step.done(dve.tensor_scalar(poly, poly, 1.0 / k, None, ALU.add))
            step.done(dve.tensor_tensor(poly, poly, z, ALU.mult))
            step.done(dve.tensor_scalar(nlam, nlam, 0.0, None, ALU.max))
            step.done(dve.scalar_tensor_tensor(poly, poly, 2.0, nlam, ALU.mult, ALU.add))
            dve.tensor_scalar(c8, poly, LRU_C, None, ALU.mult).then_inc(c8_ready, 1)
            dve.tensor_scalar(negc8, poly, -LRU_C, None, ALU.mult).then_inc(c8_ready, 1)
            dve.wait_ge(padded, 1)
            vec = mem.vec
            for c in range(DC):
                n = DC + c
                dve.wait_ge(into.free[n % 2], n // 2 + 2)
                for j in range(CONV):
                    w = vec[:, VEC[f"cw{j}"] + c:VEC[f"cw{j}"] + c + 1]
                    if j == 0:
                        step.done(dve.tensor_scalar(xc[:, c, :], xp[:, c, 0:L], w,
                                                    vec[:, VEC["conv_b"] + c:VEC["conv_b"] + c + 1], ALU.mult, ALU.add))
                        continue
                    ins = dve.scalar_tensor_tensor(xc[:, c, :], xp[:, c, j:j + L], w, xc[:, c, :], ALU.mult, ALU.add)
                    if j < CONV - 1:
                        step.done(ins)
                    else:
                        ins.then_inc(conved, 1)
            dve.wait_ge(decays, 2 * DC)
            step.done(dve.tensor_tensor(b, a, a, ALU.mult))
            dve.scalar_tensor_tensor(b, b, 1.0, r, ALU.add, ALU.mult).then_inc(squared, 1)
            dve.wait_ge(conved, DC)
            step.done(dve.tensor_tensor(i, i, xc, ALU.mult))
            dve.wait_ge(rooted, 1)
            step.done(dve.tensor_tensor(b, b, i, ALU.mult))
            for c in range(DC):
                dve.tensor_tensor_scan(xc[:, c, :], a[:, c, :], b[:, c, :], 0.0, ALU.mult, ALU.add).then_inc(dstep, 1)
            step.n = step.n + DC
            dve.wait_ge(dstep, step.n)
            for c in range(DC):
                dve.tensor_tensor(b[:, c, :], xc[:, c, :], gate[:, c, :], ALU.mult).then_inc(states, 1)
            ycut.lo(dve)
            with dve.Fori(0, turns_out) as turn:
                for s in range(UNROLL):
                    out.wait_product(dve, turn, s)
                    hc = mem.h[:, bass.ds(turn * UNROLL + s, 1), :]
                    dve.tensor_tensor(hc, hc, out.bank(s).unsqueeze(1), ALU.add).then_inc(out.free[s % 2], 1)

        @block.tensor
        def _(pe):
            into.open(pe)
            out.open(pe)
            norm.add_up(pe)
            cut.wait(pe)
            with pe.Fori(0, turns_in) as turn:
                for s in range(UNROLL):
                    into.multiply(pe, turn, s, into.bank(s))
            pe.wait_ge(w_in, 32)
            for c in range(DC):
                pe.wait_ge(conved, c + 1)
                for k, w in enumerate((wa, wx)):
                    n = 2 * c + k
                    if n >= 4:
                        pe.wait_ge(gate_out, n - 3)
                    pe.matmul(mem.ps[:, 2 + n % 4, 0:L], w[:, c, :], xc[:, c, :], start=True,
                              stop=True).then_inc(gated, 1)
            ycut.wait(pe)
            with pe.Fori(0, turns_out) as turn:
                for s in range(UNROLL):
                    out.multiply(pe, turn, s, out.bank(s))


def lru_in_out(act, into, gate, xp, turn, s, base, cut_next):
    into.wait_product(act, turn, s)
    if cut_next:
        into.cut_hi(act, turn + (s + 2) // UNROLL, (s + 2) % UNROLL)
    c = (turn - base) * UNROLL + s
    c = bass.ds(c, 1) if not isinstance(c, int) else slice(c, c + 1)
    src = into.bank(s).unsqueeze(1)
    if base == 0:
        ins = act.activation(gate[:, c, :], src, ACT.Gelu_apprx_tanh)
    else:
        ins = act.copy(xp[:, c, CONV - 1:], src)
    ins.then_inc(into.free[s % 2], 1)


def peer(nc, ctx, mem, d, layer):
    def sem(name):
        return ctx.sem(f"peer{layer}_{name}")

    T = L if layer == 0 else SEQ
    G, NG = T // GT, T // ST
    act_w = mem.big[:, 0:NK * T].rearrange("p (i t) -> p i t", t=T)
    h = mem.h[:, :, L - T:L]
    take = mem.take
    qt, at = take(HALF * T, (2, G, PH, GT))
    xn, at = take(at, (DC, T))
    spread, _ = take(HALF * T, (G, 3, PH, TOPK))
    scores, at = take(at, (G, 2 * NK))
    rstd, at = take(at, (1, L))
    keys, at = take(at, (2, NK))
    s1, at = take(at, (2, NK))
    s2, at = take(at, (2, NK))
    cand, at = take(at, (TOPK, TOPK))
    cand2, at = take(at, (TOPK, TOPK))
    hot, at = take(at, (2, TOPK, TOPK))
    top, at = take(at, (2, TOPK))
    topi, at = take(at, (2, TOPK))
    best, at = take(at, (2, TOPK))
    place, at = take(at, (2, TOPK))
    ij, at = take(at, (2, G, TOPK))
    gates, at = take(at, (G, TOPK))
    den, at = take(at, (2, G))
    rstd = rstd[:, 0, :]
    topi, place, best_at = topi.bitcast(U32), place.bitcast(U32), best[:, 1, :].bitcast(U32)
    iota = mem.con[:, CON["iota"]:CON["iota"] + P]
    head_mask = mem.con[:, CON["head"]:CON["head"] + PH]
    token_mask = mem.con[:, CON["token"]:CON["token"] + GT]

    norm = Norm(nc, ctx, mem, f"peer{layer}_n", h, DC, VEC[f"ffn{layer}"], xn, rstd[:, 0:T], 2, T)
    cut = Cut(nc, ctx, mem, f"peer{layer}_x", xn, T)
    st = Stream(nc, ctx, mem, f"peer{layer}_s", T)
    keys_in, scored, scores_out, dstep, shifted, exped, spread_done, placed, chosen = (
        sem(n) for n in ("keys_in", "scored", "scores_out", "dve_steps", "shifted", "exped", "spread_done", "placed",
                         "chosen"))
    turns_taken = sem("turns_taken")
    hots_ready, scattered, gated = sem("hots_ready"), sem("scattered"), sem("gated")
    w_hi_cut, w_lo_cut = sem("w_hi_cut"), sem("w_lo_cut")

    TQ, TH = 2 * PH // UNROLL, HALF // UNROLL
    U0, U1, V0, V1, END = TQ, TQ + TH, TQ + 2 * TH, TQ + 3 * TH, TQ + 4 * TH
    MID = U0 + TH * 3 // 4

    if T <= 256:
        pieces = [[(c // 2, 256 * (c % 2), 0, T)] for c in range(DC)]
    else:
        side = 512 - T
        pieces = [[(c, 0, 0, T)] for c in range(6)]
        pieces += [[(b, T, 0, side), (b + 1, T, side, T - side)] for b in (0, 2)]
    GBANK = 6

    def products(pe, half, m, bank):
        pe.wait_ge(hots_ready, half * NG + m + 1)
        for t in range(ST):
            o = mem.ps[:, GBANK + bank, t * HALF:(t + 1) * HALF]
            pe.matmul(o, mem.b_hot[:, t, :], mem.a_hi[:, t, :], start=True, stop=False)
            mm = pe.matmul(o, mem.b_hot[:, t, :], mem.a_lo[:, t, :], start=False, stop=True)
        mm.then_inc(scattered, 1)

    def hots(dve, step, half, m):
        tok = bass.ds(m * ST, ST) if not isinstance(m, int) else slice(m * ST, m * ST + ST)
        wide, wide_a = [P, ST, P], [P, ST, HALF]
        first = iota[:, half * HALF:(half + 1) * HALF]
        dve.wait_ge(scattered, half * NG + m)
        dve.tensor_tensor(mem.b_hot[:, :, :], iota.unsqueeze(1).to_broadcast(wide),
                          mem.idx_j[:, tok].unsqueeze(2).to_broadcast(wide), ALU.is_equal).then_inc(step.sem, 1)
        step.n = step.n + 1
        step.done(dve.tensor_tensor(mem.a_lo[:, :, :], first.unsqueeze(1).to_broadcast(wide_a),
                                    mem.idx_i[:, tok].unsqueeze(2).to_broadcast(wide_a), ALU.is_equal))
        hot_a = mem.a_lo[:, :, :].bitcast(F32)
        step.done(dve.tensor_tensor(mem.a_hi[:, :, :], hot_a,
                                    mem.g_hi[:, tok].bitcast(F32).unsqueeze(2).to_broadcast(wide_a), ALU.mult))
        dve.tensor_tensor(mem.a_lo[:, :, :], hot_a, mem.g_lo[:, tok].bitcast(F32).unsqueeze(2).to_broadcast(wide_a),
                          ALU.mult).then_inc(hots_ready, 1)

    HOT_STEPS = 3

    def gate_act(dve, half, m, bank):
        tok = bass.ds(m * ST, ST) if not isinstance(m, int) else slice(m * ST, m * ST + ST)
        dve.wait_ge(scattered, half * NG + m + 1)
        w = act_w[:, half * HALF:(half + 1) * HALF, tok]
        g = mem.ps[:, GBANK + bank, :].rearrange("p (t i) -> p i t", i=HALF)
        dve.tensor_tensor(w, w, g, ALU.mult).then_inc(gated, 1)

    def cut_w_hi(act, n, r):
        i = bass.ds(n, 1) if not isinstance(n, int) else slice(n, n + 1)
        act.copy(mem.xhi[:, r:r + 1, 0:T], act_w[:, i, :]).then_inc(w_hi_cut, 1)

    def cut_w_lo(dve, n, r):
        i = bass.ds(n, 1) if not isinstance(n, int) else slice(n, n + 1)
        dve.wait_ge(w_hi_cut, n + 1)
        dve.tensor_tensor(mem.xlo[:, r:r + 1, 0:T], act_w[:, i, :], mem.xhi[:, r:r + 1, 0:T].bitcast(F32),
                          ALU.subtract).then_inc(w_lo_cut, 1)

    def apply_v(pe, turn, s, first=False):
        r = s % 2
        pe.wait_ge(st.hi_ready, turn * UNROLL + (s + 1))
        pe.wait_ge(w_lo_cut, (turn - V0) * UNROLL + (s + 1))
        seen = set()
        for w, x in ((mem.whi, mem.xhi), (mem.whi, mem.xlo), (mem.wlo, mem.xhi)):
            if w is mem.wlo:
                pe.wait_ge(st.lo_ready[r], turn * 2 + (s // 2 + 1))
            for c in range(DC):
                for bank, col, tok, n in pieces[c]:
                    mm = pe.matmul(mem.ps[:, bank, col:col + n], w[:, r, c * P:(c + 1) * P], x[:, r, tok:tok + n],
                                   start=first and bank not in seen, stop=False, skip_group_check=True)
                    seen.add(bank)
        mm.then_inc(st.done[r], 1)

    with nc.Block() as block:
        @block.sync
        def _(sp):
            for s in range(UNROLL):
                st.load(sp, 0, s, d["query"][layer, s], first=True)
            sp.dma_start(keys, d["keys"][layer]).then_inc(keys_in, 16)
            with sp.Fori(1, TQ) as turn:
                for s in range(UNROLL):
                    st.load(sp, turn, s, tile_of(d["query"][layer], turn, s))
            with sp.Fori(U0, V0) as turn:
                for s in range(UNROLL):
                    st.load(sp, turn, s, tile_of(d["u"][layer], turn - U0, s))
            with sp.Fori(V0, END) as turn:
                for s in range(UNROLL):
                    st.load(sp, turn, s, tile_of(d["v"][layer], turn - V0, s))

        @block.gpsimd
        def _(pool):
            with pool.Fori(0, U1) as turn:
                for s in range(UNROLL):
                    st.cut_lo(pool, turn, s)
            with pool.Fori(U1, END) as turn:
                for s in (1, 3):
                    st.cut_lo(pool, turn, s)

        @block.scalar
        def _(act):
            norm.root(act)
            st.cut_hi(act, 0, 0)
            st.cut_hi(act, 0, 1)
            cut.hi(act, norm.scaled)
            with act.Fori(0, TQ) as turn:
                for s in range(UNROLL):
                    st.wait_product(act, turn, s)
                    st.cut_hi(act, turn + (s + 2) // UNROLL, (s + 2) % UNROLL)
                    act.copy(qt[:, s % 2, :, bass.ds(turn * 2 + s // 2, 1), :].rearrange("p g a t -> p g (a t)"),
                             st.bank(s).rearrange("p (g t) -> p g t", t=GT)).then_inc(st.free[s % 2], 1)

            def take_act(turn):
                for s in range(UNROLL):
                    st.wait_product(act, turn, s)
                    st.cut_hi(act, turn + (s + 2) // UNROLL, (s + 2) % UNROLL)
                    act.activation(act_w[:, bass.ds((turn - U0) * UNROLL + s, 1), :], st.bank(s).unsqueeze(1),
                                   ACT.Gelu_apprx_tanh).then_inc(st.free[s % 2], 1)

            with act.Fori(U0, MID) as turn:
                take_act(turn)
            act.wait_ge(shifted, 1)
            act.activation(gates, gates, ACT.Exp).then_inc(exped, 1)
            with act.Fori(MID, U1) as turn:
                take_act(turn)
            act.wait_ge(chosen, 1)
            with act.Fori(U1, V0) as turn:
                take_act(turn)
            for r in range(2):
                act.wait_ge(st.done[r], V0 * 2)
            act.wait_ge(gated, NG)
            for r in range(2):
                cut_w_hi(act, r, r)

            def next_v(turn, w=True):
                for s in range(UNROLL):
                    st.wait_product(act, turn, s)
                    st.cut_hi(act, turn + (s + 2) // UNROLL, (s + 2) % UNROLL)
                    if w or s < 2:
                        cut_w_hi(act, (turn - V0) * UNROLL + (s + 2), s % 2)

            with act.Fori(V0, V1 - 1) as turn:
                next_v(turn)
            next_v(V1 - 1, w=False)
            act.wait_ge(gated, 2 * NG)
            for r in range(2):
                cut_w_hi(act, HALF + r, r)
            with act.Fori(V1, END - 1) as turn:
                next_v(turn)
            for s in range(2):
                st.wait_product(act, END - 1, s)
                st.cut_hi(act, END - 1, s + 2)
                cut_w_hi(act, NK - 2 + s, s)

        @block.vector
        def _(dve):
            step = Steps(dve, dstep)
            norm.square(dve)
            norm.scale(dve, xn)
            cut.lo(dve)
            with dve.Fori(0, G // 2) as pair:
                for k in range(2):
                    dve.wait_ge(scored, pair * 2 + (k + 1))
                    dve.tensor_copy(scores[:, bass.ds(pair * 2 + k, 1), :],
                                    mem.ps[:, 2 + k, 0:2 * NK].unsqueeze(1)).then_inc(scores_out, 1)
            if G % 2:
                dve.wait_ge(scored, G)
                dve.tensor_copy(scores[:, G - 1, :], mem.ps[:, 2, 0:2 * NK]).then_inc(scores_out, 1)
            dve.wait_ge(scores_out, G)

            def top16(values, spare, found, found_at):
                for ins in (lambda: dve.max(found[:, 0:8], values),
                            lambda: dve.match_replace(spare, found[:, 0:8], values, NEG),
                            lambda: dve.max(found[:, 8:16], spare),
                            lambda: dve.max_index(found_at[:, 0:8], found[:, 0:8], values),
                            lambda: dve.max_index(found_at[:, 8:16], found[:, 8:16], spare)):
                    dve.sem_inc(turns_taken, 1)
                    step.done(ins())

            per_group = 1 + 2 * 5 + 1 + 5 + 6
            cube = [P, 2, TOPK, TOPK]
            with dve.Fori(0, G) as g:
                step.enter(g, per_group)
                step.done(dve.tensor_copy(s1.rearrange("p a b -> p (a b)").unsqueeze(1), scores[:, bass.ds(g, 1), :]))
                for half in range(2):
                    top16(s1[:, half, :], s2[:, half, :], top[:, half, :], topi[:, half, :])
                step.done(dve.tensor_tensor(cand, top[:, 0, :].unsqueeze(2).to_broadcast([P, TOPK, TOPK]),
                                            top[:, 1, :].unsqueeze(1).to_broadcast([P, TOPK, TOPK]), ALU.add))
                top16(cand.rearrange("p a b -> p (a b)"), cand2.rearrange("p a b -> p (a b)"), best[:, 0, :], best_at)
                step.done(dve.tensor_copy(gates[:, bass.ds(g, 1), :], best[:, 0:1, :]))
                step.done(dve.tensor_scalar(place[:, 0, :], best_at, 4, None, ALU.logical_shift_right))
                step.done(dve.tensor_scalar(place[:, 1, :], best_at, TOPK - 1, None, ALU.bitwise_and))
                step.done(dve.tensor_tensor(hot, iota[:, 0:TOPK].unsqueeze(1).unsqueeze(1).to_broadcast(cube),
                                            place.unsqueeze(3).to_broadcast(cube), ALU.is_equal))
                step.done(dve.tensor_tensor(hot, hot, topi.unsqueeze(2).to_broadcast(cube), ALU.mult))
                step.done(dve.tensor_reduce(ij[:, :, bass.ds(g, 1), :].rearrange("p a g k -> p a (g k)"), hot, AX.X,
                                            ALU.add))
                step.leave(G, per_group)
            wide = [P, G, TOPK]
            step.done(dve.tensor_copy(den[:, 0, :], gates[:, :, 0]))
            dve.tensor_tensor(gates, gates, den[:, 0, :].unsqueeze(2).to_broadcast(wide),
                              ALU.subtract).then_inc(shifted, 1)
            by_head = [P, G, PH, TOPK]
            mask = head_mask.unsqueeze(1).unsqueeze(3).to_broadcast(by_head)
            for w in range(2):
                dve.tensor_tensor(spread[:, :, w, :, :], ij[:, w, :, :].unsqueeze(2).to_broadcast(by_head), mask,
                                  ALU.mult).then_inc(placed, 1)
            dve.wait_ge(exped, 1)
            step.done(dve.tensor_reduce(den[:, 0, :], gates, AX.X, ALU.add))
            step.done(dve.reciprocal(den[:, 1, :], den[:, 0, :]))
            step.done(dve.tensor_tensor(gates, gates, den[:, 1, :].unsqueeze(2).to_broadcast(wide), ALU.mult))
            dve.tensor_tensor(spread[:, :, 2, :, :], gates.unsqueeze(2).to_broadcast(by_head), mask,
                              ALU.mult).then_inc(placed, 1)
            dve.wait_ge(spread_done, 1)
            step.done(dve.tensor_copy(mem.idx_i[:, 0:T], mem.ps[:, 2, 0:T]))
            step.done(dve.tensor_copy(mem.idx_j[:, 0:T], mem.ps[:, 3, 0:T]))
            step.done(dve.tensor_copy(mem.g_hi[:, 0:T], mem.ps[:, 4, 0:T]))
            dve.tensor_tensor(mem.g_lo[:, 0:T], mem.ps[:, 4, 0:T], mem.g_hi[:, 0:T].bitcast(F32),
                              ALU.subtract).then_inc(chosen, 1)
            dve.wait_ge(chosen, 1)

            def scatter_turn(turn, half, base, last):
                step_base = step.n
                for u in range(2):
                    if u == 0 or half == 0 or not last:
                        st.cut_lo(dve, turn + u, 2 * (1 - u))
                    else:
                        st.cut_lo(dve, turn + u, 0)
                    if half == 1:
                        for k in range(2):
                            if not (last and u == 1):
                                cut_w_lo(dve, (turn - V0) * UNROLL + (2 * u + 2 + k), k)
                    m = (turn - base) * 2 + u
                    gate_act(dve, half, m, u)
                    if not (last and u == 1 and NG == 2 * TH):
                        hots(dve, step, half, m + 1)

            def scatter_half(half, base, last_turn):
                for r in range(2):
                    dve.wait_ge(st.free[r], (U1 if half == 0 else V0) * 2 + 1)
                hots(dve, step, half, 0)
                with dve.Fori(base, last_turn) as turn:
                    step.enter(turn - base, 2 * HOT_STEPS)
                    scatter_turn(turn, half, base, False)
                    step.leave(last_turn - base, 2 * HOT_STEPS)
                scatter_turn(last_turn, half, base, True)
                for m in range(2 * TH, NG):
                    gate_act(dve, half, m, m % 2)
                    if m + 1 < NG:
                        hots(dve, step, half, m + 1)

            st.cut_lo(dve, U1, 0)
            scatter_half(0, U1, V0 - 1)
            for r in range(2):
                cut_w_lo(dve, r, r)
            scatter_half(1, V0, V1 - 1)
            for r in range(2):
                cut_w_lo(dve, HALF + r, r)

            def lo_turn(turn, last):
                for u in range(2):
                    if not (last and u == 1):
                        st.cut_lo(dve, turn + u, 2 * (1 - u))
                        for k in range(2):
                            cut_w_lo(dve, (turn - V0) * UNROLL + (2 * u + 2 + k), k)

            with dve.Fori(V1, END - 1) as turn:
                lo_turn(turn, False)
            lo_turn(END - 1, True)
            for r in range(2):
                dve.wait_ge(st.done[r], END * 2)
            for c in range(DC):
                for bank, col, tok, n in pieces[c]:
                    dve.tensor_tensor(h[:, c, tok:tok + n], h[:, c, tok:tok + n], mem.ps[:, bank, col:col + n],
                                      ALU.add).then_inc(chosen, 1)
            dve.wait_ge(chosen, 1 + sum(len(x) for x in pieces))

        @block.tensor
        def _(pe):
            st.open(pe)
            norm.add_up(pe)
            cut.wait(pe)
            with pe.Fori(0, TQ) as turn:
                for s in range(UNROLL):
                    st.multiply(pe, turn, s, st.bank(s))
            pe.wait_ge(keys_in, 16)
            for r in range(2):
                pe.wait_ge(st.free[r], TQ * 2 + 1)

            for g in range(G):
                if g >= 2:
                    pe.wait_ge(scores_out, g - 1)
                for half in range(2):
                    mm = pe.matmul(mem.ps[:, 2 + g % 2, half * NK:(half + 1) * NK],
                                   qt[:, half, g, :, :].rearrange("p h t -> p (h t)"), keys[:, half, :],
                                   start=True, stop=True)
                mm.then_inc(scored, 1)
            with pe.Fori(U0, U1) as turn:
                for s in range(UNROLL):
                    st.multiply(pe, turn, s, st.bank(s))
            pe.wait_ge(placed, 3)
            pe.wait_ge(scores_out, G)
            for g in range(G):
                for w in range(3):
                    mm = pe.matmul(mem.ps[:, 2 + w, g * GT:(g + 1) * GT],
                                   spread[:, g, w, :, :].rearrange("p h k -> p (h k)"), token_mask, start=True,
                                   stop=True)
            mm.then_inc(spread_done, 1)
            with pe.Fori(U1, V0) as turn:
                for s in range(UNROLL):
                    st.multiply(pe, turn, s, st.bank(s))
                    if s % 2:
                        products(pe, 0, (turn - U1) * 2 + s // 2, s // 2)
            for m in range(2 * TH, NG):
                products(pe, 0, m, m % 2)
            for r in range(2):
                pe.wait_ge(st.free[r], V0 * 2 + 1)

            def v_turn(turn, half, first=False):
                for s in range(UNROLL):
                    apply_v(pe, turn, s, first and s == 0)
                    if s % 2 and half == 0:
                        products(pe, 1, (turn - V0) * 2 + s // 2, s // 2)

            v_turn(V0, 0, first=True)
            with pe.Fori(V0 + 1, V1) as turn:
                v_turn(turn, 0)
            for m in range(2 * TH, NG):
                products(pe, 1, m, m % 2)
            with pe.Fori(V1, END) as turn:
                v_turn(turn, 1)


def finish(nc, ctx, mem, d):
    xn, at = mem.take(0, (DC, SEQ))
    rstd, at = mem.take(at, (1, SEQ))
    norm = Norm(nc, ctx, mem, "final", mem.h[:, :, META:L], DC, VEC["final"], xn, rstd[:, 0, :], 2, SEQ)
    stored = ctx.sem("final_stored")
    with nc.Block() as block:
        @block.vector
        def _(dve):
            norm.square(dve)
            norm.scale(dve, xn)

        @block.tensor
        def _(pe):
            norm.add_up(pe)

        @block.scalar
        def _(act):
            norm.root(act)

        @block.sync
        def _(sp):
            for c in range(DC):
                sp.wait_ge(norm.scaled, c + 1)
                sp.dma_start(d["out"][:, c, :], xn[:, c, :]).then_inc(stored, 16)
            sp.wait_ge(stored, 16 * DC)


def trunk(nc, d):
    with ExitStack() as ctx:
        mem = Memory(nc, ctx)
        with Stage(nc) as own:
            mla(nc, own, mem, d)
        with Stage(nc) as own:
            peer(nc, own, mem, d, 0)
        with Stage(nc) as own:
            rglru(nc, own, mem, d)
        with Stage(nc) as own:
            peer(nc, own, mem, d, 1)
        with Stage(nc) as own:
            finish(nc, own, mem, d)


def column_tiles(w):
    *lead, rows, cols = w.shape
    n = len(lead)
    w = w.reshape(*lead, rows // P, P, cols // P, P)
    w = w.transpose(*range(n), n + 2, n + 1, n, n + 3)
    return np.ascontiguousarray(w).reshape(*lead, cols // P, P, rows)


def lay_out(inputs):
    a = {k: np.asarray(v) for k, v in inputs.items()}
    chunked = lambda t: np.ascontiguousarray(t.T.reshape(DC, P, -1).transpose(1, 0, 2))
    columns = lambda v: v.reshape(-1, P).T
    half = ROPE // 2
    swap = np.r_[half:ROPE, 0:half]
    rows = lambda w: np.ascontiguousarray(w.reshape(-1, P, w.shape[-1]).transpose(1, 0, 2))

    w_in = a["mla_w_in"][0]
    lat, kr = w_in[:, :QLORA + KVLORA], w_in[:, QLORA + KVLORA:]
    q_up = a["mla_w_q_up"][0].reshape(QLORA, HEADS, NOPE + ROPE)
    q_rope = q_up[:, :, NOPE:]
    q_up = np.concatenate([x.reshape(QLORA, -1) for x in (q_up[:, :, :NOPE], q_rope, q_rope[:, :, swap])], axis=1)
    kv_up = a["mla_w_kv_up"][0].reshape(KVLORA, HEADS, NOPE + VH)
    kv_up = np.concatenate([x.reshape(KVLORA, -1) for x in (kv_up[:, :, :NOPE], kv_up[:, :, NOPE:])], axis=1)
    vec = [a["mixer_norm"][0], a["mixer_norm"][1], a["ffn_norm"][0], a["ffn_norm"][1], a["final_norm"],
           a["lru_b_gate_a"][0], a["lru_b_gate_x"][0], a["lru_conv_b"][0], *a["lru_conv_w"][0], a["lru_lambda"][0],
           a["mla_q_norm"][0], a["mla_kv_norm"][0]]
    con, idm = constants()
    layers = a["peer_u"].shape[0]
    u = a["peer_u"].reshape(layers, NK, NK, DC, P).transpose(0, 1, 4, 3, 2)
    return {
        "x": chunked(a["x"][0]),
        "meta": chunked(a["meta_tokens"]),
        "pos": np.ascontiguousarray(a["positions"]),
        "con": con,
        "idm": idm,
        "vec": np.ascontiguousarray(np.concatenate([columns(v) for v in vec], axis=1)),
        "mla_down": column_tiles(np.concatenate([lat, kr, kr, kr[:, swap], kr[:, swap]], axis=1)),
        "mla_q_up": rows(q_up),
        "mla_kv_up": rows(kv_up),
        "mla_out": column_tiles(a["mla_w_out"][0]),
        "query": column_tiles(a["peer_w_query"]),
        "keys": np.ascontiguousarray(a["peer_sub_keys"].transpose(0, 3, 1, 2)),
        "u": np.ascontiguousarray(u).reshape(layers, NK, P, D),
        "v": a["peer_v"].reshape(layers, NK, P, D),
        "lru_in": column_tiles(a["lru_w_in"][0]),
        "lru_wa": np.ascontiguousarray(a["lru_w_gate_a"][0].transpose(1, 0, 2)),
        "lru_wx": np.ascontiguousarray(a["lru_w_gate_x"][0].transpose(1, 0, 2)),
        "lru_out": column_tiles(a["lru_w_out"][0]),
    }


def kernel(**inputs):
    import concourse.bacc as bacc
    from concourse.bass_utils import run_bass_kernel_spmd

    nc = bacc.Bacc("TRN2", target_bir_lowering=False, num_devices=1)
    arrays, d = {}, {}
    for name, array in lay_out(inputs).items():
        arrays[f"in_{name}"] = array
        d[name] = nc.dram_tensor(f"in_{name}", array.shape, mybir.dt.from_np(array.dtype), kind="ExternalInput").ap()
    d["out"] = nc.dram_tensor("out_0", (P, DC, SEQ), F32, kind="ExternalOutput").ap()
    trunk(nc, d)
    result = run_bass_kernel_spmd(nc, [arrays], core_ids=[0])
    out = result.results[0]["out_0"]
    return np.ascontiguousarray(out.transpose(2, 1, 0)).reshape(1, SEQ, D)
```

```python
from contextlib import ExitStack

import numpy as np

import concourse.bass as bass
from concourse import mybir

P = 128
D = 1024
DC = D // P
SEQ = 256
META = 16
L = SEQ + META
EPS = 1e-6

HEADS, NOPE, ROPE, VH = 8, 128, 64, 128
QLORA, KVLORA = 384, 256
QC, KVC = QLORA // P, KVLORA // P
SCALE = float(1.0 / np.sqrt(NOPE + ROPE))
Q0 = (0, 128, L - P)
NKEYS_SEEN = (128, 256, L)

PH, NK, TOPK, QH = 8, 128, 16, 128
GT = 16
HALF = NK // 2
ST = 8
PARTS = 3
UNROLL = 4
HW = D // 2
HALVES = 2 * UNROLL
SLOTS = 4

CONV = 4
LRU_C = 8.0

BIG = NK * L
NEG = -3.0e38

ALU = mybir.AluOpType
ACT = mybir.ActivationFunctionType
AX = mybir.AxisListType
F32 = mybir.dt.float32
F32R = mybir.dt.float32r
BF16 = mybir.dt.bfloat16
U32 = mybir.dt.uint32
I32 = mybir.dt.int32

VEC = {}
for _i, _n in enumerate(["mix0", "mix1", "ffn0", "ffn1", "final", "b_a", "b_x", "conv_b", "cw0", "cw1", "cw2",
                         "cw3", "lam"]):
    VEC[_n] = _i * DC
VEC["q_norm"] = 13 * DC
VEC["kv_norm"] = VEC["q_norm"] + QC
NVEC = VEC["kv_norm"] + KVC

CON = {"iota": 0, "head": P, "token": P + PH, "freq": P + PH + GT, "sign": P + PH + GT + 1,
       "eps": P + PH + GT + 2}
NCON = P + PH + GT + 3


def constants():
    p = np.arange(P)
    con = np.zeros((P, NCON), np.float32)
    con[:, :P] = np.arange(P)
    con[:, CON["head"]:CON["head"] + PH] = (p[:, None] // GT) == np.arange(PH)
    con[:, CON["token"]:CON["token"] + GT] = (p[:, None] % GT) == np.arange(GT)
    half = ROPE // 2
    freqs = np.float32(10000.0) ** (-np.arange(half, dtype=np.float32) / np.float32(half))
    con[:, CON["freq"]] = freqs[p % half]
    con[:, CON["eps"]] = EPS
    con[:, CON["sign"]] = np.where(p % ROPE < half, -1.0, 1.0)
    x = np.arange(L) - (L - P)
    tri = np.where(x[None, :] > p[:, None], -1e30, 0.0)
    return con, np.concatenate([np.eye(P), tri], axis=1).astype(np.float32)


class Steps:

    def __init__(self, eng, sem):
        self.eng, self.sem, self.n = eng, sem, 0

    def done(self, ins):
        ins.then_inc(self.sem, 1)
        self.n = self.n + 1
        self.eng.wait_ge(self.sem, self.n)

    def add(self, ins):
        ins.then_inc(self.sem, 1)
        self.n = self.n + 1

    def wait(self, back):
        self.eng.wait_ge(self.sem, self.n - (back - 1))

    def enter(self, turn, per_turn):
        self.base = self.n
        self.n = turn * per_turn + self.base

    def leave(self, turns, per_turn):
        self.n = self.base + turns * per_turn


class Stage:

    def __init__(self, nc):
        self.nc, self.sems = nc, []

    def __enter__(self):
        return self

    def sem(self, name):
        self.sems.append(self.nc.alloc_semaphore(name))
        return self.sems[-1]

    def __exit__(self, kind, *_):
        if kind is None:
            self.nc.clear_and_free_semaphores(self.sems)
            self.nc.all_engine_barrier()


class Memory:

    def __init__(self, nc, ctx):
        def sb(name, shape, dt=F32):
            return ctx.enter_context(nc.sbuf_tensor(name, shape, dt))

        self.big = sb("big", [P, BIG])
        self.h = sb("h", [P, DC, L])
        self.xhi = sb("xhi", [P, DC, L], F32R)
        self.xlo = sb("xlo", [P, DC, L], F32R)
        self.raw = sb("raw", [P, UNROLL, D])
        self.whi = sb("whi", [P, SLOTS, HW], F32R)
        self.wlo = sb("wlo", [P, SLOTS, HW], F32R)
        self.j_hot = sb("j_hot", [P, P, ST], BF16)
        self.i_hot = sb("i_hot", [P, HALF, ST], BF16)
        self.i_gate = sb("i_gate", [P, PARTS, HALF, ST], BF16)
        self.iota = sb("iota", [P, P, ST], BF16)
        self.idx = sb("idx", [P, 2, L], BF16)
        self.g = sb("g", [P, PARTS, L], BF16)
        self.con = sb("con", [P, NCON])
        self.vec = sb("vec", [P, NVEC])
        self.token = sb("token", [P, GT], BF16)
        self.ones = sb("ones", [P, P])
        self.unread = sb("unread", [P, 4])
        self.ps = ctx.enter_context(nc.psum_tensor("ps", [P, 8, 512], F32))

    def take(self, at, shape):
        n = int(np.prod(shape))
        assert at + n <= BIG, (at, shape)
        v = self.big[:, at:at + n]
        if len(shape) == 2:
            v = v.rearrange("p (a b) -> p a b", b=shape[1])
        if len(shape) == 3:
            v = v.rearrange("p (a b c) -> p a b c", b=shape[1], c=shape[2])
        if len(shape) == 4:
            v = v.rearrange("p (a b c d) -> p a b c d", b=shape[1], c=shape[2], d=shape[3])
        return v, at + n


class Stream:

    def __init__(self, nc, ctx, mem, name, tokens):
        def sem(what):
            return ctx.sem(f"{name}_{what}")

        self.mem, self.T = mem, tokens
        self.landed = [sem(f"landed{s}") for s in range(UNROLL)]
        self.hi_ready = sem("hi_ready")
        self.lo_ready = [sem(f"lo_ready{k}") for k in range(SLOTS)]
        self.done = sem("done")
        self.free = [sem(f"free{r}") for r in range(2)]

    def load(self, sp, turn, s, src, first=False):
        if not first:
            for e in range(2):
                sp.wait_ge(self.lo_ready[(2 * s + e) % SLOTS], turn * 2 + (s // 2 - 1))
        sp.dma_start(self.mem.raw[:, s, :], src).then_inc(self.landed[s], 16)

    def cut_hi(self, act, turn, s, first=False):
        act.wait_ge(self.landed[s], turn * 16 + 16)
        for e in range(2):
            q = 2 * s + e
            if not first:
                act.wait_ge(self.done, turn * HALVES + (q + 1 - SLOTS))
            act.copy(self.mem.whi[:, q % SLOTS, :], self.mem.raw[:, s, e * HW:(e + 1) * HW]).then_inc(self.hi_ready, 1)

    def cut_lo(self, eng, turn, s, e):
        q = 2 * s + e
        eng.wait_ge(self.hi_ready, turn * HALVES + (q + 1))
        eng.tensor_tensor(self.mem.wlo[:, q % SLOTS, :], self.mem.raw[:, s, e * HW:(e + 1) * HW],
                          self.mem.whi[:, q % SLOTS, :].bitcast(F32),
                          ALU.subtract).then_inc(self.lo_ready[q % SLOTS], 1)

    def open(self, pe):
        for free in self.free:
            pe.sem_inc(free, 1)

    def wait_hi(self, pe, turn, s, e):
        pe.wait_ge(self.hi_ready, turn * HALVES + (2 * s + e + 1))

    def wait_lo(self, pe, turn, s, e):
        q = 2 * s + e
        pe.wait_ge(self.lo_ready[q % SLOTS], turn * 2 + (q // SLOTS + 1))

    def multiply(self, pe, turn, s, out, cut=None):
        m = self.mem
        pe.wait_ge(self.free[s % 2], turn * 2 + (s // 2 + 1))
        for e in range(2):
            k = (2 * s + e) % SLOTS
            self.wait_hi(pe, turn, s, e)
            for c in range(DC // 2):
                w, x = m.whi[:, k, c * P:(c + 1) * P], e * DC // 2 + c
                if cut:
                    cut.ready(pe, x)
                pe.matmul(out, w, m.xhi[:, x, 0:self.T], start=(x == 0), stop=False)
                pe.matmul(out, w, m.xlo[:, x, 0:self.T], start=False, stop=False)
            self.wait_lo(pe, turn, s, e)
            for c in range(DC // 2):
                x = e * DC // 2 + c
                mm = pe.matmul(out, m.wlo[:, k, c * P:(c + 1) * P], m.xhi[:, x, 0:self.T], start=False,
                               stop=(x == DC - 1))
            mm.then_inc(self.done, 1)

    def wait_product(self, eng, turn, s):
        eng.wait_ge(self.done, turn * HALVES + 2 * (s + 1))

    def bank(self, s):
        return self.mem.ps[:, s % 2, 0:self.T]


class Norm:

    def __init__(self, nc, ctx, mem, name, src, chunks, gain, squares, rstd, bank, tokens):
        def sem(what):
            return ctx.sem(f"{name}_{what}")

        self.mem, self.src, self.C, self.gain = mem, src, chunks, gain
        self.squares, self.rstd, self.T = squares, rstd, tokens
        self.sum = mem.ps[:, bank, 0:tokens]
        self.rows = chunks // 2 if chunks == DC else chunks
        self.squared, self.added, self.summed = sem("squared"), sem("added"), sem("summed")
        self.rooted, self.scaled = sem("rooted"), sem("scaled")

    def square_half(self, act):
        act.activation(self.squares[:, self.rows:, :], self.src[:, self.rows:, :], ACT.Square).then_inc(self.squared, 1)

    def square(self, dve):
        first, r = self.squares[:, 0:self.rows, :], self.rows
        ins = dve.tensor_tensor(first, self.src[:, 0:r, :], self.src[:, 0:r, :], ALU.mult)
        if r < self.C:
            ins.then_inc(self.squared, 1)
            dve.wait_ge(self.squared, 2)
            ins = dve.tensor_tensor(first, first, self.squares[:, r:, :], ALU.add)
        ins.then_inc(self.added, 1)

    def add_up(self, pe):
        pe.wait_ge(self.added, 1)
        for c in range(self.rows):
            mm = pe.matmul(self.sum, self.mem.ones[:, :], self.squares[:, c, :], start=(c == 0),
                           stop=(c == self.rows - 1))
        mm.then_inc(self.summed, 1)

    def root(self, act):
        act.wait_ge(self.summed, 1)
        act.activation(self.rstd, self.sum, ACT.Ln, bias=self.mem.con[:, CON["eps"]:CON["eps"] + 1],
                       scale=1.0 / (self.C * P)).then_inc(self.rooted, 1)
        act.wait_ge(self.rooted, 1)
        act.activation(self.rstd, self.rstd, ACT.Exp, scale=-0.5).then_inc(self.rooted, 1)

    def scale(self, dve, out):
        dve.wait_ge(self.rooted, 2)
        for c in range(self.C):
            dve.scalar_tensor_tensor(out[:, c, :], self.src[:, c, :], self.mem.vec[:, self.gain + c:self.gain + c + 1],
                                     self.rstd, ALU.mult, ALU.mult).then_inc(self.scaled, 1)


class Cut:

    def __init__(self, nc, ctx, mem, name, src, tokens):
        self.mem, self.src, self.T = mem, src, tokens
        self.hi_cut = ctx.sem(f"{name}_hi_cut")
        self.lo_cut = [ctx.sem(f"{name}_lo_cut{k}") for k in range(2)]

    def hi(self, act, *ready):
        for c in range(DC):
            act.wait_ge(ready[c % len(ready)], c // len(ready) + 1)
            act.copy(self.mem.xhi[:, c, 0:self.T], self.src[:, c, :]).then_inc(self.hi_cut, 1)

    def lo_chunk(self, eng, c):
        eng.wait_ge(self.hi_cut, c + 1)
        eng.tensor_tensor(self.mem.xlo[:, c, 0:self.T], self.src[:, c, :], self.mem.xhi[:, c, 0:self.T].bitcast(F32),
                          ALU.subtract).then_inc(self.lo_cut[c % 2], 1)

    def lo(self, eng, odd):
        for c in range(odd, DC, 2):
            self.lo_chunk(eng, c)

    def ready(self, pe, c):
        pe.wait_ge(self.hi_cut, c + 1)
        pe.wait_ge(self.lo_cut[c % 2], c // 2 + 1)


def mla(nc, ctx, mem, d):
    def sem(name):
        return ctx.sem("mla_" + name)

    take = mem.take
    lat, at = take(0, (QC + KVC, L))
    kr, at = take(at, (2, L))
    latn, at = take(at, (QC + KVC, L))
    qn, at = take(at, (HEADS, L))
    kn, at = take(at, (HEADS, L))
    qr, at = take(at, (HEADS // 2, L))
    qs, at = take(at, (HEADS // 2, L))
    v, at = take(at, (3, HEADS * VH))
    wq, at = take(at, (QC, 2 * HEADS * P))
    wkv, at = take(at, (KVC, 2 * HEADS * P))
    cosv, at = take(at, (1, L))
    sinv, at = take(at, (1, L))
    ang, at = take(at, (1, L))
    tmp, at = take(at, (1, L))
    rstd, at = take(at, (2, L))
    idm, at = take(at, (1, P + L))
    post, at = take(at, (1, L))
    xn, at = take(at, (DC, L))
    sm = xn[:, 0:3, :], xn[:, 3:6, :]
    pt = latn[:, 0:3, :]
    o, at = take(at, (HEADS, L))
    small = wq[:, 0, 0:16], wq[:, 0, 16:32]
    ident, smask = idm[:, 0, 0:P], idm[:, 0, P:P + L]
    kpe, post = kr[:, 0, :], post[:, 0, :]
    posi = post.bitcast(I32)
    cosv, sinv, ang, tmp = cosv[:, 0, :], sinv[:, 0, :], ang[:, 0, :], tmp[:, 0, :]

    iota_set = sem("iota_set")
    consts_in, x_in, w_in, pos_in, ones_set = sem("consts_in"), sem("x_in"), sem("w_in"), sem("pos_in"), sem("ones")
    dstep, pos_ready, pos_spread, reduced, sines, angles = (
        sem("dve_steps"), sem("pos_ready"), sem("pos_spread"), sem("reduced"), sem("sines"), sem("angles"))
    up_done, up_out, rotated = sem("up_done"), [sem(f"up_out{r}") for r in range(2)], sem("rotated")
    scored, top_found, exped, probs, turned, turned_out, weighed, o_out = (
        sem("scored"), sem("top_found"), sem("exped"), sem("probs"), sem("turned"),
        sem("turned_out"), sem("weighed"), sem("o_out"))

    norm = Norm(nc, ctx, mem, "mla_n", mem.h[:, :, :], DC, VEC["mix0"], xn, rstd[:, 0, :], 2, L)
    cut = Cut(nc, ctx, mem, "mla_x", xn, L)
    down = Stream(nc, ctx, mem, "mla_down", L)
    norm_q = Norm(nc, ctx, mem, "mla_nq", lat[:, 0:QC, :], QC, VEC["q_norm"], latn[:, 0:QC, :], rstd[:, 0, :], 2, L)
    norm_kv = Norm(nc, ctx, mem, "mla_nkv", lat[:, QC:, :], KVC, VEC["kv_norm"], latn[:, QC:, :], rstd[:, 1, :], 3,
                   L)
    out_cut = Cut(nc, ctx, mem, "mla_o", o, L)
    proj = Stream(nc, ctx, mem, "mla_out", L)
    n_down = QC + KVC + 2
    X_LOADS = 3
    ups = ([(qn[:, h, :], wq, h * P, 0, QC) for h in range(HEADS)]
           + [(qr[:, h, :], wq, (HEADS + h) * P, 0, QC) for h in range(HEADS // 2)]
           + [(qs[:, h, :], wq, (HEADS + HEADS // 2 + h) * P, 0, QC) for h in range(HEADS // 2)]
           + [(kn[:, h, :], wkv, h * P, QC, KVC) for h in range(HEADS)])
    vals = [(t, min(P, L - t * P), half) for t in range(3) for half in range(2)]
    n_up = len(ups) + len(vals)

    def take_up(copy, n):
        if n < len(ups):
            return copy(ups[n][0], mem.ps[:, 4 + n % 4, 0:L])
        t, rows, half = vals[n - len(ups)]
        return copy(v[0:rows, t, half * 512:half * 512 + 512], mem.ps[0:rows, 4 + n % 4, :])

    with nc.Block() as block:
        @block.sync
        def _(sp):
            sp.dma_start(mem.h[:, :, 0:META], d["meta"]).then_inc(x_in, 16)
            for c in range(X_LOADS - 1):
                sp.dma_start(mem.h[:, 4 * c:4 * c + 4, META:L], d["x"][:, 4 * c:4 * c + 4, :]).then_inc(x_in, 16)
            sp.dma_start(mem.con[:, :], d["con"]).then_inc(consts_in, 16)
            sp.dma_start(mem.vec[:, :], d["vec"]).then_inc(consts_in, 16)
            sp.dma_start(idm[:, 0, :], d["idm"]).then_inc(consts_in, 16)
            sp.dma_start(posi[0:1, META:L], d["pos"]).then_inc(pos_in, 16)
            for n in range(UNROLL):
                down.load(sp, 0, n, d["mla_down"][n], first=True)
            sp.dma_start(wq, d["mla_q_up"]).then_inc(w_in, 16)
            sp.dma_start(wkv, d["mla_kv_up"]).then_inc(w_in, 16)
            for n in range(UNROLL, n_down):
                down.load(sp, n // UNROLL, n % UNROLL, d["mla_down"][n])
            for k in range(SLOTS):
                sp.wait_ge(down.lo_ready[k], (2 * n_down - k + SLOTS - 1) // SLOTS)
            for s in range(UNROLL):
                proj.load(sp, 0, s, d["mla_out"][s], first=True)
            with sp.Fori(1, DC // UNROLL) as turn:
                for s in range(UNROLL):
                    proj.load(sp, turn, s, tile_of(d["mla_out"], turn, s))

        @block.gpsimd
        def _(pool):
            for n in range(n_down):
                if n == 1:
                    cut.lo(pool, 1)
                for e in range(2):
                    down.cut_lo(pool, n // UNROLL, n % UNROLL, e)
            lo_of_turns(pool, proj, DC // UNROLL, out_cut)

        @block.scalar
        def _(act):
            act.wait_ge(x_in, 16 * X_LOADS)
            norm.square_half(act)
            act.wait_ge(consts_in, 48)
            down.cut_hi(act, 0, 0, first=True)
            norm.root(act)
            down.cut_hi(act, 0, 1, first=True)
            cut.hi(act, norm.scaled)
            act.wait_ge(reduced, 1)
            act.activation(sinv, ang, ACT.Sin).then_inc(sines, 1)
            act.activation(cosv, ang, ACT.Sin, scale=0.5).then_inc(sines, 1)
            for n in range(n_down):
                down.wait_product(act, n // UNROLL, n % UNROLL)
                if n + 2 < n_down:
                    down.cut_hi(act, (n + 2) // UNROLL, (n + 2) % UNROLL)
                dst = lat[:, n, :] if n < QC + KVC else kr[:, n - QC - KVC, :]
                act.copy(dst, down.bank(n)).then_inc(down.free[n % 2], 1)
            norm_q.root(act)
            norm_kv.root(act)
            for n in range(1, n_up, 2):
                act.wait_ge(up_done, n + 1)
                take_up(act.copy, n).then_inc(up_out[1], 1)
            act.wait_ge(down.done, 2 * n_down)
            proj.cut_hi(act, 0, 0, first=True)
            proj.cut_hi(act, 0, 1, first=True)

            def exps(head, e):
                for t in range(3):
                    nk = NKEYS_SEEN[t]
                    act.wait_ge(top_found, head * 3 + (t + 1))
                    act.activation(sm[e][:, t, 0:nk], sm[e][:, t, 0:nk], ACT.Exp, bias=small[e][:, t:t + 1],
                                   accum_out=small[e][:, 3 + t:4 + t]).then_inc(exped, 1)

            def take_out(head):
                for k in range(3):
                    rows = min(P, L - k * P)
                    first = Q0[2] if k == 2 else k * P
                    act.wait_ge(turned, head * 3 + (k + 1))
                    act.copy(pt[0:rows, k, first:L], mem.ps[0:rows, 3 + k, first:L]).then_inc(turned_out, 1)
                act.wait_ge(weighed, head + 1)
                at_head = bass.ds(head, 1) if not isinstance(head, int) else slice(head, head + 1)
                act.copy(o[:, at_head, :], mem.ps[:, 7:8, 0:L]).then_inc(o_out, 1)

            exps(0, 0)
            with act.Fori(0, HEADS // 2 - 1) as pair:
                for e in range(2):
                    exps(pair * 2 + (e + 1), 1 - e)
                    take_out(pair * 2 + e)
            exps(HEADS - 1, 1)
            take_out(HEADS - 2)
            take_out(HEADS - 1)
            act.wait_ge(o_out, HEADS)
            out_cut.hi(act, o_out)
            with act.Fori(0, DC // UNROLL - 1) as turn:
                for s in range(UNROLL):
                    proj.wait_product(act, turn, s)
                    proj.cut_hi(act, turn + (s + 2) // UNROLL, (s + 2) % UNROLL)
            for s in range(2):
                proj.wait_product(act, DC // UNROLL - 1, s)
                proj.cut_hi(act, DC // UNROLL - 1, s + 2)

        @block.vector
        def _(dve):
            step = Steps(dve, dstep)
            dve.memset(mem.ones[:, :], 1.0).then_inc(ones_set, 1)
            dve.wait_ge(x_in, 16 * X_LOADS)
            norm.square(dve)
            dve.wait_ge(consts_in, 48)
            dve.tensor_copy(post[0:1, 0:META], mem.con[0:1, 0:META]).then_inc(pos_ready, 1)
            dve.wait_ge(pos_in, 16)
            dve.tensor_scalar(post[0:1, META:L], posi[0:1, META:L], float(META), None,
                              ALU.add).then_inc(pos_ready, 1)
            norm.scale(dve, xn)
            cut.lo(dve, 0)
            dve.tensor_copy(mem.iota[:, :, :], mem.con[:, 0:P].unsqueeze(2).to_broadcast([P, P, ST])).then_inc(iota_set, 1)
            dve.tensor_copy(mem.token[:, :], mem.con[:, CON["token"]:CON["token"] + GT]).then_inc(iota_set, 1)
            dve.wait_ge(iota_set, 2)
            two_pi = (6.28125, float(np.float32(2 * np.pi - 6.28125) // 2.0 ** -20 * 2.0 ** -20))
            rest = 2 * np.pi - two_pi[0] - two_pi[1]
            magic = 1.5 * 2.0 ** 23
            dve.wait_ge(pos_spread, 1)
            step.done(dve.tensor_scalar(ang, mem.ps[:, 3, 0:L], mem.con[:, CON["freq"]:CON["freq"] + 1], None,
                                        ALU.mult))
            step.done(dve.tensor_scalar(tmp, ang, float(1 / (2 * np.pi)), magic, ALU.mult, ALU.add))
            step.done(dve.tensor_scalar(tmp, tmp, -magic, None, ALU.add))
            for part in (*two_pi, rest):
                step.done(dve.scalar_tensor_tensor(ang, tmp, -float(part), ang, ALU.mult, ALU.add))
            dve.tensor_scalar(ang, ang, float(np.float32(-np.pi)), float(np.float32(np.pi)), ALU.max,
                              ALU.min).then_inc(reduced, 1)
            dve.wait_ge(sines, 2)
            step.done(dve.tensor_tensor(cosv, cosv, cosv, ALU.mult))
            step.done(dve.tensor_scalar(cosv, cosv, -2.0, 1.0, ALU.mult, ALU.add))
            step.done(dve.tensor_scalar(sinv, sinv, mem.con[:, CON["sign"]:CON["sign"] + 1], None, ALU.mult))
            dve.wait_ge(down.free[0], (n_down + 1) // 2 + 1)
            dve.wait_ge(down.free[1], n_down // 2 + 1)
            norm_q.square(dve)
            norm_kv.square(dve)
            step.done(dve.tensor_tensor(kr[:, 0, :], kr[:, 0, :], cosv, ALU.mult))
            step.done(dve.tensor_tensor(kr[:, 1, :], kr[:, 1, :], sinv, ALU.mult))
            dve.tensor_tensor(kr[:, 0, :], kr[:, 0, :], kr[:, 1, :], ALU.add).then_inc(rotated, 1)
            norm_q.scale(dve, latn[:, 0:QC, :])
            norm_kv.scale(dve, latn[:, QC:, :])
            for n in range(0, n_up, 2):
                dve.wait_ge(up_done, n + 1)
                take_up(dve.tensor_copy, n).then_inc(up_out[0], 1)
            dve.wait_ge(up_out[0], (n_up + 1) // 2)
            dve.wait_ge(up_out[1], n_up // 2)
            wide = [P, HEADS // 2, L]
            step.done(dve.tensor_tensor(qr, qr, cosv.unsqueeze(1).to_broadcast(wide), ALU.mult))
            step.done(dve.tensor_tensor(qs, qs, sinv.unsqueeze(1).to_broadcast(wide), ALU.mult))
            dve.tensor_tensor(qr, qr, qs, ALU.add).then_inc(rotated, 1)

            def tops(head, e):
                for t in range(3):
                    nk = NKEYS_SEEN[t]
                    dve.wait_ge(scored, head * 3 + (t + 1))
                    step.add(dve.scalar_tensor_tensor(sm[e][:, t, 0:nk], mem.ps[:, t, 0:nk], SCALE,
                                                      smask[:, L - P - Q0[t]:L - P - Q0[t] + nk], ALU.mult, ALU.add))
                    step.wait(1)
                    dve.tensor_reduce(small[e][:, t:t + 1], sm[e][:, t, 0:nk], AX.X, ALU.max,
                                      negate=True).then_inc(top_found, 1)

            def divide(head, e):
                for t in range(3):
                    nk = NKEYS_SEEN[t]
                    dve.wait_ge(exped, head * 3 + (t + 1))
                    step.done(dve.reciprocal(small[e][:, 6 + t:7 + t], small[e][:, 3 + t:4 + t]))
                    dve.tensor_scalar(sm[e][:, t, 0:nk], sm[e][:, t, 0:nk], small[e][:, 6 + t:7 + t], None,
                                      ALU.mult).then_inc(probs, 1)

            per_pair = 2 * 3 * 2
            tops(0, 0)
            with dve.Fori(0, HEADS // 2 - 1) as pair:
                step.enter(pair, per_pair)
                for e in range(2):
                    divide(pair * 2 + e, e)
                    tops(pair * 2 + (e + 1), 1 - e)
                step.leave(HEADS // 2 - 1, per_pair)
            divide(HEADS - 2, 0)
            tops(HEADS - 1, 1)
            divide(HEADS - 1, 1)
            out_cut.lo(dve, 0)
            with dve.Fori(0, DC // UNROLL) as turn:
                for s in range(UNROLL):
                    proj.wait_product(dve, turn, s)
                    hc = mem.h[:, bass.ds(turn * UNROLL + s, 1), :]
                    dve.tensor_tensor(hc, hc, proj.bank(s).unsqueeze(1), ALU.add).then_inc(proj.free[s % 2], 1)

        @block.tensor
        def _(pe):
            down.open(pe)
            proj.open(pe)
            pe.wait_ge(ones_set, 1)
            norm.add_up(pe)
            pe.wait_ge(pos_ready, 2)
            pe.matmul(mem.ps[:, 3, 0:L], mem.ones[0:1, :], post[0:1, :], start=True, stop=True).then_inc(pos_spread, 1)
            for n in range(n_down):
                down.multiply(pe, n // UNROLL, n % UNROLL, down.bank(n), cut if n == 0 else None)
            pe.wait_ge(reduced, 1)
            norm_q.add_up(pe)
            norm_kv.add_up(pe)
            pe.wait_ge(w_in, 32)
            pe.wait_ge(norm_q.scaled, QC)
            pe.wait_ge(norm_kv.scaled, KVC)
            for n in range(n_up):
                if n >= 4:
                    pe.wait_ge(up_out[n % 2], (n - 4) // 2 + 1)
                bank = 4 + n % 4
                if n < len(ups):
                    _, w, col, c0, count = ups[n]
                    for c in range(count):
                        mm = pe.matmul(mem.ps[:, bank, 0:L], w[:, c, col:col + P], latn[:, c0 + c, :], start=(c == 0),
                                       stop=(c == count - 1))
                else:
                    t, rows, half = vals[n - len(ups)]
                    for c in range(KVC):
                        mm = pe.matmul(mem.ps[0:rows, bank, :], latn[:, QC + c, t * P:t * P + rows],
                                       wkv[:, c, HEADS * P + half * 512:HEADS * P + half * 512 + 512], start=(c == 0),
                                       stop=(c == KVC - 1))
                mm.then_inc(up_done, 1)
            pe.wait_ge(rotated, 2)
            pe.wait_ge(up_out[0], (n_up + 1) // 2)
            pe.wait_ge(up_out[1], n_up // 2)

            def scores(head):
                pair, lanes = head // 2, slice(ROPE * (head % 2), ROPE * (head % 2) + ROPE)
                for t in range(3):
                    nk = NKEYS_SEEN[t]
                    if head:
                        pe.wait_ge(top_found, (head - 1) * 3 + t + 1)
                    pe.matmul(mem.ps[:, t, 0:nk], qn[:, head, Q0[t]:Q0[t] + P], kn[:, head, 0:nk], start=True,
                              stop=False)
                    pe.matmul(mem.ps[:, t, 0:nk], qr[lanes, pair, Q0[t]:Q0[t] + P], kpe[lanes, 0:nk], start=False,
                              stop=True).then_inc(scored, 1)

            scores(0)
            scores(1)
            for head in range(HEADS):
                for k in range(3):
                    rows = min(P, L - k * P)
                    for t in range(k, 3):
                        pe.wait_ge(probs, head * 3 + t + 1)
                        tr = pe.transpose(mem.ps[0:rows, 3 + k, Q0[t]:Q0[t] + P],
                                          sm[head % 2][:, t, k * P:k * P + rows], ident)
                    tr.then_inc(turned, 1)
                if head + 2 < HEADS:
                    scores(head + 2)
                pe.wait_ge(o_out, head)
                for k in range(3):
                    rows = min(P, L - k * P)
                    first = Q0[2] if k == 2 else k * P
                    pe.wait_ge(turned_out, head * 3 + k + 1)
                    mm = pe.matmul(mem.ps[:, 7, first:L], v[0:rows, k, head * P:head * P + P], pt[0:rows, k, first:L],
                                   start=(k == 0), stop=(k == 2))
                mm.then_inc(weighed, 1)
            multiply_turns(pe, proj, 0, DC // UNROLL, out_cut)


def lo_of_turns(pool, stream, turns, cut):
    for s in range(UNROLL):
        if s == 1:
            cut.lo(pool, 1)
        for e in range(2):
            stream.cut_lo(pool, 0, s, e)
    with pool.Fori(1, turns) as turn:
        for s in range(UNROLL):
            for e in range(2):
                stream.cut_lo(pool, turn, s, e)


def multiply_turns(pe, stream, first, last, cut):
    for s in range(UNROLL):
        stream.multiply(pe, first, s, stream.bank(s), cut if s == 0 else None)
    with pe.Fori(first + 1, last) as turn:
        for s in range(UNROLL):
            stream.multiply(pe, turn, s, stream.bank(s))


def tile_of(tiles, turn, s):
    return tiles[bass.ds(turn * UNROLL + s, 1)].rearrange("a p f -> p (a f)")


def rglru(nc, ctx, mem, d):
    def sem(name):
        return ctx.sem("lru_" + name)

    take = mem.take
    xn, at = take(0, (DC, L))
    gate, at = take(at, (DC, L))
    xp, at = take(at, (DC, L + CONV - 1))
    xc, at = take(at, (DC, L))
    r, at = take(at, (DC, L))
    i, at = take(at, (DC, L))
    a, at = take(at, (DC, L))
    b, at = take(at, (DC, L))
    wa, at = take(at, (DC, P))
    wx, at = take(at, (DC, P))
    rstd, at = take(at, (1, L))
    small, at = take(at, (9, DC))
    rstd = rstd[:, 0, :]
    nlam, e, z, z2, poly, c8, negc8, half_ba, half_bx = (small[:, n, :] for n in range(9))

    norm = Norm(nc, ctx, mem, "lru_n", mem.h[:, :, :], DC, VEC["mix1"], xn, rstd, 2, L)
    cut = Cut(nc, ctx, mem, "lru_x", xn, L)
    st = Stream(nc, ctx, mem, "lru_s", L)
    ycut = Cut(nc, ctx, mem, "lru_y", b, L)
    dstep, padded, w_in, conved, gated, gate_out, lam_abs, lam_exp, ready, decays, squared, rooted, scanned, gelus = (
        sem(n) for n in ("dve_steps", "padded", "w_in", "conved", "gated", "gate_out", "lam_abs", "lam_exp",
                         "ready", "decays", "squared", "rooted", "scanned", "gelus"))
    states = [sem("states_even"), sem("states_odd")]
    GATE, OUT, END = DC // UNROLL, 2 * DC // UNROLL, 3 * DC // UNROLL

    with nc.Block() as block:
        @block.sync
        def _(sp):
            for s in range(UNROLL):
                st.load(sp, 0, s, d["lru_w"][s], first=True)
            sp.dma_start(wa, d["lru_wa"]).then_inc(w_in, 16)
            sp.dma_start(wx, d["lru_wx"]).then_inc(w_in, 16)
            with sp.Fori(1, END) as turn:
                for s in range(UNROLL):
                    st.load(sp, turn, s, tile_of(d["lru_w"], turn, s))

        @block.gpsimd
        def _(pool):
            lo_of_turns(pool, st, OUT, cut)
            for s in range(2):
                for e in range(2):
                    st.cut_lo(pool, OUT, s, e)
            for c in range(1, DC, 2):
                pool.wait_ge(scanned, c + 1)
                pool.wait_ge(gelus, c + 1)
                pool.tensor_tensor(b[:, c, :], xc[:, c, :], gate[:, c, :], ALU.mult).then_inc(states[1], 1)
                ycut.lo_chunk(pool, c)
            for s in range(2, UNROLL):
                for e in range(2):
                    st.cut_lo(pool, OUT, s, e)
            with pool.Fori(OUT + 1, END) as turn:
                for s in range(UNROLL):
                    for e in range(2):
                        st.cut_lo(pool, turn, s, e)

        @block.scalar
        def _(act):
            norm.square_half(act)
            st.cut_hi(act, 0, 0, first=True)
            norm.root(act)
            st.cut_hi(act, 0, 1, first=True)
            cut.hi(act, norm.scaled)
            act.wait_ge(lam_abs, 1)
            act.activation(e, z, ACT.Exp, scale=-1.0).then_inc(lam_exp, 1)
            with act.Fori(0, GATE) as turn:
                for s in range(UNROLL):
                    st.cut_hi(act, turn + (s + 2) // UNROLL, (s + 2) % UNROLL)
                    st.wait_product(act, turn, s)
                    act.copy(xp[:, bass.ds(turn * UNROLL + s, 1), CONV - 1:],
                             st.bank(s).unsqueeze(1)).then_inc(st.free[s % 2], 1)

            def gates(c):
                for k, (dst, bias) in enumerate(((r, half_ba), (i, half_bx))):
                    act.wait_ge(gated, 2 * c + k + 1)
                    act.activation(dst[:, c, :], mem.ps[:, 2 + (2 * c + k) % 4, 0:L], ACT.Tanh,
                                   bias=bias[:, c:c + 1], scale=0.5).then_inc(gate_out, 1)
                act.wait_ge(gate_out, 2 * c + 1)
                act.activation(a[:, c, :], r[:, c, :], ACT.Exp, bias=negc8[:, c:c + 1],
                               scale=negc8[:, c:c + 1]).then_inc(decays, 1)
                act.activation(r[:, c, :], r[:, c, :], ACT.Tanh, bias=c8[:, c:c + 1],
                               scale=c8[:, c:c + 1]).then_inc(decays, 1)

            act.wait_ge(ready, 4)
            for c in range(DC):
                n = DC + c
                st.cut_hi(act, (n + 2) // UNROLL, (n + 2) % UNROLL)
                st.wait_product(act, n // UNROLL, n % UNROLL)
                act.copy(gate[:, c, :], st.bank(n % 2)).then_inc(st.free[n % 2], 1)
                if c:
                    gates(c - 1)
            gates(DC - 1)
            for k in range(2):
                q = slice(k * DC // 2, (k + 1) * DC // 2)
                act.wait_ge(squared, (k + 1) * DC // 2)
                act.activation(b[:, q, :], b[:, q, :], ACT.Sqrt).then_inc(rooted, 1)
            act.wait_ge(st.free[0], GATE * 4 + 1)
            act.wait_ge(st.free[1], GATE * 4 + 1)
            for c in range(DC):
                act.activation(gate[:, c, :], gate[:, c, :], ACT.Gelu_apprx_tanh).then_inc(gelus, 1)
            ycut.hi(act, *states)
            with act.Fori(OUT, END - 1) as turn:
                for s in range(UNROLL):
                    st.cut_hi(act, turn + (s + 2) // UNROLL, (s + 2) % UNROLL)
            for s in range(2):
                st.cut_hi(act, END - 1, s + 2)

        @block.vector
        def _(dve):
            step = Steps(dve, dstep)
            lam = mem.vec[:, VEC["lam"]:VEC["lam"] + DC]
            norm.square(dve)
            dve.memset(xp[:, :, 0:CONV - 1], 0.0).then_inc(padded, 1)
            step.done(dve.tensor_scalar(nlam, lam, -1.0, None, ALU.mult))
            dve.tensor_tensor(z, lam, nlam, ALU.max).then_inc(lam_abs, 1)
            norm.scale(dve, xn)
            cut.lo(dve, 0)
            dve.wait_ge(lam_exp, 1)
            step.done(dve.tensor_scalar(z, e, 2.0, None, ALU.add))
            step.done(dve.reciprocal(z, z))
            step.done(dve.tensor_tensor(z, z, e, ALU.mult))
            step.done(dve.tensor_tensor(z2, z, z, ALU.mult))
            step.done(dve.tensor_scalar(poly, z2, 1.0 / 17, 1.0 / 15, ALU.mult, ALU.add))
            for k in (13, 11, 9, 7, 5, 3, 1):
                step.done(dve.tensor_tensor(poly, poly, z2, ALU.mult))
                step.done(dve.tensor_scalar(poly, poly, 1.0 / k, None, ALU.add))
            step.done(dve.tensor_tensor(poly, poly, z, ALU.mult))
            step.done(dve.tensor_scalar(nlam, nlam, 0.0, None, ALU.max))
            step.done(dve.scalar_tensor_tensor(poly, poly, 2.0, nlam, ALU.mult, ALU.add))
            dve.tensor_scalar(c8, poly, LRU_C / 2, None, ALU.mult).then_inc(ready, 1)
            dve.tensor_scalar(negc8, poly, -LRU_C / 2, None, ALU.mult).then_inc(ready, 1)
            for half, bias in ((half_ba, "b_a"), (half_bx, "b_x")):
                dve.tensor_scalar(half, mem.vec[:, VEC[bias]:VEC[bias] + DC], 0.5, None, ALU.mult).then_inc(ready, 1)
            dve.wait_ge(padded, 1)
            vec = mem.vec
            for c in range(DC):
                dve.wait_ge(st.free[c % 2], c // 2 + 2)
                for j in range(CONV):
                    w = vec[:, VEC[f"cw{j}"] + c:VEC[f"cw{j}"] + c + 1]
                    if j == 0:
                        step.done(dve.tensor_scalar(xc[:, c, :], xp[:, c, 0:L], w,
                                                    vec[:, VEC["conv_b"] + c:VEC["conv_b"] + c + 1], ALU.mult, ALU.add))
                        continue
                    ins = dve.scalar_tensor_tensor(xc[:, c, :], xp[:, c, j:j + L], w, xc[:, c, :], ALU.mult, ALU.add)
                    if j < CONV - 1:
                        step.done(ins)
                    else:
                        ins.then_inc(conved, 1)
            dve.wait_ge(conved, DC)
            for c in range(DC):
                dve.wait_ge(decays, 2 * (c + 1))
                step.done(dve.tensor_tensor(b[:, c, :], a[:, c, :], a[:, c, :], ALU.mult))
                dve.scalar_tensor_tensor(b[:, c, :], b[:, c, :], 1.0, r[:, c, :], ALU.add, ALU.mult).then_inc(squared, 1)
                step.add(dve.scalar_tensor_tensor(i[:, c, :], i[:, c, :], 1.0, xc[:, c, :], ALU.add, ALU.mult))
            for c in range(DC):
                dve.wait_ge(rooted, c // (DC // 2) + 1)
                step.done(dve.scalar_tensor_tensor(b[:, c, :], b[:, c, :], 0.5, i[:, c, :], ALU.mult, ALU.mult))
                dve.tensor_tensor_scan(xc[:, c, :], a[:, c, :], b[:, c, :], 0.0, ALU.mult, ALU.add).then_inc(scanned, 1)
                if c % 2 == 0:
                    dve.wait_ge(scanned, c + 1)
                    dve.wait_ge(gelus, c + 1)
                    dve.tensor_tensor(b[:, c, :], xc[:, c, :], gate[:, c, :], ALU.mult).then_inc(states[0], 1)
                elif c >= 3:
                    ycut.lo_chunk(dve, c - 3)
            ycut.lo_chunk(dve, DC - 2)
            with dve.Fori(OUT, END) as turn:
                for s in range(UNROLL):
                    st.wait_product(dve, turn, s)
                    hc = mem.h[:, bass.ds((turn - OUT) * UNROLL + s, 1), :]
                    dve.tensor_tensor(hc, hc, st.bank(s).unsqueeze(1), ALU.add).then_inc(st.free[s % 2], 1)

        @block.tensor
        def _(pe):
            st.open(pe)
            norm.add_up(pe)
            multiply_turns(pe, st, 0, GATE, cut)
            pe.wait_ge(w_in, 32)
            for c in range(DC):
                n = DC + c
                st.multiply(pe, n // UNROLL, n % UNROLL, st.bank(n))
                pe.wait_ge(conved, c + 1)
                for k, w in enumerate((wa, wx)):
                    m = 2 * c + k
                    if m >= 4:
                        pe.wait_ge(gate_out, m - 3)
                    pe.matmul(mem.ps[:, 2 + m % 4, 0:L], w[:, c, :], xc[:, c, :], start=True,
                              stop=True).then_inc(gated, 1)
            multiply_turns(pe, st, OUT, END, ycut)


def peer(nc, ctx, mem, d, layer):
    def sem(name):
        return ctx.sem(f"peer{layer}_{name}")

    T = L if layer == 0 else SEQ
    G, NG = T // GT, T // ST
    act_w = mem.big[:, 0:NK * T].rearrange("p (i t) -> p i t", t=T)
    h = mem.h[:, :, L - T:L]
    take = mem.take
    qt, at = take(HALF * T, (2, G, PH, GT))
    xn, at = take(at, (DC, T))
    SPREADS = 2 + PARTS
    spread, _ = take(HALF * T, (G * SPREADS * PH * TOPK // 2,))
    spread = spread.bitcast(BF16).rearrange("p (g w h k) -> p g w h k", w=SPREADS, h=PH, k=TOPK)
    scores, at = take(at, (G, 2 * NK))
    rstd, at = take(at, (1, L))
    keys, at = take(at, (2, NK))
    s1, at = take(at, (4, NK))
    s2, at = take(at, (4, NK))
    cand, at = take(at, (2, TOPK * TOPK))
    cand2, at = take(at, (2, TOPK * TOPK))
    hot, at = take(at, (4, TOPK, TOPK))
    top, at = take(at, (4, TOPK))
    topi, at = take(at, (4, TOPK))
    best, at = take(at, (2, TOPK))
    best_at, at = take(at, (2, TOPK))
    place, at = take(at, (4, TOPK))
    ij, at = take(at, (2, G, TOPK))
    gates, at = take(at, (G, TOPK))
    g_rest, at = take(at, (G, TOPK))
    g_part, _ = take(at, (PARTS, G, TOPK // 2))
    g_part = g_part.bitcast(BF16)
    den, at = take(at, (2, G))
    rstd = rstd[:, 0, :]
    topi, place, best_at = topi.bitcast(U32), place.bitcast(U32), best_at.bitcast(U32)
    iota = mem.con[:, CON["iota"]:CON["iota"] + P]
    head_mask = mem.con[:, CON["head"]:CON["head"] + PH]

    norm = Norm(nc, ctx, mem, f"peer{layer}_n", h, DC, VEC[f"ffn{layer}"], xn, rstd[:, 0:T], 2, T)
    cut = Cut(nc, ctx, mem, f"peer{layer}_x", xn, T)
    st = Stream(nc, ctx, mem, f"peer{layer}_s", T)
    keys_in, scored, scores_out, dstep, shifted, exped, spread_done, placed, chosen = (
        sem(n) for n in ("keys_in", "scored", "scores_out", "dve_steps", "shifted", "exped", "spread_done", "placed",
                         "chosen"))
    turns_taken = sem("turns_taken")
    hots_ready, scattered, gated = sem("hots_ready"), sem("scattered"), sem("gated")
    w_hi_cut, w_lo_cut = sem("w_hi_cut"), sem("w_lo_cut")

    TQ, TH = 2 * PH // UNROLL, HALF // UNROLL
    U0, U1, V0, V1, END = TQ, TQ + TH, TQ + 2 * TH, TQ + 3 * TH, TQ + 4 * TH
    MID, SPREAD = U0 + TH * 3 // 4, U1 - 2

    GBANK = 7
    if T <= 256:
        pieces = [[[(c // 2, 256 * (c % 2), 0, T)] for c in range(DC)]] * 2
    else:
        side = 512 - T
        pieces = [[[(c, 0, 0, T)] for c in range(GBANK)] + [last]
                  for last in ([(0, T, 0, side), (1, T, side, T - side)], [(GBANK, 0, 0, T)])]

    def products(pe, half, m):
        pe.wait_ge(hots_ready, half * NG + m + 1)
        for t in range(ST):
            o = mem.ps[:, GBANK, t * HALF:(t + 1) * HALF]
            for k in range(PARTS):
                mm = pe.matmul(o, mem.j_hot[:, :, t], mem.i_gate[:, k, :, t], start=(k == 0), stop=(k == PARTS - 1))
        mm.then_inc(scattered, 1)

    def hots(dve, step, half, m):
        tok = bass.ds(m * ST, ST) if not isinstance(m, int) else slice(m * ST, m * ST + ST)
        wide, wide_i = [P, P, ST], [P, HALF, ST]
        dve.wait_ge(scattered, half * NG + m)
        step.add(dve.tensor_tensor(mem.i_hot[:, :, :], mem.iota[:, half * HALF:(half + 1) * HALF, :],
                                   mem.idx[:, 0, tok].unsqueeze(1).to_broadcast(wide_i), ALU.is_equal))
        step.add(dve.tensor_tensor(mem.j_hot[:, :, :], mem.iota[:, :, :],
                                   mem.idx[:, 1, tok].unsqueeze(1).to_broadcast(wide), ALU.is_equal))
        step.wait(2)
        for k in range(PARTS):
            ins = dve.tensor_tensor(mem.i_gate[:, k], mem.i_hot[:, :, :],
                                    mem.g[:, k, tok].unsqueeze(1).to_broadcast(wide_i), ALU.mult)
            if k < PARTS - 1:
                step.add(ins)
            else:
                ins.then_inc(hots_ready, 1)

    HOT_STEPS = 2 + PARTS - 1
    GROUPS_AFTER = [1, 3]
    LAST_AFTER = GROUPS_AFTER if NG == 2 * TH else list(range(UNROLL))
    assert 2 * (TH - 1) + len(LAST_AFTER) == NG

    def gate_act(dve, half, m):
        tok = bass.ds(m * ST, ST) if not isinstance(m, int) else slice(m * ST, m * ST + ST)
        dve.wait_ge(scattered, half * NG + m + 1)
        w = act_w[:, half * HALF:(half + 1) * HALF, tok]
        g = mem.ps[:, GBANK, :].rearrange("p (t i) -> p i t", i=HALF)
        dve.tensor_tensor(w, w, g, ALU.mult).then_inc(gated, 1)

    def cut_w_hi(act, n, r):
        i = bass.ds(n, 1) if not isinstance(n, int) else slice(n, n + 1)
        act.copy(mem.xhi[:, r:r + 1, 0:T], act_w[:, i, :]).then_inc(w_hi_cut, 1)

    def cut_w_lo(dve, n, r):
        i = bass.ds(n, 1) if not isinstance(n, int) else slice(n, n + 1)
        dve.wait_ge(w_hi_cut, n + 1)
        dve.tensor_tensor(mem.xlo[:, r:r + 1, 0:T], act_w[:, i, :], mem.xhi[:, r:r + 1, 0:T].bitcast(F32),
                          ALU.subtract).then_inc(w_lo_cut, 1)

    def apply_v(pe, turn, s, half, fresh=()):
        pe.wait_ge(w_lo_cut, (turn - V0) * UNROLL + (s + 1))
        fresh = set(fresh)
        for e in range(2):
            k = (2 * s + e) % SLOTS
            st.wait_hi(pe, turn, s, e)
            for w, x in ((mem.whi, mem.xhi), (mem.whi, mem.xlo), (mem.wlo, mem.xhi)):
                if w is mem.wlo:
                    st.wait_lo(pe, turn, s, e)
                for c in range(DC // 2):
                    for bank, col, tok, n in pieces[half][e * DC // 2 + c]:
                        mm = pe.matmul(mem.ps[:, bank, col:col + n], w[:, k, c * P:(c + 1) * P],
                                       x[:, s, tok:tok + n], start=bank in fresh, stop=False,
                                       skip_group_check=True)
                        fresh.discard(bank)
            mm.then_inc(st.done, 1)

    with nc.Block() as block:
        @block.sync
        def _(sp):
            for s in range(UNROLL):
                st.load(sp, 0, s, d["query"][layer, s], first=True)
            sp.dma_start(keys, d["keys"][layer]).then_inc(keys_in, 16)
            with sp.Fori(1, TQ) as turn:
                for s in range(UNROLL):
                    st.load(sp, turn, s, tile_of(d["query"][layer], turn, s))
            with sp.Fori(U0, V0) as turn:
                for s in range(UNROLL):
                    st.load(sp, turn, s, tile_of(d["u"][layer], turn - U0, s))
            with sp.Fori(V0, END) as turn:
                for s in range(UNROLL):
                    st.load(sp, turn, s, tile_of(d["v"][layer], turn - V0, s))

        @block.gpsimd
        def _(pool):
            lo_of_turns(pool, st, U1, cut)
            with pool.Fori(U1, V1) as turn:
                for q in (0, 2, 3, 4, 6, 7):
                    st.cut_lo(pool, turn, q // 2, q % 2)
            with pool.Fori(V1, END) as turn:
                for q in (2, 3, 6, 7):
                    st.cut_lo(pool, turn, q // 2, q % 2)

        @block.scalar
        def _(act):
            norm.square_half(act)
            st.cut_hi(act, 0, 0, first=True)
            norm.root(act)
            st.cut_hi(act, 0, 1, first=True)
            cut.hi(act, norm.scaled)
            with act.Fori(0, TQ) as turn:
                for s in range(UNROLL):
                    st.wait_product(act, turn, s)
                    st.cut_hi(act, turn + (s + 2) // UNROLL, (s + 2) % UNROLL)
                    act.copy(qt[:, s % 2, :, bass.ds(turn * 2 + s // 2, 1), :].rearrange("p g a t -> p g (a t)"),
                             st.bank(s).rearrange("p (g t) -> p g t", t=GT)).then_inc(st.free[s % 2], 1)

            def load_gelu(n):
                k = 2 * layer + n
                act.activation(mem.unread[:, k:k + 1], mem.con[:, 0:1], ACT.Gelu_apprx_tanh)

            def take_act(turn):
                for s in range(UNROLL):
                    st.wait_product(act, turn, s)
                    st.cut_hi(act, turn + (s + 2) // UNROLL, (s + 2) % UNROLL)
                    act.activation(act_w[:, bass.ds((turn - U0) * UNROLL + s, 1), :], st.bank(s).unsqueeze(1),
                                   ACT.Gelu_apprx_tanh).then_inc(st.free[s % 2], 1)

            load_gelu(0)
            with act.Fori(U0, MID) as turn:
                take_act(turn)
            act.wait_ge(shifted, 1)
            act.activation(gates, gates, ACT.Exp).then_inc(exped, 1)
            load_gelu(1)
            with act.Fori(MID, U1) as turn:
                take_act(turn)
            act.wait_ge(chosen, SPREADS)
            with act.Fori(U1, V0) as turn:
                take_act(turn)
            act.wait_ge(st.done, V0 * HALVES)
            act.wait_ge(gated, NG)
            for s in range(UNROLL):
                cut_w_hi(act, s, s)

            def next_v(turn, hi=True, w=True):
                for s in range(UNROLL):
                    if hi or s < 2:
                        st.cut_hi(act, turn + (s + 2) // UNROLL, (s + 2) % UNROLL)
                    if w:
                        st.wait_product(act, turn, s)
                        cut_w_hi(act, (turn - V0) * UNROLL + (s + 4), s)

            with act.Fori(V0, V1 - 1) as turn:
                next_v(turn)
            next_v(V1 - 1, w=False)
            act.wait_ge(st.done, V1 * HALVES)
            act.wait_ge(gated, 2 * NG)
            for s in range(UNROLL):
                cut_w_hi(act, HALF + s, s)
            with act.Fori(V1, END - 1) as turn:
                next_v(turn)
            next_v(END - 1, hi=False, w=False)

        @block.vector
        def _(dve):
            step = Steps(dve, dstep)
            norm.square(dve)
            norm.scale(dve, xn)
            cut.lo(dve, 0)
            with dve.Fori(0, G // 2) as pair:
                for k in range(2):
                    dve.wait_ge(scored, pair * 2 + (k + 1))
                    dve.tensor_copy(scores[:, bass.ds(pair * 2 + k, 1), :],
                                    mem.ps[:, 2 + k, 0:2 * NK].unsqueeze(1)).then_inc(scores_out, 1)
            if G % 2:
                dve.wait_ge(scored, G)
                dve.tensor_copy(scores[:, G - 1, :], mem.ps[:, 2, 0:2 * NK]).then_inc(scores_out, 1)
            dve.wait_ge(scores_out, G)

            def top16(rows):
                for k, op in enumerate((lambda v, spare, f, at: dve.max(f[:, 0:8], v),
                                        lambda v, spare, f, at: dve.match_replace(spare, f[:, 0:8], v, NEG),
                                        lambda v, spare, f, at: dve.max(f[:, 8:16], spare),
                                        lambda v, spare, f, at: dve.max_index(at[:, 0:8], f[:, 0:8], v),
                                        lambda v, spare, f, at: dve.max_index(at[:, 8:16], f[:, 8:16], spare))):
                    for row in rows:
                        step.wait(len(rows) if k else 1)
                        dve.sem_inc(turns_taken, 1)
                        step.add(op(*row))

            def find(first, w):
                grp = bass.ds(first, w) if not isinstance(first, int) else slice(first, first + w)
                step.done(dve.tensor_copy(s1[:, 0:2 * w, :].rearrange("p (a g) n -> p a g n", g=w),
                                          scores[:, grp, :].rearrange("p g (a n) -> p a g n", n=NK)))
                top16([(s1[:, k, :], s2[:, k, :], top[:, k, :], topi[:, k, :]) for k in range(2 * w)])
                step.add(dve.tensor_tensor(cand[:, 0:w, :].rearrange("p g (a b) -> p g a b", b=TOPK),
                                           top[:, 0:w, :].unsqueeze(3).to_broadcast([P, w, TOPK, TOPK]),
                                           top[:, w:2 * w, :].unsqueeze(2).to_broadcast([P, w, TOPK, TOPK]), ALU.add))
                top16([(cand[:, k, :], cand2[:, k, :], best[:, k, :], best_at[:, k, :]) for k in range(w)])
                step.add(dve.tensor_copy(gates[:, grp, :], best[:, 0:w, :]))
                step.wait(1)
                step.add(dve.tensor_scalar(place[:, 0:w, :], best_at[:, 0:w, :], 4, None, ALU.logical_shift_right))
                step.done(dve.tensor_scalar(place[:, w:2 * w, :], best_at[:, 0:w, :], TOPK - 1, None,
                                            ALU.bitwise_and))
                cube = [P, 2 * w, TOPK, TOPK]
                step.done(dve.tensor_tensor(hot[:, 0:2 * w], iota[:, 0:TOPK].unsqueeze(1).unsqueeze(1).to_broadcast(cube),
                                            place[:, 0:2 * w, :].unsqueeze(3).to_broadcast(cube), ALU.is_equal))
                step.done(dve.tensor_tensor(hot[:, 0:2 * w], hot[:, 0:2 * w],
                                            topi[:, 0:2 * w, :].unsqueeze(2).to_broadcast(cube), ALU.mult))
                step.add(dve.tensor_reduce(ij[:, :, grp, :].rearrange("p a g k -> p a (g k)"),
                                           hot[:, 0:2 * w].rearrange("p (a g) k b -> p a (g k) b", g=w), AX.X,
                                           ALU.add))

            per_pair = 1 + 5 * 4 + 1 + 5 * 2 + 6
            with dve.Fori(0, G // 2) as pair:
                step.enter(pair, per_pair)
                find(pair * 2, 2)
                step.leave(G // 2, per_pair)
            if G % 2:
                find(G - 1, 1)
            step.wait(1)
            wide = [P, G, TOPK]
            step.done(dve.tensor_copy(den[:, 0, :], gates[:, :, 0]))
            dve.tensor_tensor(gates, gates, den[:, 0, :].unsqueeze(2).to_broadcast(wide),
                              ALU.subtract).then_inc(shifted, 1)
            by_head = [P, G, PH, TOPK]
            mask = head_mask.unsqueeze(1).unsqueeze(3).to_broadcast(by_head)
            for w in range(2):
                dve.tensor_tensor(spread[:, :, w, :, :], ij[:, w, :, :].unsqueeze(2).to_broadcast(by_head), mask,
                                  ALU.mult).then_inc(placed, 1)
            dve.wait_ge(exped, 1)
            step.done(dve.tensor_reduce(den[:, 0, :], gates, AX.X, ALU.add))
            step.done(dve.reciprocal(den[:, 1, :], den[:, 0, :]))
            step.done(dve.tensor_tensor(gates, gates, den[:, 1, :].unsqueeze(2).to_broadcast(wide), ALU.mult))
            for k in range(PARTS):
                step.done(dve.tensor_copy(g_part[:, k], gates if k == 0 else g_rest))
                dve.tensor_tensor(spread[:, :, 2 + k, :, :], g_part[:, k].unsqueeze(2).to_broadcast(by_head), mask,
                                  ALU.mult).then_inc(placed, 1)
                if k < PARTS - 1:
                    step.done(dve.tensor_tensor(g_rest, gates if k == 0 else g_rest, g_part[:, k], ALU.subtract))
            dve.wait_ge(spread_done, 1)
            for w in range(SPREADS):
                dst = mem.idx[:, w, 0:T] if w < 2 else mem.g[:, w - 2, 0:T]
                dve.tensor_copy(dst, mem.ps[:, 2 + w, 0:T]).then_inc(chosen, 1)
            dve.wait_ge(chosen, SPREADS)

            def scatter_turn(turn, half, m, after, last):
                for s in range(UNROLL):
                    if s % 2 == 0:
                        st.cut_lo(dve, turn + (s + 2) // UNROLL, (s + 2) % UNROLL, 1)
                    if half == 1 and not last:
                        cut_w_lo(dve, (turn - V0) * UNROLL + (s + 4), s)
                    if s in after:
                        k = after.index(s)
                        gate_act(dve, half, m + k)
                        if not last or m + k + 1 < NG:
                            hots(dve, step, half, m + k + 1)

            def scatter_half(half, base, last_turn):
                hots(dve, step, half, 0)
                for r in range(2):
                    dve.wait_ge(st.free[r], (U1 if half == 0 else V0) * 2 + 1)
                with dve.Fori(base, last_turn) as turn:
                    step.enter(turn - base, 2 * HOT_STEPS)
                    scatter_turn(turn, half, (turn - base) * 2, GROUPS_AFTER, False)
                    step.leave(last_turn - base, 2 * HOT_STEPS)
                scatter_turn(last_turn, half, 2 * (TH - 1), LAST_AFTER, True)

            st.cut_lo(dve, U1, 0, 1)
            scatter_half(0, U1, V0 - 1)
            for s in range(UNROLL):
                cut_w_lo(dve, s, s)
            scatter_half(1, V0, V1 - 1)
            for s in range(UNROLL):
                cut_w_lo(dve, HALF + s, s)

            def lo_turn(turn, last):
                for s in range(UNROLL):
                    if s % 2 == 0 and not (last and s == 2):
                        for e in range(2):
                            st.cut_lo(dve, turn + (s + 2) // UNROLL, (s + 2) % UNROLL, e)
                    if not last:
                        cut_w_lo(dve, (turn - V0) * UNROLL + (s + 4), s)

            st.cut_lo(dve, V1, 0, 0)
            with dve.Fori(V1, END - 1) as turn:
                lo_turn(turn, False)
            lo_turn(END - 1, True)
            dve.wait_ge(st.done, END * HALVES)
            for c in range(DC):
                parts = pieces[0][c] + [p for p in pieces[1][c] if p not in pieces[0][c]]
                for k, (bank, col, tok, n) in enumerate(parts):
                    step.add(dve.tensor_tensor(h[:, c, tok:tok + n], h[:, c, tok:tok + n],
                                               mem.ps[:, bank, col:col + n], ALU.add))
                    if len(parts) > 1:
                        step.wait(1)

        @block.tensor
        def _(pe):
            st.open(pe)
            norm.add_up(pe)
            multiply_turns(pe, st, 0, TQ, cut)
            pe.wait_ge(keys_in, 16)
            for r in range(2):
                pe.wait_ge(st.free[r], TQ * 2 + 1)

            for g in range(G):
                if g >= 2:
                    pe.wait_ge(scores_out, g - 1)
                for half in range(2):
                    mm = pe.matmul(mem.ps[:, 2 + g % 2, half * NK:(half + 1) * NK],
                                   qt[:, half, g, :, :].rearrange("p h t -> p (h t)"), keys[:, half, :],
                                   start=True, stop=True)
                mm.then_inc(scored, 1)
            def u_tiles(first, last):
                with pe.Fori(first, last) as turn:
                    for s in range(UNROLL):
                        st.multiply(pe, turn, s, st.bank(s))

            u_tiles(U0, SPREAD)
            pe.wait_ge(placed, SPREADS)
            pe.wait_ge(scores_out, G)
            for g in range(G):
                for w in range(SPREADS):
                    mm = pe.matmul(mem.ps[:, 2 + w, g * GT:(g + 1) * GT],
                                   spread[:, g, w, :, :].rearrange("p h k -> p (h k)"), mem.token[:, :],
                                   start=True, stop=True)
            mm.then_inc(spread_done, 1)
            u_tiles(SPREAD, U1)

            def u_turn(turn, m, after):
                for s in range(UNROLL):
                    st.multiply(pe, turn, s, st.bank(s))
                    if s in after:
                        products(pe, 0, m + after.index(s))

            with pe.Fori(U1, V0 - 1) as turn:
                u_turn(turn, (turn - U1) * 2, GROUPS_AFTER)
            u_turn(V0 - 1, 2 * (TH - 1), LAST_AFTER)
            for r in range(2):
                pe.wait_ge(st.free[r], V0 * 2 + 1)

            def v_turn(turn, half, m=0, after=(), fresh=()):
                for s in range(UNROLL):
                    apply_v(pe, turn, s, half, fresh if s == 0 else ())
                    if s in after:
                        products(pe, 1, m + after.index(s))

            v_turn(V0, 0, 0, GROUPS_AFTER, fresh=range(GBANK))
            with pe.Fori(V0 + 1, V1 - 1) as turn:
                v_turn(turn, 0, (turn - V0) * 2, GROUPS_AFTER)
            v_turn(V1 - 1, 0, 2 * (TH - 1), LAST_AFTER)
            v_turn(V1, 1, fresh=[GBANK])
            with pe.Fori(V1 + 1, END) as turn:
                v_turn(turn, 1)


def finish(nc, ctx, mem, d):
    xn, at = mem.take(0, (DC, SEQ))
    rstd, at = mem.take(at, (1, SEQ))
    norm = Norm(nc, ctx, mem, "final", mem.h[:, :, META:L], DC, VEC["final"], xn, rstd[:, 0, :], 2, SEQ)
    stored = ctx.sem("final_stored")
    with nc.Block() as block:
        @block.vector
        def _(dve):
            norm.square(dve)
            norm.scale(dve, xn)

        @block.tensor
        def _(pe):
            norm.add_up(pe)

        @block.scalar
        def _(act):
            norm.square_half(act)
            norm.root(act)

        @block.sync
        def _(sp):
            for c in range(DC):
                sp.wait_ge(norm.scaled, c + 1)
                sp.dma_start(d["out"][:, c, :], xn[:, c, :]).then_inc(stored, 16)
            sp.wait_ge(stored, 16 * DC)


def trunk(nc, d):
    with ExitStack() as ctx:
        mem = Memory(nc, ctx)
        with Stage(nc) as own:
            mla(nc, own, mem, d)
        with Stage(nc) as own:
            peer(nc, own, mem, d, 0)
        with Stage(nc) as own:
            rglru(nc, own, mem, d)
        with Stage(nc) as own:
            peer(nc, own, mem, d, 1)
        with Stage(nc) as own:
            finish(nc, own, mem, d)


def column_tiles(w):
    *lead, rows, cols = w.shape
    n = len(lead)
    w = w.reshape(*lead, rows // P, P, cols // P, P)
    w = w.transpose(*range(n), n + 2, n + 1, n, n + 3)
    return np.ascontiguousarray(w).reshape(*lead, cols // P, P, rows)


def lay_out(inputs):
    a = {k: np.asarray(v) for k, v in inputs.items()}
    chunked = lambda t: np.ascontiguousarray(t.T.reshape(DC, P, -1).transpose(1, 0, 2))
    columns = lambda v: v.reshape(-1, P).T
    half = ROPE // 2
    swap = np.r_[half:ROPE, 0:half]
    rows = lambda w: np.ascontiguousarray(w.reshape(-1, P, w.shape[-1]).transpose(1, 0, 2))

    w_in = a["mla_w_in"][0]
    lat, kr = w_in[:, :QLORA + KVLORA], w_in[:, QLORA + KVLORA:]
    q_up = a["mla_w_q_up"][0].reshape(QLORA, HEADS, NOPE + ROPE)
    q_rope = q_up[:, :, NOPE:]
    q_up = np.concatenate([x.reshape(QLORA, -1) for x in (q_up[:, :, :NOPE], q_rope, q_rope[:, :, swap])], axis=1)
    kv_up = a["mla_w_kv_up"][0].reshape(KVLORA, HEADS, NOPE + VH)
    kv_up = np.concatenate([x.reshape(KVLORA, -1) for x in (kv_up[:, :, :NOPE], kv_up[:, :, NOPE:])], axis=1)
    vec = [a["mixer_norm"][0], a["mixer_norm"][1], a["ffn_norm"][0], a["ffn_norm"][1], a["final_norm"],
           a["lru_b_gate_a"][0], a["lru_b_gate_x"][0], a["lru_conv_b"][0], *a["lru_conv_w"][0], a["lru_lambda"][0],
           a["mla_q_norm"][0], a["mla_kv_norm"][0]]
    con, idm = constants()
    layers = a["peer_u"].shape[0]
    lru_in = a["lru_w_in"][0]
    u = a["peer_u"].reshape(layers, NK, NK, DC, P).transpose(0, 1, 4, 3, 2)
    return {
        "x": chunked(a["x"][0]),
        "meta": chunked(a["meta_tokens"]),
        "pos": np.ascontiguousarray(a["positions"]),
        "con": con,
        "idm": idm,
        "vec": np.ascontiguousarray(np.concatenate([columns(v) for v in vec], axis=1)),
        "mla_down": column_tiles(np.concatenate([lat, kr, kr, kr[:, swap], kr[:, swap]], axis=1)),
        "mla_q_up": rows(q_up),
        "mla_kv_up": rows(kv_up),
        "mla_out": column_tiles(a["mla_w_out"][0]),
        "query": column_tiles(a["peer_w_query"]),
        "keys": np.ascontiguousarray(a["peer_sub_keys"].transpose(0, 3, 1, 2)),
        "u": np.ascontiguousarray(u).reshape(layers, NK, P, D),
        "v": a["peer_v"].reshape(layers, NK, P, D),
        "lru_w": np.concatenate([column_tiles(w) for w in (lru_in[:, D:], lru_in[:, :D], a["lru_w_out"][0])]),
        "lru_wa": np.ascontiguousarray(a["lru_w_gate_a"][0].transpose(1, 0, 2)),
        "lru_wx": np.ascontiguousarray(a["lru_w_gate_x"][0].transpose(1, 0, 2)),
    }


def kernel(**inputs):
    import concourse.bacc as bacc
    from concourse.bass_utils import run_bass_kernel_spmd

    nc = bacc.Bacc("TRN2", target_bir_lowering=False, num_devices=1)
    arrays, d = {}, {}
    for name, array in lay_out(inputs).items():
        arrays[f"in_{name}"] = array
        d[name] = nc.dram_tensor(f"in_{name}", array.shape, mybir.dt.from_np(array.dtype), kind="ExternalInput").ap()
    d["out"] = nc.dram_tensor("out_0", (P, DC, SEQ), F32, kind="ExternalOutput").ap()
    trunk(nc, d)
    result = run_bass_kernel_spmd(nc, [arrays], core_ids=[0])
    out = result.results[0]["out_0"]
    return np.ascontiguousarray(out.transpose(2, 1, 0)).reshape(1, SEQ, D)
```

```python
from contextlib import ExitStack

import numpy as np

import concourse.bass as bass
from concourse import mybir

P = 128
D = 1024
DC = D // P
SEQ = 256
META = 16
L = SEQ + META
EPS = 1e-6

HEADS, NOPE, ROPE, VH = 8, 128, 64, 128
QLORA, KVLORA = 384, 256
QC, KVC = QLORA // P, KVLORA // P
SCALE = float(1.0 / np.sqrt(NOPE + ROPE))
Q0 = (0, 128, L - P)
NKEYS_SEEN = (128, 256, L)

PH, NK, TOPK, QH = 8, 128, 16, 128
GT = 16
HALF = NK // 2
ST = 8
PARTS = 3
UNROLL = 4
HW = D // 2
HALVES = 2 * UNROLL
SLOTS = 4

SUM_BANK, FINAL_SUM_BANK = 2, 4

CONV = 4
LRU_C = 8.0

BIG = NK * L
NEG = -3.0e38

ALU = mybir.AluOpType
ACT = mybir.ActivationFunctionType
AX = mybir.AxisListType
F32 = mybir.dt.float32
F32R = mybir.dt.float32r
BF16 = mybir.dt.bfloat16
U32 = mybir.dt.uint32
I32 = mybir.dt.int32

VEC = {}
for _i, _n in enumerate(["mix0", "mix1", "ffn0", "ffn1", "final", "b_a", "b_x", "conv_b", "cw0", "cw1", "cw2",
                         "cw3", "lam"]):
    VEC[_n] = _i * DC
VEC["q_norm"] = 13 * DC
VEC["kv_norm"] = VEC["q_norm"] + QC
NVEC = VEC["kv_norm"] + KVC

CON = {"iota": 0, "head": P, "token": P + PH, "freq": P + PH + GT, "sign": P + PH + GT + 1,
       "eps": P + PH + GT + 2}
NCON = P + PH + GT + 3


def constants():
    p = np.arange(P)
    con = np.zeros((P, NCON), np.float32)
    con[:, :P] = np.arange(P)
    con[:, CON["head"]:CON["head"] + PH] = (p[:, None] // GT) == np.arange(PH)
    con[:, CON["token"]:CON["token"] + GT] = (p[:, None] % GT) == np.arange(GT)
    half = ROPE // 2
    freqs = np.float32(10000.0) ** (-np.arange(half, dtype=np.float32) / np.float32(half))
    con[:, CON["freq"]] = freqs[p % half]
    con[:, CON["eps"]] = EPS
    con[:, CON["sign"]] = np.where(p % ROPE < half, -1.0, 1.0)
    x = np.arange(L) - (L - P)
    tri = np.where(x[None, :] > p[:, None], -1e30, 0.0)
    return con, np.concatenate([np.eye(P), tri], axis=1).astype(np.float32)


class Steps:

    def __init__(self, eng, sem):
        self.eng, self.sem, self.n = eng, sem, 0

    def done(self, ins):
        ins.then_inc(self.sem, 1)
        self.n = self.n + 1
        self.eng.wait_ge(self.sem, self.n)

    def add(self, ins):
        ins.then_inc(self.sem, 1)
        self.n = self.n + 1

    def wait(self, back):
        self.eng.wait_ge(self.sem, self.n - (back - 1))

    def enter(self, turn, per_turn):
        self.base = self.n
        self.n = turn * per_turn + self.base

    def leave(self, turns, per_turn):
        self.n = self.base + turns * per_turn


class Stage:

    def __init__(self, nc):
        self.nc, self.sems = nc, []

    def __enter__(self):
        return self

    def sem(self, name):
        self.sems.append(self.nc.alloc_semaphore(name))
        return self.sems[-1]

    def __exit__(self, kind, *_):
        if kind is None:
            self.nc.clear_and_free_semaphores(self.sems)
            self.nc.all_engine_barrier()


class Memory:

    def __init__(self, nc, ctx):
        def sb(name, shape, dt=F32):
            return ctx.enter_context(nc.sbuf_tensor(name, shape, dt))

        self.big = sb("big", [P, BIG])
        self.h = sb("h", [P, DC, L])
        self.xhi = sb("xhi", [P, DC, L], F32R)
        self.xlo = sb("xlo", [P, DC, L], F32R)
        self.raw = sb("raw", [P, UNROLL, D])
        self.whi = sb("whi", [P, SLOTS, HW], F32R)
        self.wlo = sb("wlo", [P, SLOTS, HW], F32R)
        self.j_hot = sb("j_hot", [P, P, ST], BF16)
        self.i_hot = sb("i_hot", [P, HALF, ST], BF16)
        self.i_gate = sb("i_gate", [P, PARTS, HALF, ST], BF16)
        self.iota = sb("iota", [P, P, ST], BF16)
        self.idx = sb("idx", [P, 2, L], BF16)
        self.g = sb("g", [P, PARTS, L], BF16)
        self.con = sb("con", [P, NCON])
        self.vec = sb("vec", [P, NVEC])
        self.token = sb("token", [P, GT], BF16)
        self.ones = sb("ones", [P, P])
        self.unread = sb("unread", [P, 8])
        self.ps = ctx.enter_context(nc.psum_tensor("ps", [P, 8, 512], F32))

    def take(self, at, shape):
        n = int(np.prod(shape))
        assert at + n <= BIG, (at, shape)
        v = self.big[:, at:at + n]
        if len(shape) == 2:
            v = v.rearrange("p (a b) -> p a b", b=shape[1])
        if len(shape) == 3:
            v = v.rearrange("p (a b c) -> p a b c", b=shape[1], c=shape[2])
        if len(shape) == 4:
            v = v.rearrange("p (a b c d) -> p a b c d", b=shape[1], c=shape[2], d=shape[3])
        return v, at + n


class Stream:

    def __init__(self, nc, ctx, mem, name, tokens):
        def sem(what):
            return ctx.sem(f"{name}_{what}")

        self.mem, self.T = mem, tokens
        self.landed = [sem(f"landed{s}") for s in range(UNROLL)]
        self.hi_ready = sem("hi_ready")
        self.lo_ready = [sem(f"lo_ready{k}") for k in range(SLOTS)]
        self.done = sem("done")
        self.free = [sem(f"free{r}") for r in range(2)]

    def load(self, sp, turn, s, src, first=False):
        if not first:
            for e in range(2):
                sp.wait_ge(self.lo_ready[(2 * s + e) % SLOTS], turn * 2 + (s // 2 - 1))
        sp.dma_start(self.mem.raw[:, s, :], src).then_inc(self.landed[s], 16)

    def load_ahead(self, sp, turn, tiles):
        for s in range(UNROLL):
            self.load(sp, turn, s, tiles[s])
        for s in range(UNROLL):
            sp.wait_ge(self.landed[s], (turn + 1) * 16)

    def loaded_before(self, sp):
        for landed in self.landed:
            sp.sem_inc(landed, 16)

    def cut_hi(self, act, turn, s, first=False):
        for e in range(2):
            self.cut_hi_half(act, turn, s, e, first)

    def cut_hi_half(self, act, turn, s, e, first=False):
        q = 2 * s + e
        if e == 0:
            act.wait_ge(self.landed[s], turn * 16 + 16)
        if not first:
            act.wait_ge(self.done, turn * HALVES + (q + 1 - SLOTS))
        act.copy(self.mem.whi[:, q % SLOTS, :], self.mem.raw[:, s, e * HW:(e + 1) * HW]).then_inc(self.hi_ready, 1)

    def cut_lo(self, eng, turn, s, e):
        q = 2 * s + e
        eng.wait_ge(self.hi_ready, turn * HALVES + (q + 1))
        eng.tensor_tensor(self.mem.wlo[:, q % SLOTS, :], self.mem.raw[:, s, e * HW:(e + 1) * HW],
                          self.mem.whi[:, q % SLOTS, :].bitcast(F32),
                          ALU.subtract).then_inc(self.lo_ready[q % SLOTS], 1)

    def open(self, pe):
        for free in self.free:
            pe.sem_inc(free, 1)

    def wait_hi(self, pe, turn, s, e):
        pe.wait_ge(self.hi_ready, turn * HALVES + (2 * s + e + 1))

    def wait_lo(self, pe, turn, s, e):
        q = 2 * s + e
        pe.wait_ge(self.lo_ready[q % SLOTS], turn * 2 + (q // SLOTS + 1))

    def multiply(self, pe, turn, s, out, cut=None):
        m = self.mem
        pe.wait_ge(self.free[s % 2], turn * 2 + (s // 2 + 1))
        for e in range(2):
            k = (2 * s + e) % SLOTS
            self.wait_hi(pe, turn, s, e)
            for c in range(DC // 2):
                w, x = m.whi[:, k, c * P:(c + 1) * P], e * DC // 2 + c
                if cut:
                    cut.ready(pe, x)
                pe.matmul(out, w, m.xhi[:, x, 0:self.T], start=(x == 0), stop=False)
                pe.matmul(out, w, m.xlo[:, x, 0:self.T], start=False, stop=False)
            self.wait_lo(pe, turn, s, e)
            for c in range(DC // 2):
                x = e * DC // 2 + c
                mm = pe.matmul(out, m.wlo[:, k, c * P:(c + 1) * P], m.xhi[:, x, 0:self.T], start=False,
                               stop=(x == DC - 1))
            mm.then_inc(self.done, 1)

    def wait_product(self, eng, turn, s):
        eng.wait_ge(self.done, turn * HALVES + 2 * (s + 1))

    def bank(self, s):
        return self.mem.ps[:, s % 2, 0:self.T]


class Norm:

    def __init__(self, nc, ctx, mem, name, src, chunks, gain, squares, rstd, bank, tokens, given=False):
        def sem(what):
            return ctx.sem(f"{name}_{what}")

        self.mem, self.src, self.C, self.gain = mem, src, chunks, gain
        self.squares, self.rstd, self.T = squares, rstd, tokens
        self.sum, self.given = mem.ps[:, bank, 0:tokens], given
        self.rows = chunks // 2 if chunks == DC else chunks
        self.squared, self.added, self.summed = sem("squared"), sem("added"), sem("summed")
        self.rooted, self.scaled = sem("rooted"), sem("scaled")

    def square_half(self, act):
        act.activation(self.squares[:, self.rows:, :], self.src[:, self.rows:, :], ACT.Square).then_inc(self.squared, 1)

    def square(self, dve):
        first, r = self.squares[:, 0:self.rows, :], self.rows
        ins = dve.tensor_tensor(first, self.src[:, 0:r, :], self.src[:, 0:r, :], ALU.mult)
        if r < self.C:
            ins.then_inc(self.squared, 1)
            dve.wait_ge(self.squared, 2)
            ins = dve.tensor_tensor(first, first, self.squares[:, r:, :], ALU.add)
        ins.then_inc(self.added, 1)

    def add_up(self, pe):
        pe.wait_ge(self.added, 1)
        for c in range(self.rows):
            mm = pe.matmul(self.sum, self.mem.ones[:, :], self.squares[:, c, :], start=(c == 0),
                           stop=(c == self.rows - 1))
        mm.then_inc(self.summed, 1)

    def root(self, act):
        if not self.given:
            act.wait_ge(self.summed, 1)
        act.activation(self.rstd, self.sum, ACT.Ln, bias=self.mem.con[:, CON["eps"]:CON["eps"] + 1],
                       scale=1.0 / (self.C * P)).then_inc(self.rooted, 1)
        act.wait_ge(self.rooted, 1)
        act.activation(self.rstd, self.rstd, ACT.Exp, scale=-0.5).then_inc(self.rooted, 1)

    def wait_root(self, dve):
        dve.wait_ge(self.rooted, 2)

    def scale_chunk(self, dve, out, c):
        dve.scalar_tensor_tensor(out[:, c, :], self.src[:, c, :], self.mem.vec[:, self.gain + c:self.gain + c + 1],
                                 self.rstd, ALU.mult, ALU.mult).then_inc(self.scaled, 1)

    def scale(self, dve, out):
        self.wait_root(dve)
        for c in range(self.C):
            self.scale_chunk(dve, out, c)


class NextSum:

    def __init__(self, ctx, mem, name, src, squares, tokens, column, bank=SUM_BANK):
        self.mem, self.src, self.squares = mem, src, squares
        self.sum, self.column = mem.ps[:, bank, 0:tokens], column
        self.updated = ctx.sem(f"{name}_updated")
        self.squared = ctx.sem(f"{name}_squared")
        self.gathered = ctx.sem(f"{name}_gathered")

    def square(self, act, c, k):
        if k == DC - 1:
            act.activation(self.mem.unread[:, self.column:self.column + 1], self.mem.con[:, 0:1], ACT.Ln,
                           bias=self.mem.con[:, CON["eps"]:CON["eps"] + 1])
        act.wait_ge(self.updated, k + 1)
        act.activation(self.squares[:, c, :], self.src[:, c, :], ACT.Square).then_inc(self.squared, 1)

    def gather(self, dve, c):
        dve.wait_ge(self.squared, c + 1)
        if c > 1:
            dve.wait_ge(self.gathered, c - 1)
        dve.tensor_tensor(self.squares[:, 0, :], self.squares[:, 0, :], self.squares[:, c, :],
                          ALU.add).then_inc(self.gathered, 1)

    def add_gathered(self, pe):
        pe.wait_ge(self.gathered, DC - 1)
        pe.matmul(self.sum, self.mem.ones[:, :], self.squares[:, 0, :], start=True, stop=True)

    def add_all(self, pe, order):
        for k, c in enumerate(order):
            pe.wait_ge(self.squared, k + 1)
            pe.matmul(self.sum, self.mem.ones[:, :], self.squares[:, c, :], start=(k == 0), stop=(k == DC - 1))


class Cut:

    def __init__(self, nc, ctx, mem, name, src, tokens):
        self.mem, self.src, self.T = mem, src, tokens
        self.hi_cut = ctx.sem(f"{name}_hi_cut")
        self.lo_cut = [ctx.sem(f"{name}_lo_cut{k}") for k in range(2)]

    def hi_chunk(self, act, ready, c):
        act.wait_ge(ready, c + 1)
        act.copy(self.mem.xhi[:, c, 0:self.T], self.src[:, c, :]).then_inc(self.hi_cut, 1)

    def hi(self, act, ready):
        for c in range(DC):
            self.hi_chunk(act, ready, c)

    def lo_chunk(self, eng, c):
        eng.wait_ge(self.hi_cut, c + 1)
        eng.tensor_tensor(self.mem.xlo[:, c, 0:self.T], self.src[:, c, :], self.mem.xhi[:, c, 0:self.T].bitcast(F32),
                          ALU.subtract).then_inc(self.lo_cut[c % 2], 1)

    def lo(self, eng, odd):
        for c in range(odd, DC, 2):
            self.lo_chunk(eng, c)

    def ready(self, pe, c):
        pe.wait_ge(self.hi_cut, c + 1)
        pe.wait_ge(self.lo_cut[c % 2], c // 2 + 1)


def mla(nc, ctx, mem, d):
    def sem(name):
        return ctx.sem("mla_" + name)

    take = mem.take
    lat, at = take(0, (QC + KVC, L))
    kr, at = take(at, (2, L))
    latn, at = take(at, (QC + KVC, L))
    qn, at = take(at, (HEADS, L))
    kn, at = take(at, (HEADS, L))
    qr, at = take(at, (HEADS // 2, L))
    qs, at = take(at, (HEADS // 2, L))
    v, at = take(at, (3, HEADS * VH))
    cosv, at = take(at, (1, L))
    sinv, at = take(at, (1, L))
    ang, at = take(at, (1, L))
    tmp, at = take(at, (1, L))
    rstd, at = take(at, (2, L))
    idm, at = take(at, (1, P + L))
    post, at = take(at, (1, L))
    xn, at = take(at, (DC, L))
    sm = xn[:, 0:3, :], xn[:, 3:6, :]
    pt = latn[:, 0:3, :]
    o, at = take(at, (HEADS, L))
    small, at = take(at, (2, 16))
    small = small[:, 0, :], small[:, 1, :]
    lat_hi, lat_lo = mem.xhi[:, 0:QC + KVC, :], mem.xlo[:, 0:QC + KVC, :]
    ident, smask = idm[:, 0, 0:P], idm[:, 0, P:P + L]
    kpe, post = kr[:, 0, :], post[:, 0, :]
    posi = post.bitcast(I32)
    cosv, sinv, ang, tmp = cosv[:, 0, :], sinv[:, 0, :], ang[:, 0, :], tmp[:, 0, :]

    iota_set, lat_hi_cut, lat_lo_cut = sem("iota_set"), sem("lat_hi_cut"), sem("lat_lo_cut")
    consts_in, x_in, pos_in, ones_set = sem("consts_in"), sem("x_in"), sem("pos_in"), sem("ones")
    dstep, pos_ready, pos_spread, reduced, sines = (
        sem("dve_steps"), sem("pos_ready"), sem("pos_spread"), sem("reduced"), sem("sines"))
    up_out, rotated = [sem(f"up_out{r}") for r in range(2)], sem("rotated")
    scored, top_found, exped, probs, turned, turned_out, weighed, o_out = (
        sem("scored"), sem("top_found"), sem("exped"), sem("probs"), sem("turned"),
        sem("turned_out"), sem("weighed"), sem("o_out"))

    norm = Norm(nc, ctx, mem, "mla_n", mem.h[:, :, :], DC, VEC["mix0"], xn, rstd[:, 0, :], 2, L)
    cut = Cut(nc, ctx, mem, "mla_x", xn, L)
    down = Stream(nc, ctx, mem, "mla_down", L)
    norm_q = Norm(nc, ctx, mem, "mla_nq", lat[:, 0:QC, :], QC, VEC["q_norm"], latn[:, 0:QC, :], rstd[:, 0, :], 2, L)
    norm_kv = Norm(nc, ctx, mem, "mla_nkv", lat[:, QC:, :], KVC, VEC["kv_norm"], latn[:, QC:, :], rstd[:, 1, :], 3,
                   L)
    out_cut = Cut(nc, ctx, mem, "mla_o", o, L)
    proj = Stream(nc, ctx, mem, "mla_out", L)
    next_sum = NextSum(ctx, mem, "mla_next", mem.h[:, :, :], qn, L, 4)
    n_down = QC + KVC + 2
    X_LOADS = 3
    ups = [qr[:, g, :] for g in range(HEADS // 2)] + [qs[:, g, :] for g in range(HEADS // 2)]
    ups += [qn[:, g, :] for g in range(HEADS)] + [kn[:, g, :] for g in range(HEADS)]
    N_Q = 2 * HEADS
    blocks = [(m, c) for m in range(N_Q) for c in range(QC)]
    blocks += [(m, QC + c) for m in range(N_Q, len(ups)) for c in range(KVC)]
    halves = [blocks[k:k + 4] for k in range(0, len(blocks), 4)]
    val_halves = [(cols, c) for cols in range(2) for c in range(KVC)]
    vals = [(t, min(P, L - t * P), cols) for cols in range(2) for t in range(3)]
    n_up = len(ups) + len(vals)
    n_tiles = n_down + (len(halves) + len(val_halves)) // 2

    def last_half(m):
        if m < len(ups):
            k = max(k for k, blocks_of in enumerate(halves) if m in [b[0] for b in blocks_of])
        else:
            k = len(halves) + KVC * vals[m - len(ups)][2] + KVC - 1
        return 2 * n_down + k

    def take_up(copy, m):
        if m < len(ups):
            return copy(ups[m], mem.ps[:, 4 + m % 4, 0:L])
        t, rows, cols = vals[m - len(ups)]
        return copy(v[0:rows, t, cols * HW:cols * HW + HW], mem.ps[0:rows, 4 + m % 4, :])

    with nc.Block() as block:
        @block.sync
        def _(sp):
            sp.dma_start(mem.h[:, :, 0:META], d["meta"]).then_inc(x_in, 16)
            for c in range(X_LOADS - 1):
                sp.dma_start(mem.h[:, 4 * c:4 * c + 4, META:L], d["x"][:, 4 * c:4 * c + 4, :]).then_inc(x_in, 16)
            sp.dma_start(mem.con[:, :], d["con"]).then_inc(consts_in, 16)
            sp.dma_start(mem.vec[:, :], d["vec"]).then_inc(consts_in, 16)
            sp.dma_start(idm[:, 0, :], d["idm"]).then_inc(consts_in, 16)
            sp.dma_start(posi[0:1, META:L], d["pos"]).then_inc(pos_in, 16)
            for n in range(UNROLL):
                down.load(sp, 0, n, d["mla_down"][n], first=True)
            with sp.Fori(1, n_tiles // UNROLL) as turn:
                for s in range(UNROLL):
                    down.load(sp, turn, s, tile_of(d["mla_down"], turn, s))
            for n in range(n_tiles // UNROLL * UNROLL, n_tiles):
                down.load(sp, n // UNROLL, n % UNROLL, d["mla_down"][n])
            for k in range(SLOTS):
                sp.wait_ge(down.lo_ready[k], (2 * n_tiles - k + SLOTS - 1) // SLOTS)
            for s in range(UNROLL):
                proj.load(sp, 0, s, d["mla_out"][s], first=True)
            with sp.Fori(1, DC // UNROLL) as turn:
                for s in range(UNROLL):
                    proj.load(sp, turn, s, tile_of(d["mla_out"], turn, s))
            proj.load_ahead(sp, DC // UNROLL, d["query"][0])

        @block.gpsimd
        def _(pool):
            first_los(pool, down, cut)
            for n in range(1, n_tiles):
                for e in range(2):
                    down.cut_lo(pool, n // UNROLL, n % UNROLL, e)
            for e in range(2):
                proj.cut_lo(pool, 0, 0, e)
            for c in range(DC):
                out_cut.lo_chunk(pool, c)
            for s in range(1, UNROLL):
                for e in range(2):
                    proj.cut_lo(pool, 0, s, e)
            with pool.Fori(1, DC // UNROLL) as turn:
                for s in range(UNROLL):
                    for e in range(2):
                        proj.cut_lo(pool, turn, s, e)

        @block.scalar
        def _(act):
            act.wait_ge(x_in, 16 * X_LOADS)
            norm.square_half(act)
            act.wait_ge(consts_in, 48)
            norm.root(act)
            first_cuts(act, down, norm, cut)
            act.wait_ge(reduced, 1)
            act.activation(sinv, ang, ACT.Sin).then_inc(sines, 1)
            act.activation(cosv, ang, ACT.Sin, scale=0.5).then_inc(sines, 1)

            def latents_hi(c0, count, scaled):
                for c in range(count):
                    act.wait_ge(scaled, c + 1)
                    act.copy(lat_hi[:, c0 + c, :], latn[:, c0 + c, :]).then_inc(lat_hi_cut, 1)

            for n in range(n_down):
                if n == n_down - 1:
                    act.wait_ge(down.done, 2 * n_down - 1)
                    latents_hi(0, QC, norm_q.scaled)
                down.wait_product(act, n // UNROLL, n % UNROLL)
                down.cut_hi(act, (n + 2) // UNROLL, (n + 2) % UNROLL)
                dst = lat[:, n, :] if n < QC + KVC else kr[:, n - QC - KVC, :]
                act.copy(dst, down.bank(n)).then_inc(down.free[n % 2], 1)
                if n == QC + KVC - 1:
                    norm_q.root(act)
            norm_kv.root(act)
            for k in range(2 * n_down, 2 * n_tiles):
                ahead = k // 2 + 2
                if ahead < n_tiles:
                    down.cut_hi_half(act, ahead // UNROLL, ahead % UNROLL, k % 2)
                if k == 2 * n_down + 1:
                    latents_hi(QC, KVC, norm_kv.scaled)
                for m in range(1, n_up, 2):
                    if last_half(m) == k:
                        act.wait_ge(down.done, k + 1)
                        take_up(act.copy, m).then_inc(up_out[1], 1)
            act.wait_ge(down.done, 2 * n_tiles)
            proj.cut_hi(act, 0, 0, first=True)
            proj.cut_hi(act, 0, 1, first=True)

            def exps(head, e):
                for t in range(3):
                    nk = NKEYS_SEEN[t]
                    act.wait_ge(top_found, head * 3 + (t + 1))
                    act.activation(sm[e][:, t, 0:nk], sm[e][:, t, 0:nk], ACT.Exp, bias=small[e][:, t:t + 1],
                                   accum_out=small[e][:, 3 + t:4 + t]).then_inc(exped, 1)

            def take_out(head):
                for k in range(3):
                    rows = min(P, L - k * P)
                    first = Q0[2] if k == 2 else k * P
                    act.wait_ge(turned, head * 3 + (k + 1))
                    act.copy(pt[0:rows, k, first:L], mem.ps[0:rows, 3 + k, first:L]).then_inc(turned_out, 1)
                act.wait_ge(weighed, head + 1)
                at_head = bass.ds(head, 1) if not isinstance(head, int) else slice(head, head + 1)
                act.copy(o[:, at_head, :], mem.ps[:, 7:8, 0:L]).then_inc(o_out, 1)
                act.wait_ge(o_out, head + 1)
                act.copy(mem.xhi[:, at_head, :], o[:, at_head, :]).then_inc(out_cut.hi_cut, 1)

            exps(0, 0)
            with act.Fori(0, HEADS // 2 - 1) as pair:
                for e in range(2):
                    exps(pair * 2 + (e + 1), 1 - e)
                    take_out(pair * 2 + e)
            exps(HEADS - 1, 1)
            take_out(HEADS - 2)
            take_out(HEADS - 1)
            for n in range(DC):
                if n + 2 < DC:
                    proj.cut_hi(act, (n + 2) // UNROLL, (n + 2) % UNROLL)
                next_sum.square(act, n, n)

        @block.vector
        def _(dve):
            step = Steps(dve, dstep)
            dve.memset(mem.ones[:, :], 1.0).then_inc(ones_set, 1)
            dve.wait_ge(x_in, 16 * X_LOADS)
            norm.square(dve)
            dve.wait_ge(consts_in, 48)
            dve.tensor_copy(post[0:1, 0:META], mem.con[0:1, 0:META]).then_inc(pos_ready, 1)
            dve.wait_ge(pos_in, 16)
            dve.tensor_scalar(post[0:1, META:L], posi[0:1, META:L], float(META), None,
                              ALU.add).then_inc(pos_ready, 1)
            scale_and_cut(dve, norm, xn, cut)
            dve.tensor_copy(mem.iota[:, :, :],
                            mem.con[:, 0:P].unsqueeze(2).to_broadcast([P, P, ST])).then_inc(iota_set, 1)
            dve.tensor_copy(mem.token[:, :], mem.con[:, CON["token"]:CON["token"] + GT]).then_inc(iota_set, 1)
            dve.wait_ge(iota_set, 2)
            two_pi = (6.28125, float(np.float32(2 * np.pi - 6.28125) // 2.0 ** -20 * 2.0 ** -20))
            rest = 2 * np.pi - two_pi[0] - two_pi[1]
            magic = 1.5 * 2.0 ** 23
            dve.wait_ge(pos_spread, 1)
            step.done(dve.tensor_scalar(ang, mem.ps[:, 3, 0:L], mem.con[:, CON["freq"]:CON["freq"] + 1], None,
                                        ALU.mult))
            step.done(dve.tensor_scalar(tmp, ang, float(1 / (2 * np.pi)), magic, ALU.mult, ALU.add))
            step.done(dve.tensor_scalar(tmp, tmp, -magic, None, ALU.add))
            for part in (*two_pi, rest):
                step.done(dve.scalar_tensor_tensor(ang, tmp, -float(part), ang, ALU.mult, ALU.add))
            dve.tensor_scalar(ang, ang, float(np.float32(-np.pi)), float(np.float32(np.pi)), ALU.max,
                              ALU.min).then_inc(reduced, 1)
            dve.wait_ge(sines, 2)
            step.done(dve.tensor_tensor(cosv, cosv, cosv, ALU.mult))
            step.done(dve.tensor_scalar(cosv, cosv, -2.0, 1.0, ALU.mult, ALU.add))
            step.done(dve.tensor_scalar(sinv, sinv, mem.con[:, CON["sign"]:CON["sign"] + 1], None, ALU.mult))

            def out_of_psum(tiles):
                dve.wait_ge(down.free[0], (tiles + 1) // 2 + 1)
                dve.wait_ge(down.free[1], tiles // 2 + 1)

            out_of_psum(QC)
            norm_q.square(dve)
            out_of_psum(QC + KVC)
            norm_kv.square(dve)
            norm_q.scale(dve, latn[:, 0:QC, :])

            def latents_lo(c0, count):
                for c in range(c0, c0 + count):
                    dve.wait_ge(lat_hi_cut, c + 1)
                    dve.tensor_tensor(lat_lo[:, c, :], latn[:, c, :], lat_hi[:, c, :].bitcast(F32),
                                      ALU.subtract).then_inc(lat_lo_cut, 1)

            latents_lo(0, QC)
            out_of_psum(n_down)
            step.done(dve.tensor_tensor(kr[:, 0, :], kr[:, 0, :], cosv, ALU.mult))
            step.done(dve.tensor_tensor(kr[:, 1, :], kr[:, 1, :], sinv, ALU.mult))
            dve.tensor_tensor(kr[:, 0, :], kr[:, 0, :], kr[:, 1, :], ALU.add).then_inc(rotated, 1)
            norm_kv.scale(dve, latn[:, QC:, :])
            wide = [P, HEADS // 2, L]
            for m in range(0, n_up, 2):
                dve.wait_ge(down.done, last_half(m) + 1)
                take_up(dve.tensor_copy, m).then_inc(up_out[0], 1)
                if m == 2:
                    latents_lo(QC, KVC)
                if m == HEADS:
                    for r in range(2):
                        dve.wait_ge(up_out[r], HEADS // 2)
                    step.add(dve.tensor_tensor(qr, qr, cosv.unsqueeze(1).to_broadcast(wide), ALU.mult))
                if m == HEADS + 2:
                    step.add(dve.tensor_tensor(qs, qs, sinv.unsqueeze(1).to_broadcast(wide), ALU.mult))
                if m == HEADS + 4:
                    step.wait(1)
                    dve.tensor_tensor(qr, qr, qs, ALU.add).then_inc(rotated, 1)

            def tops(head, e):
                for t in range(3):
                    nk = NKEYS_SEEN[t]
                    dve.wait_ge(scored, head * 3 + (t + 1))
                    step.add(dve.scalar_tensor_tensor(sm[e][:, t, 0:nk], mem.ps[:, t, 0:nk], SCALE,
                                                      smask[:, L - P - Q0[t]:L - P - Q0[t] + nk], ALU.mult, ALU.add))
                    step.wait(1)
                    dve.tensor_reduce(small[e][:, t:t + 1], sm[e][:, t, 0:nk], AX.X, ALU.max,
                                      negate=True).then_inc(top_found, 1)

            def divide(head, e):
                for t in range(3):
                    nk = NKEYS_SEEN[t]
                    dve.wait_ge(exped, head * 3 + (t + 1))
                    step.done(dve.reciprocal(small[e][:, 6 + t:7 + t], small[e][:, 3 + t:4 + t]))
                    dve.tensor_scalar(sm[e][:, t, 0:nk], sm[e][:, t, 0:nk], small[e][:, 6 + t:7 + t], None,
                                      ALU.mult).then_inc(probs, 1)

            per_pair = 2 * 3 * 2
            tops(0, 0)
            with dve.Fori(0, HEADS // 2 - 1) as pair:
                step.enter(pair, per_pair)
                for e in range(2):
                    divide(pair * 2 + e, e)
                    tops(pair * 2 + (e + 1), 1 - e)
                step.leave(HEADS // 2 - 1, per_pair)
            divide(HEADS - 2, 0)
            tops(HEADS - 1, 1)
            divide(HEADS - 1, 1)
            update_residual(dve, mem, proj, 0, next_sum)

        @block.tensor
        def _(pe):
            down.open(pe)
            proj.open(pe)
            pe.wait_ge(ones_set, 1)
            norm.add_up(pe)
            pe.wait_ge(pos_ready, 2)
            pe.matmul(mem.ps[:, 3, 0:L], mem.ones[0:1, :], post[0:1, :], start=True, stop=True).then_inc(pos_spread, 1)
            for n in range(n_down):
                down.multiply(pe, n // UNROLL, n % UNROLL, down.bank(n), cut if n == 0 else None)
                if n == QC + KVC - 1:
                    norm_q.add_up(pe)
            pe.wait_ge(reduced, 1)
            norm_kv.add_up(pe)

            def passes(products, k):
                n, e = k // 2, k % 2
                down.wait_hi(pe, n // UNROLL, n % UNROLL, e)
                for m, out, x, w, first, last, latent_first in products:
                    if first:
                        if m >= 4:
                            pe.wait_ge(up_out[m % 2], (m - 4) // 2 + 1)
                        pe.wait_ge(lat_lo_cut, QC if m < N_Q else QC + KVC)
                    for part in range(2):
                        a, b = (x[part], w[0]) if latent_first else (w[0], x[part])
                        pe.matmul(out, a, b, start=first and part == 0, stop=False)
                down.wait_lo(pe, n // UNROLL, n % UNROLL, e)
                for m, out, x, w, first, last, latent_first in products:
                    a, b = (x[0], w[1]) if latent_first else (w[1], x[0])
                    mm = pe.matmul(out, a, b, start=False, stop=last)
                mm.then_inc(down.done, 1)

            for k, blocks_of in enumerate(halves):
                slot, todo = (2 * n_down + k) % SLOTS, []
                for b, (m, c) in enumerate(blocks_of):
                    w = [t[:, slot, b * P:(b + 1) * P] for t in (mem.whi, mem.wlo)]
                    x = [t[:, c, :] for t in (lat_hi, lat_lo)]
                    todo.append((m, mem.ps[:, 4 + m % 4, 0:L], x, w, c in (0, QC), c in (QC - 1, QC + KVC - 1), False))
                passes(todo, 2 * n_down + k)
            for k, (cols, c) in enumerate(val_halves):
                k = k + len(halves)
                slot, todo = (2 * n_down + k) % SLOTS, []
                for q, (t, rows, _) in enumerate(vals[3 * cols:3 * cols + 3]):
                    m = len(ups) + 3 * cols + q
                    w = [part[:, slot, :] for part in (mem.whi, mem.wlo)]
                    x = [part[:, QC + c, t * P:t * P + rows] for part in (lat_hi, lat_lo)]
                    todo.append((m, mem.ps[0:rows, 4 + m % 4, :], x, w, c == 0, c == KVC - 1, True))
                passes(todo, 2 * n_down + k)
            pe.wait_ge(rotated, 2)
            pe.wait_ge(up_out[0], (n_up + 1) // 2)
            pe.wait_ge(up_out[1], n_up // 2)

            def scores(head):
                pair, lanes = head // 2, slice(ROPE * (head % 2), ROPE * (head % 2) + ROPE)
                for t in range(3):
                    nk = NKEYS_SEEN[t]
                    if head:
                        pe.wait_ge(top_found, (head - 1) * 3 + t + 1)
                    pe.matmul(mem.ps[:, t, 0:nk], qn[:, head, Q0[t]:Q0[t] + P], kn[:, head, 0:nk], start=True,
                              stop=False)
                    pe.matmul(mem.ps[:, t, 0:nk], qr[lanes, pair, Q0[t]:Q0[t] + P], kpe[lanes, 0:nk], start=False,
                              stop=True).then_inc(scored, 1)

            scores(0)
            scores(1)
            for head in range(HEADS):
                for k in range(3):
                    rows = min(P, L - k * P)
                    for t in range(k, 3):
                        pe.wait_ge(probs, head * 3 + t + 1)
                        tr = pe.transpose(mem.ps[0:rows, 3 + k, Q0[t]:Q0[t] + P],
                                          sm[head % 2][:, t, k * P:k * P + rows], ident)
                    tr.then_inc(turned, 1)
                if head + 2 < HEADS:
                    scores(head + 2)
                pe.wait_ge(o_out, head)
                for k in range(3):
                    rows = min(P, L - k * P)
                    first = Q0[2] if k == 2 else k * P
                    pe.wait_ge(turned_out, head * 3 + k + 1)
                    mm = pe.matmul(mem.ps[:, 7, first:L], v[0:rows, k, head * P:head * P + P], pt[0:rows, k, first:L],
                                   start=(k == 0), stop=(k == 2))
                mm.then_inc(weighed, 1)
            multiply_turns(pe, proj, 0, DC // UNROLL, out_cut)
            next_sum.add_gathered(pe)


def first_cuts(act, stream, norm, cut):
    for c in range(DC):
        if c in (0, DC // 2):
            stream.cut_hi(act, 0, c // (DC // 2), first=True)
        cut.hi_chunk(act, norm.scaled, c)


def scale_and_cut(dve, norm, out, cut):
    norm.wait_root(dve)
    for c in range(DC):
        norm.scale_chunk(dve, out, c)
        if c in (2, 4, 6):
            cut.lo_chunk(dve, c - 2)
    cut.lo_chunk(dve, DC - 2)


def update_residual(dve, mem, stream, turn, next_sum):
    for c in range(DC):
        hc, s = mem.h[:, c, :], c % UNROLL
        stream.wait_product(dve, turn + c // UNROLL, s)
        dve.tensor_tensor(hc, hc, stream.bank(s), ALU.add).then_inc(next_sum.updated, 1)
        dve.wait_ge(next_sum.updated, c + 1)
        dve.sem_inc(stream.free[s % 2], 1)
        if c > 1:
            next_sum.gather(dve, c - 1)
    next_sum.gather(dve, DC - 1)


def first_los(pool, stream, cut):
    for e in range(2):
        stream.cut_lo(pool, 0, 0, e)
        for c in (e * DC // 2 + 1, e * DC // 2 + 3):
            cut.lo_chunk(pool, c)


def lo_of_turns(pool, stream, turns, cut):
    first_los(pool, stream, cut)
    for s in range(1, UNROLL):
        for e in range(2):
            stream.cut_lo(pool, 0, s, e)
    if turns > 1:
        with pool.Fori(1, turns) as turn:
            for s in range(UNROLL):
                for e in range(2):
                    stream.cut_lo(pool, turn, s, e)


def multiply_turns(pe, stream, first, last, cut):
    for s in range(UNROLL):
        stream.multiply(pe, first, s, stream.bank(s), cut if s == 0 else None)
    with pe.Fori(first + 1, last) as turn:
        for s in range(UNROLL):
            stream.multiply(pe, turn, s, stream.bank(s))


def tile_of(tiles, turn, s):
    return tiles[bass.ds(turn * UNROLL + s, 1)].rearrange("a p f -> p (a f)")


def rglru(nc, ctx, mem, d):
    def sem(name):
        return ctx.sem("lru_" + name)

    take = mem.take
    xn, at = take(0, (DC, L))
    gate, at = take(at, (DC, L))
    xp, at = take(at, (DC, L + CONV - 1))
    xc, at = take(at, (DC, L))
    r, at = take(at, (DC, L))
    i, at = take(at, (DC, L))
    a, at = take(at, (DC, L))
    b, at = take(at, (DC, L))
    wa, at = take(at, (DC, P))
    wx, at = take(at, (DC, P))
    rstd, at = take(at, (1, L))
    small, at = take(at, (9, DC))
    rstd = rstd[:, 0, :]
    nlam, e, z, z2, poly, c8, negc8, half_ba, half_bx = (small[:, n, :] for n in range(9))

    norm = Norm(nc, ctx, mem, "lru_n", mem.h[:, :, :], DC, VEC["mix1"], xn, rstd, SUM_BANK, L, given=True)
    cut = Cut(nc, ctx, mem, "lru_x", xn, L)
    st = Stream(nc, ctx, mem, "lru_s", L)
    ycut = Cut(nc, ctx, mem, "lru_y", b, L)
    dstep, padded, w_in, conved, gated, gate_out, lam_abs, lam_exp, ready, decays, squared, rooted, scanned, gelus = (
        sem(n) for n in ("dve_steps", "padded", "w_in", "conved", "gated", "gate_out", "lam_abs", "lam_exp",
                         "ready", "decays", "squared", "rooted", "scanned", "gelus"))
    states = sem("states")
    next_sum = NextSum(ctx, mem, "lru_next", mem.h[:, :, META:L], r[:, :, 0:SEQ], SEQ, 6)
    OUT, END = 2 * DC // UNROLL, 3 * DC // UNROLL
    PRODUCTS, FUNCTIONS, ROOTS, GELUS = 2, 3, DC + 3, DC + 5
    raw_gates = GELUS - DC
    gelus_at = {GELUS: [5, 0, 1], GELUS + 1: [6, 2, 3, 4], GELUS + 2: [7]}
    gelu_order = [c for n in sorted(gelus_at) for c in gelus_at[n]]

    with nc.Block() as block:
        @block.sync
        def _(sp):
            st.loaded_before(sp)
            sp.dma_start(wa, d["lru_wa"]).then_inc(w_in, 16)
            sp.dma_start(wx, d["lru_wx"]).then_inc(w_in, 16)
            with sp.Fori(1, END) as turn:
                for s in range(UNROLL):
                    st.load(sp, turn, s, tile_of(d["lru_w"], turn, s))
            st.load_ahead(sp, END, d["query"][1])

        @block.gpsimd
        def _(pool):
            lo_of_turns(pool, st, OUT, cut)
            for e in range(2):
                st.cut_lo(pool, OUT, 0, e)
            ycut.lo(pool, 1)
            for s in range(1, UNROLL):
                for e in range(2):
                    st.cut_lo(pool, OUT, s, e)
            with pool.Fori(OUT + 1, END) as turn:
                for s in range(UNROLL):
                    for e in range(2):
                        st.cut_lo(pool, turn, s, e)

        @block.scalar
        def _(act):
            norm.root(act)
            first_cuts(act, st, norm, cut)
            act.wait_ge(lam_abs, 1)
            act.activation(e, z, ACT.Exp, scale=-1.0).then_inc(lam_exp, 1)
            def gates(c):
                for k, (dst, bias) in enumerate(((r, half_ba), (i, half_bx))):
                    act.wait_ge(gated, 2 * c + k + 1)
                    act.activation(dst[:, c, :], mem.ps[:, 2 + (2 * c + k) % 4, 0:L], ACT.Tanh,
                                   bias=bias[:, c:c + 1], scale=0.5).then_inc(gate_out, 1)
                act.wait_ge(gate_out, 2 * c + 1)
                act.activation(a[:, c, :], r[:, c, :], ACT.Exp, bias=negc8[:, c:c + 1],
                               scale=negc8[:, c:c + 1]).then_inc(decays, 1)
                act.activation(r[:, c, :], r[:, c, :], ACT.Tanh, bias=c8[:, c:c + 1],
                               scale=c8[:, c:c + 1]).then_inc(decays, 1)

            for n in range(2 * DC):
                st.cut_hi(act, (n + 2) // UNROLL, (n + 2) % UNROLL)
                st.wait_product(act, n // UNROLL, n % UNROLL)
                if n < DC:
                    act.copy(xp[:, n, CONV - 1:], st.bank(n % 2)).then_inc(st.free[n % 2], 1)
                elif n < GELUS:
                    act.copy(gate[:, n - DC, :], st.bank(n % 2)).then_inc(st.free[n % 2], 1)
                if n == FUNCTIONS:
                    act.wait_ge(ready, 4)
                if 0 <= n - FUNCTIONS < DC:
                    gates(n - FUNCTIONS)
                if n in (ROOTS, ROOTS + 1):
                    k = n - ROOTS
                    q = slice(k * DC // 2, (k + 1) * DC // 2)
                    act.wait_ge(squared, (k + 1) * DC // 2)
                    act.activation(b[:, q, :], b[:, q, :], ACT.Sqrt).then_inc(rooted, 1)
                for c in gelus_at.get(n, ()):
                    if c < raw_gates:
                        act.wait_ge(st.free[(GELUS - 1) % 2], (GELUS - 1) // 2 + 2)
                        act.wait_ge(st.free[GELUS % 2], (GELUS - 2) // 2 + 2)
                        act.activation(gate[:, c, :], gate[:, c, :], ACT.Gelu_apprx_tanh).then_inc(gelus, 1)
                    else:
                        act.activation(gate[:, c, :], st.bank(n % 2), ACT.Gelu_apprx_tanh).then_inc(gelus, 1)
                        act.wait_ge(gelus, gelu_order.index(c) + 1)
                        act.sem_inc(st.free[n % 2], 1)
            ycut.hi(act, states)
            for c in range(DC):
                n = OUT * UNROLL + c + 2
                if c + 2 < DC:
                    st.cut_hi(act, n // UNROLL, n % UNROLL)
                next_sum.square(act, c, c)

        @block.vector
        def _(dve):
            step = Steps(dve, dstep)
            lam = mem.vec[:, VEC["lam"]:VEC["lam"] + DC]
            dve.memset(xp[:, :, 0:CONV - 1], 0.0).then_inc(padded, 1)
            step.done(dve.tensor_scalar(nlam, lam, -1.0, None, ALU.mult))
            dve.tensor_tensor(z, lam, nlam, ALU.max).then_inc(lam_abs, 1)
            scale_and_cut(dve, norm, xn, cut)
            dve.wait_ge(lam_exp, 1)
            step.done(dve.tensor_scalar(z, e, 2.0, None, ALU.add))
            step.done(dve.reciprocal(z, z))
            step.done(dve.tensor_tensor(z, z, e, ALU.mult))
            step.done(dve.tensor_tensor(z2, z, z, ALU.mult))
            step.done(dve.tensor_scalar(poly, z2, 1.0 / 17, 1.0 / 15, ALU.mult, ALU.add))
            for k in (13, 11, 9, 7, 5, 3, 1):
                step.done(dve.tensor_tensor(poly, poly, z2, ALU.mult))
                step.done(dve.tensor_scalar(poly, poly, 1.0 / k, None, ALU.add))
            step.done(dve.tensor_tensor(poly, poly, z, ALU.mult))
            step.done(dve.tensor_scalar(nlam, nlam, 0.0, None, ALU.max))
            step.done(dve.scalar_tensor_tensor(poly, poly, 2.0, nlam, ALU.mult, ALU.add))
            dve.tensor_scalar(c8, poly, LRU_C / 2, None, ALU.mult).then_inc(ready, 1)
            dve.tensor_scalar(negc8, poly, -LRU_C / 2, None, ALU.mult).then_inc(ready, 1)
            for half, bias in ((half_ba, "b_a"), (half_bx, "b_x")):
                dve.tensor_scalar(half, mem.vec[:, VEC[bias]:VEC[bias] + DC], 0.5, None, ALU.mult).then_inc(ready, 1)
            dve.wait_ge(padded, 1)
            vec = mem.vec

            def convolve(c):
                dve.wait_ge(st.free[c % 2], c // 2 + 2)
                for j in range(CONV):
                    w = vec[:, VEC[f"cw{j}"] + c:VEC[f"cw{j}"] + c + 1]
                    if j == 0:
                        step.done(dve.tensor_scalar(xc[:, c, :], xp[:, c, 0:L], w,
                                                    vec[:, VEC["conv_b"] + c:VEC["conv_b"] + c + 1], ALU.mult, ALU.add))
                        continue
                    ins = dve.scalar_tensor_tensor(xc[:, c, :], xp[:, c, j:j + L], w, xc[:, c, :], ALU.mult, ALU.add)
                    if j < CONV - 1:
                        step.done(ins)
                    else:
                        ins.then_inc(conved, 1)

            def inputs(c):
                dve.wait_ge(decays, 2 * (c + 1))
                dve.wait_ge(conved, c + 1)
                step.done(dve.tensor_tensor(b[:, c, :], a[:, c, :], a[:, c, :], ALU.mult))
                dve.scalar_tensor_tensor(b[:, c, :], b[:, c, :], 1.0, r[:, c, :], ALU.add, ALU.mult).then_inc(squared, 1)
                step.add(dve.scalar_tensor_tensor(i[:, c, :], i[:, c, :], 1.0, xc[:, c, :], ALU.add, ALU.mult))

            for n in range(DC + FUNCTIONS + 1):
                if n < DC:
                    convolve(n)
                if n > FUNCTIONS:
                    inputs(n - FUNCTIONS - 1)
            for c in range(DC):
                dve.wait_ge(rooted, c // (DC // 2) + 1)
                step.done(dve.scalar_tensor_tensor(b[:, c, :], b[:, c, :], 0.5, i[:, c, :], ALU.mult, ALU.mult))
                dve.tensor_tensor_scan(xc[:, c, :], a[:, c, :], b[:, c, :], 0.0, ALU.mult, ALU.add).then_inc(scanned, 1)
            for c in range(DC):
                dve.wait_ge(scanned, c + 1)
                dve.wait_ge(gelus, gelu_order.index(c) + 1)
                dve.tensor_tensor(b[:, c, :], xc[:, c, :], gate[:, c, :], ALU.mult).then_inc(states, 1)
            ycut.lo(dve, 0)
            update_residual(dve, mem, st, OUT, next_sum)

        @block.tensor
        def _(pe):
            st.open(pe)
            for n in range(2 * DC):
                st.multiply(pe, n // UNROLL, n % UNROLL, st.bank(n), cut if n == 0 else None)
                c = n - PRODUCTS
                if not 0 <= c < DC:
                    continue
                if c == 0:
                    pe.wait_ge(w_in, 32)
                pe.wait_ge(conved, c + 1)
                for k, w in enumerate((wa, wx)):
                    m = 2 * c + k
                    if m >= 4:
                        pe.wait_ge(gate_out, m - 3)
                    pe.matmul(mem.ps[:, 2 + m % 4, 0:L], w[:, c, :], xc[:, c, :], start=True,
                              stop=True).then_inc(gated, 1)
            multiply_turns(pe, st, OUT, END, ycut)
            next_sum.add_gathered(pe)


def peer(nc, ctx, mem, d, layer):
    def sem(name):
        return ctx.sem(f"peer{layer}_{name}")

    T = L if layer == 0 else SEQ
    G, NG = T // GT, T // ST
    act_w = mem.big[:, 0:NK * T].rearrange("p (i t) -> p i t", t=T)
    h = mem.h[:, :, L - T:L]
    take = mem.take
    qt, at = take(HALF * T, (2, G, PH, GT))
    xn, at = take(at, (DC, T))
    SPREADS = 2 + PARTS
    spread, _ = take(HALF * T, (G * SPREADS * PH * TOPK // 2,))
    spread = spread.bitcast(BF16).rearrange("p (g w h k) -> p g w h k", w=SPREADS, h=PH, k=TOPK)
    scores, at = take(at, (G, 2 * NK))
    rstd, at = take(at, (1, L))
    keys, at = take(at, (2, NK))
    s1, at = take(at, (4, NK))
    s2, at = take(at, (4, NK))
    cand, at = take(at, (2, TOPK * TOPK))
    cand2, at = take(at, (2, TOPK * TOPK))
    hot, at = take(at, (4, TOPK, TOPK))
    top, at = take(at, (4, TOPK))
    topi, at = take(at, (4, TOPK))
    best, at = take(at, (2, TOPK))
    best_at, at = take(at, (2, TOPK))
    place, at = take(at, (4, TOPK))
    ij, at = take(at, (2, G, TOPK))
    gates, at = take(at, (G, TOPK))
    g_rest, at = take(at, (G, TOPK))
    g_part, _ = take(at, (PARTS, G, TOPK // 2))
    g_part = g_part.bitcast(BF16)
    den, at = take(at, (2, G))
    rstd = rstd[:, 0, :]
    topi, place, best_at = topi.bitcast(U32), place.bitcast(U32), best_at.bitcast(U32)
    iota = mem.con[:, CON["iota"]:CON["iota"] + P]
    head_mask = mem.con[:, CON["head"]:CON["head"] + PH]

    norm = Norm(nc, ctx, mem, f"peer{layer}_n", h, DC, VEC[f"ffn{layer}"], xn, rstd[:, 0:T], SUM_BANK, T, given=True)
    cut = Cut(nc, ctx, mem, f"peer{layer}_x", xn, T)
    st = Stream(nc, ctx, mem, f"peer{layer}_s", T)
    keys_in, scored, scores_out, dstep, shifted, exped, spread_done, placed, chosen = (
        sem(n) for n in ("keys_in", "scored", "scores_out", "dve_steps", "shifted", "exped", "spread_done", "placed",
                         "chosen"))
    turns_taken = sem("turns_taken")
    hots_ready, scattered, gated = sem("hots_ready"), sem("scattered"), sem("gated")
    w_hi_cut, w_lo_cut = sem("w_hi_cut"), sem("w_lo_cut")

    TQ, TH = 2 * PH // UNROLL, HALF // UNROLL
    U0, U1, V0, V1, END = TQ, TQ + TH, TQ + 2 * TH, TQ + 3 * TH, TQ + 4 * TH
    MID, SPREAD = U0 + TH * 3 // 4, U1 - 2

    GBANK = 7
    if T <= 256:
        pieces = [[[(c // 2, 256 * (c % 2), 0, T)] for c in range(DC)]] * 2
    else:
        side = 512 - T
        pieces = [[[(c, 0, 0, T)] for c in range(GBANK)] + [last]
                  for last in ([(0, T, 0, side), (1, T, side, T - side)], [(GBANK, 0, 0, T)])]

    sum_bank = SUM_BANK if layer == 0 else FINAL_SUM_BANK
    h_order = sorted(range(DC), key=lambda c: pieces[1][c][0][0] != sum_bank)
    next_sum = NextSum(ctx, mem, f"peer{layer}_next", h, take(0, (DC, T))[0], T, 5 + 2 * layer, sum_bank)

    def products(pe, half, m):
        pe.wait_ge(hots_ready, half * NG + m + 1)
        for t in range(ST):
            o = mem.ps[:, GBANK, t * HALF:(t + 1) * HALF]
            for k in range(PARTS):
                mm = pe.matmul(o, mem.j_hot[:, :, t], mem.i_gate[:, k, :, t], start=(k == 0), stop=(k == PARTS - 1))
        mm.then_inc(scattered, 1)

    def hots(dve, step, half, m):
        tok = bass.ds(m * ST, ST) if not isinstance(m, int) else slice(m * ST, m * ST + ST)
        wide, wide_i = [P, P, ST], [P, HALF, ST]
        dve.wait_ge(scattered, half * NG + m)
        step.add(dve.tensor_tensor(mem.i_hot[:, :, :], mem.iota[:, half * HALF:(half + 1) * HALF, :],
                                   mem.idx[:, 0, tok].unsqueeze(1).to_broadcast(wide_i), ALU.is_equal))
        step.add(dve.tensor_tensor(mem.j_hot[:, :, :], mem.iota[:, :, :],
                                   mem.idx[:, 1, tok].unsqueeze(1).to_broadcast(wide), ALU.is_equal))
        step.wait(2)
        for k in range(PARTS):
            ins = dve.tensor_tensor(mem.i_gate[:, k], mem.i_hot[:, :, :],
                                    mem.g[:, k, tok].unsqueeze(1).to_broadcast(wide_i), ALU.mult)
            if k < PARTS - 1:
                step.add(ins)
            else:
                ins.then_inc(hots_ready, 1)

    HOT_STEPS = 2 + PARTS - 1
    GROUPS_AFTER = [1, 3]
    LAST_AFTER = GROUPS_AFTER if NG == 2 * TH else list(range(UNROLL))
    assert 2 * (TH - 1) + len(LAST_AFTER) == NG

    def gate_act(dve, half, m):
        tok = bass.ds(m * ST, ST) if not isinstance(m, int) else slice(m * ST, m * ST + ST)
        dve.wait_ge(scattered, half * NG + m + 1)
        w = act_w[:, half * HALF:(half + 1) * HALF, tok]
        g = mem.ps[:, GBANK, :].rearrange("p (t i) -> p i t", i=HALF)
        dve.tensor_tensor(w, w, g, ALU.mult).then_inc(gated, 1)

    def cut_w_hi(act, n, r):
        i = bass.ds(n, 1) if not isinstance(n, int) else slice(n, n + 1)
        act.copy(mem.xhi[:, r:r + 1, 0:T], act_w[:, i, :]).then_inc(w_hi_cut, 1)

    def cut_w_lo(dve, n, r):
        i = bass.ds(n, 1) if not isinstance(n, int) else slice(n, n + 1)
        dve.wait_ge(w_hi_cut, n + 1)
        dve.tensor_tensor(mem.xlo[:, r:r + 1, 0:T], act_w[:, i, :], mem.xhi[:, r:r + 1, 0:T].bitcast(F32),
                          ALU.subtract).then_inc(w_lo_cut, 1)

    def apply_v(pe, turn, s, half, fresh=()):
        pe.wait_ge(w_lo_cut, (turn - V0) * UNROLL + (s + 1))
        fresh = set(fresh)
        for e in range(2):
            k = (2 * s + e) % SLOTS
            st.wait_hi(pe, turn, s, e)
            for w, x in ((mem.whi, mem.xhi), (mem.whi, mem.xlo), (mem.wlo, mem.xhi)):
                if w is mem.wlo:
                    st.wait_lo(pe, turn, s, e)
                for c in range(DC // 2):
                    for bank, col, tok, n in pieces[half][e * DC // 2 + c]:
                        mm = pe.matmul(mem.ps[:, bank, col:col + n], w[:, k, c * P:(c + 1) * P],
                                       x[:, s, tok:tok + n], start=bank in fresh, stop=False,
                                       skip_group_check=True)
                        fresh.discard(bank)
            mm.then_inc(st.done, 1)

    with nc.Block() as block:
        @block.sync
        def _(sp):
            st.loaded_before(sp)
            sp.dma_start(keys, d["keys"][layer]).then_inc(keys_in, 16)
            with sp.Fori(1, TQ) as turn:
                for s in range(UNROLL):
                    st.load(sp, turn, s, tile_of(d["query"][layer], turn, s))
            with sp.Fori(U0, V0) as turn:
                for s in range(UNROLL):
                    st.load(sp, turn, s, tile_of(d["u"][layer], turn - U0, s))
            with sp.Fori(V0, END) as turn:
                for s in range(UNROLL):
                    st.load(sp, turn, s, tile_of(d["v"][layer], turn - V0, s))
            if layer == 0:
                st.load_ahead(sp, END, d["lru_w"])

        @block.gpsimd
        def _(pool):
            lo_of_turns(pool, st, 1, cut)
            with pool.Fori(1, TQ) as turn:
                for q in (2, 3, 6, 7):
                    st.cut_lo(pool, turn, q // 2, q % 2)
            with pool.Fori(TQ, U1) as turn:
                for s in range(UNROLL):
                    for e in range(2):
                        st.cut_lo(pool, turn, s, e)
            with pool.Fori(U1, V1) as turn:
                for q in (0, 2, 3, 4, 6, 7):
                    st.cut_lo(pool, turn, q // 2, q % 2)
            with pool.Fori(V1, END) as turn:
                for q in (2, 3, 6, 7):
                    st.cut_lo(pool, turn, q // 2, q % 2)

        @block.scalar
        def _(act):
            norm.root(act)
            first_cuts(act, st, norm, cut)
            with act.Fori(0, TQ) as turn:
                for s in range(UNROLL):
                    st.wait_product(act, turn, s)
                    st.cut_hi(act, turn + (s + 2) // UNROLL, (s + 2) % UNROLL)
                    act.copy(qt[:, s % 2, :, bass.ds(turn * 2 + s // 2, 1), :].rearrange("p g a t -> p g (a t)"),
                             st.bank(s).rearrange("p (g t) -> p g t", t=GT)).then_inc(st.free[s % 2], 1)

            def load_gelu(n):
                k = 2 * layer + n
                act.activation(mem.unread[:, k:k + 1], mem.con[:, 0:1], ACT.Gelu_apprx_tanh)

            def take_act(turn):
                for s in range(UNROLL):
                    st.wait_product(act, turn, s)
                    st.cut_hi(act, turn + (s + 2) // UNROLL, (s + 2) % UNROLL)
                    act.activation(act_w[:, bass.ds((turn - U0) * UNROLL + s, 1), :], st.bank(s).unsqueeze(1),
                                   ACT.Gelu_apprx_tanh).then_inc(st.free[s % 2], 1)

            load_gelu(0)
            with act.Fori(U0, MID) as turn:
                take_act(turn)
            act.wait_ge(shifted, 1)
            act.activation(gates, gates, ACT.Exp).then_inc(exped, 1)
            load_gelu(1)
            with act.Fori(MID, U1) as turn:
                take_act(turn)
            act.wait_ge(chosen, SPREADS)
            with act.Fori(U1, V0) as turn:
                take_act(turn)
            act.wait_ge(st.done, V0 * HALVES)
            act.wait_ge(gated, NG)
            for s in range(UNROLL):
                cut_w_hi(act, s, s)

            def next_v(turn, hi=True, w=True):
                for s in range(UNROLL):
                    if hi or s < 2:
                        st.cut_hi(act, turn + (s + 2) // UNROLL, (s + 2) % UNROLL)
                    if w:
                        st.wait_product(act, turn, s)
                        cut_w_hi(act, (turn - V0) * UNROLL + (s + 4), s)

            with act.Fori(V0, V1 - 1) as turn:
                next_v(turn)
            next_v(V1 - 1, w=False)
            act.wait_ge(st.done, V1 * HALVES)
            act.wait_ge(gated, 2 * NG)
            for s in range(UNROLL):
                cut_w_hi(act, HALF + s, s)
            with act.Fori(V1, END - 1) as turn:
                next_v(turn)
            next_v(END - 1, hi=False, w=False)
            for k, c in enumerate(h_order):
                next_sum.square(act, c, k)

        @block.vector
        def _(dve):
            step = Steps(dve, dstep)
            scale_and_cut(dve, norm, xn, cut)
            with dve.Fori(1, TQ) as turn:
                for q in (0, 1, 4, 5):
                    st.cut_lo(dve, turn, q // 2, q % 2)
            with dve.Fori(0, G // 4) as four:
                for k in range(4):
                    dve.wait_ge(scored, four * 4 + (k + 1))
                    dve.tensor_copy(scores[:, bass.ds(four * 4 + k, 1), :],
                                    mem.ps[:, 2 + k, 0:2 * NK].unsqueeze(1)).then_inc(scores_out, 1)
            for g in range(G // 4 * 4, G):
                dve.wait_ge(scored, g + 1)
                dve.tensor_copy(scores[:, g, :], mem.ps[:, 2 + g % 4, 0:2 * NK]).then_inc(scores_out, 1)
            dve.wait_ge(scores_out, G)

            def top16(rows):
                for k, op in enumerate((lambda v, spare, f, at: dve.max(f[:, 0:8], v),
                                        lambda v, spare, f, at: dve.match_replace(spare, f[:, 0:8], v, NEG),
                                        lambda v, spare, f, at: dve.max(f[:, 8:16], spare),
                                        lambda v, spare, f, at: dve.max_index(at[:, 0:8], f[:, 0:8], v),
                                        lambda v, spare, f, at: dve.max_index(at[:, 8:16], f[:, 8:16], spare))):
                    for row in rows:
                        step.wait(len(rows) if k else 1)
                        dve.sem_inc(turns_taken, 1)
                        step.add(op(*row))

            def find(first, w):
                grp = bass.ds(first, w) if not isinstance(first, int) else slice(first, first + w)
                step.done(dve.tensor_copy(s1[:, 0:2 * w, :].rearrange("p (a g) n -> p a g n", g=w),
                                          scores[:, grp, :].rearrange("p g (a n) -> p a g n", n=NK)))
                top16([(s1[:, k, :], s2[:, k, :], top[:, k, :], topi[:, k, :]) for k in range(2 * w)])
                step.add(dve.tensor_tensor(cand[:, 0:w, :].rearrange("p g (a b) -> p g a b", b=TOPK),
                                           top[:, 0:w, :].unsqueeze(3).to_broadcast([P, w, TOPK, TOPK]),
                                           top[:, w:2 * w, :].unsqueeze(2).to_broadcast([P, w, TOPK, TOPK]), ALU.add))
                top16([(cand[:, k, :], cand2[:, k, :], best[:, k, :], best_at[:, k, :]) for k in range(w)])
                step.add(dve.tensor_copy(gates[:, grp, :], best[:, 0:w, :]))
                step.wait(1)
                step.add(dve.tensor_scalar(place[:, 0:w, :], best_at[:, 0:w, :], 4, None, ALU.logical_shift_right))
                step.done(dve.tensor_scalar(place[:, w:2 * w, :], best_at[:, 0:w, :], TOPK - 1, None,
                                            ALU.bitwise_and))
                cube = [P, 2 * w, TOPK, TOPK]
                ranks = iota[:, 0:TOPK].unsqueeze(1).unsqueeze(1)
                step.done(dve.tensor_tensor(hot[:, 0:2 * w], ranks.to_broadcast(cube),
                                            place[:, 0:2 * w, :].unsqueeze(3).to_broadcast(cube), ALU.is_equal))
                step.done(dve.tensor_tensor(hot[:, 0:2 * w], hot[:, 0:2 * w],
                                            topi[:, 0:2 * w, :].unsqueeze(2).to_broadcast(cube), ALU.mult))
                step.add(dve.tensor_reduce(ij[:, :, grp, :].rearrange("p a g k -> p a (g k)"),
                                           hot[:, 0:2 * w].rearrange("p (a g) k b -> p a (g k) b", g=w), AX.X,
                                           ALU.add))

            per_pair = 1 + 5 * 4 + 1 + 5 * 2 + 6
            with dve.Fori(0, G // 2) as pair:
                step.enter(pair, per_pair)
                find(pair * 2, 2)
                step.leave(G // 2, per_pair)
            if G % 2:
                find(G - 1, 1)
            step.wait(1)
            wide = [P, G, TOPK]
            step.done(dve.tensor_copy(den[:, 0, :], gates[:, :, 0]))
            dve.tensor_tensor(gates, gates, den[:, 0, :].unsqueeze(2).to_broadcast(wide),
                              ALU.subtract).then_inc(shifted, 1)
            by_head = [P, G, PH, TOPK]
            mask = head_mask.unsqueeze(1).unsqueeze(3).to_broadcast(by_head)
            for w in range(2):
                dve.tensor_tensor(spread[:, :, w, :, :], ij[:, w, :, :].unsqueeze(2).to_broadcast(by_head), mask,
                                  ALU.mult).then_inc(placed, 1)
            dve.wait_ge(exped, 1)
            step.done(dve.tensor_reduce(den[:, 0, :], gates, AX.X, ALU.add))
            step.done(dve.reciprocal(den[:, 1, :], den[:, 0, :]))
            step.done(dve.tensor_tensor(gates, gates, den[:, 1, :].unsqueeze(2).to_broadcast(wide), ALU.mult))
            for k in range(PARTS):
                step.done(dve.tensor_copy(g_part[:, k], gates if k == 0 else g_rest))
                dve.tensor_tensor(spread[:, :, 2 + k, :, :], g_part[:, k].unsqueeze(2).to_broadcast(by_head), mask,
                                  ALU.mult).then_inc(placed, 1)
                if k < PARTS - 1:
                    step.done(dve.tensor_tensor(g_rest, gates if k == 0 else g_rest, g_part[:, k], ALU.subtract))
            dve.wait_ge(spread_done, 1)
            for w in range(SPREADS):
                dst = mem.idx[:, w, 0:T] if w < 2 else mem.g[:, w - 2, 0:T]
                dve.tensor_copy(dst, mem.ps[:, 2 + w, 0:T]).then_inc(chosen, 1)
            dve.wait_ge(chosen, SPREADS)

            def scatter_turn(turn, half, m, after, last):
                for s in range(UNROLL):
                    if s % 2 == 0:
                        st.cut_lo(dve, turn + (s + 2) // UNROLL, (s + 2) % UNROLL, 1)
                    if half == 1 and not last:
                        cut_w_lo(dve, (turn - V0) * UNROLL + (s + 4), s)
                    if s in after:
                        k = after.index(s)
                        gate_act(dve, half, m + k)
                        if not last or m + k + 1 < NG:
                            hots(dve, step, half, m + k + 1)

            def scatter_half(half, base, last_turn):
                hots(dve, step, half, 0)
                for r in range(2):
                    dve.wait_ge(st.free[r], (U1 if half == 0 else V0) * 2 + 1)
                with dve.Fori(base, last_turn) as turn:
                    step.enter(turn - base, 2 * HOT_STEPS)
                    scatter_turn(turn, half, (turn - base) * 2, GROUPS_AFTER, False)
                    step.leave(last_turn - base, 2 * HOT_STEPS)
                scatter_turn(last_turn, half, 2 * (TH - 1), LAST_AFTER, True)

            st.cut_lo(dve, U1, 0, 1)
            scatter_half(0, U1, V0 - 1)
            for s in range(UNROLL):
                cut_w_lo(dve, s, s)
            scatter_half(1, V0, V1 - 1)
            for s in range(UNROLL):
                cut_w_lo(dve, HALF + s, s)

            def lo_turn(turn, last):
                for s in range(UNROLL):
                    if s % 2 == 0 and not (last and s == 2):
                        for e in range(2):
                            st.cut_lo(dve, turn + (s + 2) // UNROLL, (s + 2) % UNROLL, e)
                    if not last:
                        cut_w_lo(dve, (turn - V0) * UNROLL + (s + 4), s)

            st.cut_lo(dve, V1, 0, 0)
            with dve.Fori(V1, END - 1) as turn:
                lo_turn(turn, False)
            lo_turn(END - 1, True)
            for k, c in enumerate(h_order):
                dve.wait_ge(st.done, END * HALVES - (c < DC // 2))
                parts = pieces[0][c] + [p for p in pieces[1][c] if p not in pieces[0][c]]
                for bank, col, tok, n in parts:
                    ins = dve.tensor_tensor(h[:, c, tok:tok + n], h[:, c, tok:tok + n], mem.ps[:, bank, col:col + n],
                                            ALU.add)
                    if len(parts) > 1:
                        step.done(ins)
                if len(parts) > 1:
                    dve.sem_inc(next_sum.updated, 1)
                else:
                    ins.then_inc(next_sum.updated, 1)

        @block.tensor
        def _(pe):
            st.open(pe)
            multiply_turns(pe, st, 0, TQ, cut)
            pe.wait_ge(keys_in, 16)
            for r in range(2):
                pe.wait_ge(st.free[r], TQ * 2 + 1)

            for g in range(G):
                if g >= 4:
                    pe.wait_ge(scores_out, g - 3)
                for half in range(2):
                    mm = pe.matmul(mem.ps[:, 2 + g % 4, half * NK:(half + 1) * NK],
                                   qt[:, half, g, :, :].rearrange("p h t -> p (h t)"), keys[:, half, :],
                                   start=True, stop=True)
                mm.then_inc(scored, 1)
            def u_tiles(first, last):
                with pe.Fori(first, last) as turn:
                    for s in range(UNROLL):
                        st.multiply(pe, turn, s, st.bank(s))

            u_tiles(U0, SPREAD)
            pe.wait_ge(placed, SPREADS)
            pe.wait_ge(scores_out, G)
            for g in range(G):
                for w in range(SPREADS):
                    mm = pe.matmul(mem.ps[:, 2 + w, g * GT:(g + 1) * GT],
                                   spread[:, g, w, :, :].rearrange("p h k -> p (h k)"), mem.token[:, :],
                                   start=True, stop=True)
            mm.then_inc(spread_done, 1)
            u_tiles(SPREAD, U1)

            def u_turn(turn, m, after):
                for s in range(UNROLL):
                    st.multiply(pe, turn, s, st.bank(s))
                    if s in after:
                        products(pe, 0, m + after.index(s))

            with pe.Fori(U1, V0 - 1) as turn:
                u_turn(turn, (turn - U1) * 2, GROUPS_AFTER)
            u_turn(V0 - 1, 2 * (TH - 1), LAST_AFTER)
            for r in range(2):
                pe.wait_ge(st.free[r], V0 * 2 + 1)

            def v_turn(turn, half, m=0, after=(), fresh=()):
                for s in range(UNROLL):
                    apply_v(pe, turn, s, half, fresh if s == 0 else ())
                    if s in after:
                        products(pe, 1, m + after.index(s))

            v_turn(V0, 0, 0, GROUPS_AFTER, fresh=range(GBANK))
            with pe.Fori(V0 + 1, V1 - 1) as turn:
                v_turn(turn, 0, (turn - V0) * 2, GROUPS_AFTER)
            v_turn(V1 - 1, 0, 2 * (TH - 1), LAST_AFTER)
            v_turn(V1, 1, fresh=[GBANK])
            with pe.Fori(V1 + 1, END) as turn:
                v_turn(turn, 1)
            next_sum.add_all(pe, h_order)


def finish(nc, ctx, mem, d):
    xn, at = mem.take(0, (DC, SEQ))
    rstd, at = mem.take(at, (1, SEQ))
    norm = Norm(nc, ctx, mem, "final", mem.h[:, :, META:L], DC, VEC["final"], xn, rstd[:, 0, :], FINAL_SUM_BANK, SEQ,
                given=True)
    stored = ctx.sem("final_stored")
    with nc.Block() as block:
        @block.vector
        def _(dve):
            norm.scale(dve, xn)

        @block.scalar
        def _(act):
            norm.root(act)

        @block.sync
        def _(sp):
            for c in range(DC):
                sp.wait_ge(norm.scaled, c + 1)
                sp.dma_start(d["out"][:, c, :], xn[:, c, :]).then_inc(stored, 16)
            sp.wait_ge(stored, 16 * DC)


def trunk(nc, d):
    with ExitStack() as ctx:
        mem = Memory(nc, ctx)
        with Stage(nc) as own:
            mla(nc, own, mem, d)
        with Stage(nc) as own:
            peer(nc, own, mem, d, 0)
        with Stage(nc) as own:
            rglru(nc, own, mem, d)
        with Stage(nc) as own:
            peer(nc, own, mem, d, 1)
        with Stage(nc) as own:
            finish(nc, own, mem, d)


def column_tiles(w):
    *lead, rows, cols = w.shape
    n = len(lead)
    w = w.reshape(*lead, rows // P, P, cols // P, P)
    w = w.transpose(*range(n), n + 2, n + 1, n, n + 3)
    return np.ascontiguousarray(w).reshape(*lead, cols // P, P, rows)


def lay_out(inputs):
    a = {k: np.asarray(v) for k, v in inputs.items()}
    chunked = lambda t: np.ascontiguousarray(t.T.reshape(DC, P, -1).transpose(1, 0, 2))
    columns = lambda v: v.reshape(-1, P).T
    half = ROPE // 2
    swap = np.r_[half:ROPE, 0:half]

    w_in = a["mla_w_in"][0]
    lat, kr = w_in[:, :QLORA + KVLORA], w_in[:, QLORA + KVLORA:]
    q_up = a["mla_w_q_up"][0].reshape(QLORA, HEADS, NOPE + ROPE)
    q_rope = q_up[:, :, NOPE:]
    q_up = np.concatenate([x.reshape(QLORA, -1) for x in (q_rope, q_rope[:, :, swap], q_up[:, :, :NOPE])], axis=1)
    kv_up = a["mla_w_kv_up"][0].reshape(KVLORA, HEADS, NOPE + VH)
    def half_tiles(w):
        w = w.reshape(-1, P, w.shape[1] // P, P).transpose(2, 0, 1, 3).reshape(-1, 4, P, P)
        return w.transpose(0, 2, 1, 3).reshape(-1, P, HW)

    k_up, v_up = kv_up[:, :, :NOPE].reshape(KVLORA, -1), kv_up[:, :, NOPE:].reshape(KVC, P, 2, HW)
    up = np.concatenate([half_tiles(q_up), half_tiles(k_up), v_up.transpose(2, 0, 1, 3).reshape(-1, P, HW)])
    up = up.reshape(-1, 2, P, HW).transpose(0, 2, 1, 3).reshape(-1, P, D)
    down = column_tiles(np.concatenate([lat, kr, kr, kr[:, swap], kr[:, swap]], axis=1))
    vec = [a["mixer_norm"][0], a["mixer_norm"][1], a["ffn_norm"][0], a["ffn_norm"][1], a["final_norm"],
           a["lru_b_gate_a"][0], a["lru_b_gate_x"][0], a["lru_conv_b"][0], *a["lru_conv_w"][0], a["lru_lambda"][0],
           a["mla_q_norm"][0], a["mla_kv_norm"][0]]
    con, idm = constants()
    layers = a["peer_u"].shape[0]
    lru_in = a["lru_w_in"][0]
    u = a["peer_u"].reshape(layers, NK, NK, DC, P).transpose(0, 1, 4, 3, 2)
    return {
        "x": chunked(a["x"][0]),
        "meta": chunked(a["meta_tokens"]),
        "pos": np.ascontiguousarray(a["positions"]),
        "con": con,
        "idm": idm,
        "vec": np.ascontiguousarray(np.concatenate([columns(v) for v in vec], axis=1)),
        "mla_down": np.concatenate([down, up]),
        "mla_out": column_tiles(a["mla_w_out"][0]),
        "query": column_tiles(a["peer_w_query"]),
        "keys": np.ascontiguousarray(a["peer_sub_keys"].transpose(0, 3, 1, 2)),
        "u": np.ascontiguousarray(u).reshape(layers, NK, P, D),
        "v": a["peer_v"].reshape(layers, NK, P, D),
        "lru_w": np.concatenate([column_tiles(w) for w in (lru_in[:, D:], lru_in[:, :D], a["lru_w_out"][0])]),
        "lru_wa": np.ascontiguousarray(a["lru_w_gate_a"][0].transpose(1, 0, 2)),
        "lru_wx": np.ascontiguousarray(a["lru_w_gate_x"][0].transpose(1, 0, 2)),
    }


def kernel(**inputs):
    import concourse.bacc as bacc
    from concourse.bass_utils import run_bass_kernel_spmd

    nc = bacc.Bacc("TRN2", target_bir_lowering=False, num_devices=1)
    arrays, d = {}, {}
    for name, array in lay_out(inputs).items():
        arrays[f"in_{name}"] = array
        d[name] = nc.dram_tensor(f"in_{name}", array.shape, mybir.dt.from_np(array.dtype), kind="ExternalInput").ap()
    d["out"] = nc.dram_tensor("out_0", (P, DC, SEQ), F32, kind="ExternalOutput").ap()
    trunk(nc, d)
    result = run_bass_kernel_spmd(nc, [arrays], core_ids=[0])
    out = result.results[0]["out_0"]
    return np.ascontiguousarray(out.transpose(2, 1, 0)).reshape(1, SEQ, D)
```
